# Optimizing a Trainium2 kernel written in Bass

```python
import math
import jax
import jax.numpy as jnp
from jax import lax
import numpy as np

D_MODEL = 1024
BATCH = 1
SEQ = 512
DEPTH = 2

CTX_LEN = 256
GRID_W = 64
HEAD_DIM = 64
N_GROUPS = 4
GROUP_HEADS = D_MODEL // (N_GROUPS * HEAD_DIM)
GW = GROUP_HEADS * HEAD_DIM
D_MIX = N_GROUPS * GW
DIFF_HALF = HEAD_DIM // 2
Q_BLOCK = 128
ROPE_BASE = 10000.0
DECAY_LORA = 64
ICLR_LORA = 64
GATE_LORA = 128
RWKV_GN_EPS = 64e-5
RWKV_COLS = 3 * GW + 2 * DECAY_LORA + 2 * ICLR_LORA + GATE_LORA
GDN_CONV = 3
GDN_CHUNK = 64
GDN_COLS = 4 * GW + 4 * GROUP_HEADS
WIN_H = 8
WIN_W = 16
ATTN_COLS = 3 * GW
IN_COLS = ATTN_COLS + RWKV_COLS + GDN_COLS + ATTN_COLS
PEER_HEADS = 8
PEER_KEYS = 128
PEER_EXPERTS = PEER_KEYS * PEER_KEYS
PEER_QDIM = 256
PEER_HALF = PEER_QDIM // 2
PEER_TOPK = 16
PEER_BLOCK = 128
DN_ALPHA = (2 * DEPTH) ** 0.25
DN_BETA = (8 * DEPTH) ** -0.25
LN_EPS = 1e-5

kernel_name = 'hybrid_diffusion_parallel_groups_peer'

F32 = jnp.float32

def _split(x, sizes):
    offs = np.cumsum(sizes)[:-1].tolist()
    return jnp.split(x, offs, axis=-1)

def _heads(x):
    return x.reshape(x.shape[0], x.shape[1], -1, HEAD_DIM)

def _layer_norm(x):
    xf = x.astype(F32)
    mu = xf.mean(-1, keepdims=True)
    var = jnp.square(xf - mu).mean(-1, keepdims=True)
    return (xf - mu) * lax.rsqrt(var + LN_EPS)

def _rms_norm(x, g):
    xf = x.astype(F32)
    return xf * lax.rsqrt(jnp.mean(xf * xf, -1, keepdims=True) + 1e-6) * g.astype(F32)

def _l2norm(x):
    xf = x.astype(F32)
    return xf * lax.rsqrt(jnp.sum(xf * xf, -1, keepdims=True) + 1e-6)

def _modulate(h, shift, scale, dtype):
    return (_layer_norm(h) * (1.0 + scale) + shift).astype(dtype)

def _post_norm(h, gate, y, g, b, dtype):
    z = DN_ALPHA * h.astype(F32) + gate.astype(F32) * y.astype(F32)
    return (_layer_norm(z) * g + b).astype(dtype)

def _dwconv_centred(x, w):
    k = w.shape[0]
    pad = k // 2
    t = x.shape[1]
    xp = jnp.pad(x, ((0, 0), (pad, pad), (0, 0)))
    out = xp[:, 0:t] * w[0]
    for i in range(1, k):
        out = out + xp[:, i:i + t] * w[i]
    return out

def _grid_pos(n_tok):
    t = jnp.arange(n_tok, dtype=jnp.int32)
    return t // GRID_W, t % GRID_W

def _rope_1d(x, pos):
    half = x.shape[-1] // 2
    inv = ROPE_BASE ** (-jnp.arange(half, dtype=F32) / half)
    ang = pos.astype(F32)[:, None] * inv
    cos = jnp.cos(ang)[:, None, :]
    sin = jnp.sin(ang)[:, None, :]
    x1 = x[..., :half].astype(F32)
    x2 = x[..., half:].astype(F32)
    return jnp.concatenate([x1 * cos - x2 * sin, x1 * sin + x2 * cos], -1)

def _rope_2d(x, row, col):
    n = x.shape[-1] // 2
    return jnp.concatenate([_rope_1d(x[..., :n], row), _rope_1d(x[..., n:], col)], -1)

def _diff_core(q, k, v, lam):
    scale = DIFF_HALF ** -0.5
    q = q.astype(F32)
    k = k.astype(F32)
    s1 = jnp.einsum('bqhd,bkhd->bhqk', q[..., :DIFF_HALF], k[..., :DIFF_HALF]) * scale
    s2 = jnp.einsum('bqhd,bkhd->bhqk', q[..., DIFF_HALF:], k[..., DIFF_HALF:]) * scale
    p = jax.nn.softmax(s1, -1) - lam * jax.nn.softmax(s2, -1)
    return jnp.einsum('bhqk,bkhd->bqhd', p, v.astype(F32))

def _diff_attention(q, k, v, qc, kc, vc, lam_vecs, norm_g, lam_init, ctx_out):
    bsz, lat_len = q.shape[:2]
    row, col = _grid_pos(lat_len)
    rot = lambda z: jnp.concatenate([_rope_2d(z[..., :DIFF_HALF], row, col),
                                     _rope_2d(z[..., DIFF_HALF:], row, col)], -1)
    q = rot(q)
    k = rot(k)
    lv = lam_vecs.astype(F32)
    lam = jnp.exp(jnp.sum(lv[0] * lv[1])) - jnp.exp(jnp.sum(lv[2] * lv[3])) + lam_init
    k_all = jnp.concatenate([k, kc.astype(F32)], 1)
    v_all = jnp.concatenate([v.astype(F32), vc.astype(F32)], 1)
    nb = lat_len // Q_BLOCK
    qb = jnp.moveaxis(q.reshape(bsz, nb, Q_BLOCK, GROUP_HEADS, HEAD_DIM), 1, 0)
    ob = lax.map(lambda qq: _diff_core(qq, k_all, v_all, lam), qb)
    o = jnp.moveaxis(ob, 0, 1).reshape(bsz, lat_len, GROUP_HEADS, HEAD_DIM)
    post = lambda z: (_rms_norm(z, norm_g) * (1.0 - lam_init)).reshape(z.shape[0], z.shape[1], GW)
    out_ctx = post(_diff_core(qc, kc, vc, lam)) if ctx_out else None
    return post(o), out_ctx

def _wkv7_scan(r, w, k, v, kk, a, s0, reverse):
    def step(s, inp):
        r_t, w_t, k_t, v_t, kk_t, a_t = inp
        sa = jnp.einsum('bhvk,bhk->bhv', s, kk_t)
        s = (s * w_t[:, :, None, :] - sa[..., None] * (kk_t * a_t)[:, :, None, :]
             + v_t[..., None] * k_t[:, :, None, :])
        return s, jnp.einsum('bhvk,bhk->bhv', s, r_t)
    xs = tuple(jnp.moveaxis(z, 1, 0) for z in (r, w, k, v, kk, a))
    s, y = lax.scan(step, s0, xs, reverse=reverse)
    return jnp.moveaxis(y, 0, 1), s

def _rwkv7(f_lat, f_ctx, mu, w0, w2, a0, a2, g2, k_k, k_a, r_k, ln_g, ln_b, ctx_out):
    shift_w = jnp.stack([mu[0], 1.0 - mu[0] - mu[1], mu[1]])

    def prep(f):
        f = _dwconv_centred(f, shift_w).astype(F32)
        r, k, v, wd, ad, gd = _split(f, [GW, GW, GW, 2 * DECAY_LORA, 2 * ICLR_LORA, GATE_LORA])
        bsz, t = f.shape[:2]
        wd = jnp.tanh(wd.reshape(bsz, t, 2, DECAY_LORA))
        ad = ad.reshape(bsz, t, 2, ICLR_LORA)
        w_raw = w0 + jnp.einsum('btdr,drc->btdc', wd, w2)
        decay = jnp.exp(-jnp.exp(-jax.nn.softplus(-w_raw) - 0.5))
        a = jax.nn.sigmoid(a0 + jnp.einsum('btdr,drc->btdc', ad, a2))
        g = jax.nn.sigmoid(gd) @ g2
        kk = _l2norm(_heads(k * k_k))
        kd = k[:, :, None] * (1.0 + (a - 1.0) * k_a)
        return r, v, g, kk, decay, a, kd

    def run(p, d, s0, rev):
        r, v, g, kk, decay, a, kd = p
        return _wkv7_scan(_heads(r), _heads(decay[:, :, d]), _heads(kd[:, :, d]), _heads(v),
                          kk, _heads(a[:, :, d]), s0, rev)

    def post(p, ys):
        r, v, g, kk, decay, a, kd = p
        bsz, t = r.shape[:2]
        y = ys[0] + ys[1]
        m = y.mean(-1, keepdims=True)
        var = jnp.square(y - m).mean(-1, keepdims=True)
        yn = ((y - m) * lax.rsqrt(var + RWKV_GN_EPS)).reshape(bsz, t, GW) * ln_g + ln_b
        rh, vh = _heads(r), _heads(v)
        bonus = ((rh * _heads(kd[:, :, 0]) * r_k).sum(-1, keepdims=True) * vh
                 + (rh * _heads(kd[:, :, 1]) * r_k).sum(-1, keepdims=True) * vh)
        return (yn + bonus.reshape(bsz, t, GW)) * g

    pl, pc = prep(f_lat), prep(f_ctx)
    s0 = jnp.zeros((f_lat.shape[0], GROUP_HEADS, HEAD_DIM, HEAD_DIM), F32)
    y_lat, y_ctx = [], []
    for d, rev in ((0, False), (1, True)):
        yc, sc = run(pc, d, s0, rev)
        yl, _ = run(pl, d, sc, rev)
        y_lat.append(yl)
        y_ctx.append(yc)
    out_ctx = post(pc, y_ctx) if ctx_out else None
    return post(pl, y_lat), out_ctx

def _gdn_chunked(q, k, v, beta, g, s0):
    bsz, t, h, dk = q.shape
    dv = v.shape[-1]
    n = t // GDN_CHUNK
    ch = lambda z: jnp.moveaxis(z.reshape(bsz, n, GDN_CHUNK, h, *z.shape[3:]), 3, 2)
    q, k, v, beta, g = ch(q), ch(k), ch(v), ch(beta), ch(g)
    gc = jnp.cumsum(g, axis=-1)
    i = jnp.arange(GDN_CHUNK)
    incl = i[:, None] >= i[None, :]
    strict = i[:, None] > i[None, :]
    decay = jnp.exp(jnp.where(incl, gc[..., :, None] - gc[..., None, :], -jnp.inf))
    kb = k * beta[..., None]
    a_low = jnp.where(strict, jnp.einsum('bnhid,bnhjd->bnhij', kb, k) * decay, 0.0)
    tmat = a_low + jnp.eye(GDN_CHUNK, dtype=F32)
    rhs = jnp.concatenate([v * beta[..., None], kb * jnp.exp(gc)[..., None]], -1)
    sol = lax.linalg.triangular_solve(tmat, rhs, left_side=True, lower=True, unit_diagonal=True)
    u, w = sol[..., :dv], sol[..., dv:]
    qk = jnp.where(incl, jnp.einsum('bnhid,bnhjd->bnhij', q, k) * decay, 0.0)
    qg = q * jnp.exp(gc)[..., None]
    kg = k * jnp.exp(gc[..., -1:] - gc)[..., None]
    glast = jnp.exp(gc[..., -1])

    def step(s, xs):
        qg_i, kg_i, u_i, w_i, qk_i, gl_i = xs
        v_new = u_i - jnp.einsum('bhcd,bhdv->bhcv', w_i, s)
        o = jnp.einsum('bhcd,bhdv->bhcv', qg_i, s) + jnp.einsum('bhij,bhjv->bhiv', qk_i, v_new)
        s = s * gl_i[..., None, None] + jnp.einsum('bhcd,bhcv->bhdv', kg_i, v_new)
        return s, o

    xs = tuple(jnp.moveaxis(z, 1, 0) for z in (qg, kg, u, w, qk, glast))
    s, o = lax.scan(step, s0, xs)
    o = jnp.moveaxis(jnp.moveaxis(o, 0, 1), 2, 3).reshape(bsz, t, h, dv)
    return o, s

def _gated_deltanet(f_lat, f_ctx, conv_w, a_log, dt_bias, norm_g, ctx_out):
    def prep(f):
        qkv, gate, ab = _split(f, [3 * GW, GW, 4 * GROUP_HEADS])
        qkv = jax.nn.silu(_dwconv_centred(qkv, conv_w).astype(F32))
        q, k, v = [_heads(z) for z in _split(qkv, [GW, GW, GW])]
        q = _l2norm(q) * HEAD_DIM ** -0.5
        k = _l2norm(k)
        ab = ab.astype(F32).reshape(f.shape[0], f.shape[1], 2, 2, GROUP_HEADS)
        log_alpha = -jnp.exp(a_log) * jax.nn.softplus(ab[:, :, 0] + dt_bias)
        beta = jax.nn.sigmoid(ab[:, :, 1])
        return q, k, v, gate, log_alpha, beta

    def run(p, d, s0):
        tr = (lambda z: jnp.flip(z, 1)) if d == 1 else (lambda z: z)
        q, k, v, gate, log_alpha, beta = p
        o, s = _gdn_chunked(tr(q), tr(k), tr(v), tr(beta[:, :, d]), tr(log_alpha[:, :, d]), s0)
        return tr(o), s

    def post(p, os_):
        gate = p[3]
        o = os_[0] + os_[1]
        y = _rms_norm(o, norm_g) * jax.nn.silu(_heads(gate.astype(F32)))
        return y.reshape(o.shape[0], o.shape[1], GW)

    pl, pc = prep(f_lat), prep(f_ctx)
    s0 = jnp.zeros((f_lat.shape[0], GROUP_HEADS, HEAD_DIM, HEAD_DIM), F32)
    o_lat, o_ctx = [], []
    for d in range(2):
        oc, sc = run(pc, d, s0)
        ol, _ = run(pl, d, sc)
        o_lat.append(ol)
        o_ctx.append(oc)
    out_ctx = post(pc, o_ctx) if ctx_out else None
    return post(pl, o_lat), out_ctx

def _softmax_attn(q, k, v):
    s = jnp.einsum('bqhd,bkhd->bhqk', q.astype(F32), k.astype(F32)) * HEAD_DIM ** -0.5
    return jnp.einsum('bhqk,bkhd->bqhd', jax.nn.softmax(s, -1), v.astype(F32))

def _neighbourhood_attention(q, k, v, qc, kc, vc, rpb, ctx_out):
    bsz, lat_len = q.shape[:2]
    rows = lat_len // GRID_W
    kh = min(WIN_H, rows)
    scale = HEAD_DIM ** -0.5
    grid = lambda z: z.astype(F32).reshape(bsz, rows, GRID_W, GROUP_HEADS, HEAD_DIM)
    qg, kg, vg = grid(q), grid(k), grid(v)
    kc32, vc32 = kc.astype(F32), vc.astype(F32)
    rpb = rpb.astype(F32)
    cq = jnp.arange(GRID_W)
    c_start = jnp.clip(cq - WIN_W // 2, 0, GRID_W - WIN_W)
    col_ok = (cq[None, :] >= c_start[:, None]) & (cq[None, :] < c_start[:, None] + WIN_W)
    d_col = jnp.clip(cq[None, :] - cq[:, None], -(WIN_W - 1), WIN_W - 1) + (WIN_W - 1)

    def row_block(r):
        rs = jnp.clip(r - kh // 2, 0, rows - kh)
        q_r = lax.dynamic_index_in_dim(qg, r, axis=1, keepdims=False)
        k_r = lax.dynamic_slice_in_dim(kg, rs, kh, axis=1)
        v_r = lax.dynamic_slice_in_dim(vg, rs, kh, axis=1)
        s = jnp.einsum('bqhd,bkwhd->bqhkw', q_r, k_r) * scale
        d_row = rs + jnp.arange(kh) - r + (WIN_H - 1)
        bias = rpb[:, d_row[None, :, None], d_col[:, None, :]]
        s = jnp.where(col_ok[:, None, None, :], s + jnp.transpose(bias, (1, 0, 2, 3)), -jnp.inf)
        s_c = jnp.einsum('bqhd,bchd->bqhc', q_r, kc32) * scale
        p = jax.nn.softmax(jnp.concatenate(
            [s.reshape(bsz, GRID_W, GROUP_HEADS, kh * GRID_W), s_c], -1), -1)
        p_win = p[..., :kh * GRID_W].reshape(bsz, GRID_W, GROUP_HEADS, kh, GRID_W)
        return (jnp.einsum('bqhkw,bkwhd->bqhd', p_win, v_r)
                + jnp.einsum('bqhc,bchd->bqhd', p[..., kh * GRID_W:], vc32))

    o = lax.map(row_block, jnp.arange(rows))
    out_lat = jnp.moveaxis(o, 0, 1).reshape(bsz, lat_len, GW)
    out_ctx = _softmax_attn(qc, kc, vc).reshape(bsz, qc.shape[1], GW) if ctx_out else None
    return out_lat, out_ctx

def _peer(h, w_q, keys, u_tab, v_tab):
    bsz, t, d = h.shape
    blocks = h.reshape(bsz * t // PEER_BLOCK, PEER_BLOCK, d)
    keys = keys.astype(F32)

    def block(tb):
        q = (tb @ w_q).astype(F32).reshape(PEER_BLOCK, PEER_HEADS, 2, PEER_HALF)
        s = jnp.einsum('thpd,hpnd->thpn', q, keys)
        top_s, top_i = lax.top_k(s, PEER_TOPK)
        cand_s = (top_s[:, :, 0, :, None] + top_s[:, :, 1, None, :]).reshape(
            PEER_BLOCK, PEER_HEADS, PEER_TOPK * PEER_TOPK)
        cand_i = (top_i[:, :, 0, :, None] * PEER_KEYS + top_i[:, :, 1, None, :]).reshape(
            PEER_BLOCK, PEER_HEADS, PEER_TOPK * PEER_TOPK)
        best_s, pos = lax.top_k(cand_s, PEER_TOPK)
        idx = jnp.take_along_axis(cand_i, pos, axis=-1)
        gate = jax.nn.softmax(best_s, -1)
        u = jnp.take(u_tab, idx, axis=0).astype(F32)
        act = jax.nn.gelu(jnp.einsum('td,thkd->thk', tb.astype(F32), u), approximate=False)
        v = jnp.take(v_tab, idx, axis=0).astype(F32)
        return jnp.einsum('thk,thkd->td', gate * act, v)

    return lax.map(block, blocks).reshape(bsz, t, d)

def _qkv_heads(p):
    return [_heads(z) for z in _split(p, [GW, GW, GW])]

def setup_inputs(seed: int = 0) -> dict:
    key = jax.random.key(seed)
    ks = iter(jax.random.split(key, 48))
    nrm = lambda shape, std: jax.random.normal(next(ks), shape, F32) * std
    uni = lambda shape, lo, hi: jax.random.uniform(next(ks), shape, F32, lo, hi)
    L, D = DEPTH, D_MODEL
    return {
        'x': nrm((BATCH, SEQ, D), 1.0),
        'c': nrm((BATCH, D), 1.0),
        'ctx': nrm((BATCH, CTX_LEN, D), 1.0),
        'c_ctx': nrm((D,), 1.0),
        'w_ada': nrm((L, D, 6 * D), 0.5 * D ** -0.5),
        'b_ada': nrm((L, 6 * D), 0.02),
        'w_in': nrm((L, D, IN_COLS), D ** -0.5),
        'w_out': nrm((L, D_MIX, D), DN_BETA * D_MIX ** -0.5),
        'ln_mix_g': 1.0 + nrm((L, D), 0.02),
        'ln_mix_b': nrm((L, D), 0.02),
        'ln_ffn_g': 1.0 + nrm((L, D), 0.02),
        'ln_ffn_b': nrm((L, D), 0.02),
        'diff_lam': nrm((L, 4, DIFF_HALF), 0.1),
        'diff_norm_g': 1.0 + nrm((L, HEAD_DIM), 0.02),
        'rwkv_mu': uni((L, 2, RWKV_COLS), 0.0, 0.5),
        'rwkv_w0': uni((L, 2, GW), -6.0, 0.0),
        'rwkv_w2': nrm((L, 2, DECAY_LORA, GW), 0.1),
        'rwkv_a0': nrm((L, 2, GW), 0.3),
        'rwkv_a2': nrm((L, 2, ICLR_LORA, GW), 0.5 * ICLR_LORA ** -0.5),
        'rwkv_g2': nrm((L, GATE_LORA, GW), GATE_LORA ** -0.5),
        'rwkv_kk': 0.85 + nrm((L, GW), 0.05),
        'rwkv_ka': 1.0 + nrm((L, GW), 0.05),
        'rwkv_rk': nrm((L, GROUP_HEADS, HEAD_DIM), 0.1),
        'rwkv_ln_g': 1.0 + nrm((L, GW), 0.02),
        'rwkv_ln_b': nrm((L, GW), 0.02),
        'gdn_conv': nrm((L, GDN_CONV, 3 * GW), GDN_CONV ** -0.5),
        'gdn_a_log': jnp.log(uni((L, 2, GROUP_HEADS), 1.0, 16.0)),
        'gdn_dt_bias': uni((L, 2, GROUP_HEADS), -5.0, -2.0),
        'gdn_norm_g': 1.0 + nrm((L, HEAD_DIM), 0.02),
        'nat_rpb': nrm((L, GROUP_HEADS, 2 * WIN_H - 1, 2 * WIN_W - 1), 0.2),
        'peer_wq': nrm((L, D, PEER_HEADS * PEER_QDIM), D ** -0.5),
        'peer_keys': nrm((L, PEER_HEADS, 2, PEER_KEYS, PEER_HALF), PEER_HALF ** -0.5),
        'peer_u': nrm((L, PEER_EXPERTS, D), D ** -0.5),
        'peer_v': nrm((L, PEER_EXPERTS, D), DN_BETA),
    }

def reference(x, c, ctx, c_ctx, w_ada, b_ada, w_in, w_out, ln_mix_g, ln_mix_b, ln_ffn_g, ln_ffn_b,
              diff_lam, diff_norm_g, rwkv_mu, rwkv_w0, rwkv_w2, rwkv_a0, rwkv_a2, rwkv_g2,
              rwkv_kk, rwkv_ka, rwkv_rk, rwkv_ln_g, rwkv_ln_b, gdn_conv, gdn_a_log, gdn_dt_bias,
              gdn_norm_g, nat_rpb, peer_wq, peer_keys, peer_u, peer_v):
    dtype = x.dtype
    h_lat, h_ctx = x, ctx
    col_sizes = [ATTN_COLS, RWKV_COLS, GDN_COLS, ATTN_COLS]
    for l in range(DEPTH):
        last = l == DEPTH - 1
        lam_init = 0.8 - 0.6 * math.exp(-0.3 * l)
        m_lat = jnp.split((jax.nn.silu(c) @ w_ada[l] + b_ada[l])[:, None, :], 6, axis=-1)
        m_ctx = jnp.split((jax.nn.silu(c_ctx) @ w_ada[l] + b_ada[l])[None, None, :], 6, axis=-1)
        u_lat = _modulate(h_lat, m_lat[0], m_lat[1], dtype)
        u_ctx = _modulate(h_ctx, m_ctx[0], m_ctx[1], dtype)
        pa, pb, pc, pd = _split(u_lat @ w_in[l], col_sizes)
        ca, cb, cc, cd = _split(u_ctx @ w_in[l], col_sizes)
        qa, ka, va = _qkv_heads(pa)
        qca, kca, vca = _qkv_heads(ca)
        ya, yca = _diff_attention(qa, ka, va, qca, kca, vca, diff_lam[l], diff_norm_g[l],
                                  lam_init, not last)
        yb, ycb = _rwkv7(pb, cb, rwkv_mu[l], rwkv_w0[l], rwkv_w2[l], rwkv_a0[l], rwkv_a2[l],
                         rwkv_g2[l], rwkv_kk[l], rwkv_ka[l], rwkv_rk[l], rwkv_ln_g[l],
                         rwkv_ln_b[l], not last)
        yc, ycc = _gated_deltanet(pc, cc, gdn_conv[l], gdn_a_log[l], gdn_dt_bias[l],
                                  gdn_norm_g[l], not last)
        qd, kd, vd = _qkv_heads(pd)
        qcd, kcd, vcd = _qkv_heads(cd)
        yd, ycd = _neighbourhood_attention(qd, kd, vd, qcd, kcd, vcd, nat_rpb[l], not last)
        mix = jnp.concatenate([ya, yb, yc, yd], -1).astype(dtype) @ w_out[l]
        h_lat = _post_norm(h_lat, m_lat[2], mix, ln_mix_g[l], ln_mix_b[l], dtype)
        ffn = _peer(_modulate(h_lat, m_lat[3], m_lat[4], dtype), peer_wq[l], peer_keys[l],
                    peer_u[l], peer_v[l])
        h_lat = _post_norm(h_lat, m_lat[5], ffn, ln_ffn_g[l], ln_ffn_b[l], dtype)
        if not last:
            mix_c = jnp.concatenate([yca, ycb, ycc, ycd], -1).astype(dtype) @ w_out[l]
            h_ctx = _post_norm(h_ctx, m_ctx[2], mix_c, ln_mix_g[l], ln_mix_b[l], dtype)
            ffn_c = _peer(_modulate(h_ctx, m_ctx[3], m_ctx[4], dtype), peer_wq[l], peer_keys[l],
                          peer_u[l], peer_v[l])
            h_ctx = _post_norm(h_ctx, m_ctx[5], ffn_c, ln_ffn_g[l], ln_ffn_b[l], dtype)
    return h_lat


_drawn_inputs = setup_inputs


def setup_inputs(seed=0):
    import zlib

    import numpy as np

    out = dict(_drawn_inputs(seed))
    spreads = {}
    factors = {'ctx': 2.784,
     'b_ada': 3.124,
     'diff_lam': 5.16,
     'diff_norm_g': 29.798,
     'rwkv_w2': 8.0,
     'rwkv_a0': 7.655,
     'rwkv_a2': 5.933,
     'rwkv_kk': 23.023,
     'rwkv_ka': 7.843,
     'rwkv_rk': 3.288,
     'rwkv_ln_g': 47.218,
     'rwkv_ln_b': 40.207,
     'gdn_a_log': 6.093,
     'gdn_dt_bias': 3.93,
     'gdn_norm_g': 39.042,
     'nat_rpb': 24.812}
    for name, (base, spread) in spreads.items():
        noise = np.random.default_rng([zlib.crc32(name.encode()), seed]).standard_normal(out[name].shape)
        drawn = base * np.exp(spread * noise) if base else spread * noise
        out[name] = jnp.asarray(drawn.astype(out[name].dtype))
    for name, factor in factors.items():
        out[name] = (out[name] * factor).astype(out[name].dtype)
    return out
```

```python
from contextlib import ExitStack, contextmanager

import numpy as np

import concourse.bass as bass
import concourse.mybir as mybir

F32 = mybir.dt.float32
U32 = mybir.dt.uint32
ALU = mybir.AluOpType
ACT = mybir.ActivationFunctionType
X = mybir.AxisListType.X
P = 128

D = 1024
SEQ = 512
CTX = 256
TOK = CTX + SEQ
TILES = TOK // P
CTX_TILES = CTX // P
DEPTH = 2
GRID_W = 64
HD = 64
HEADS = 4
GW = HEADS * HD
ATTN_COLS = 3 * GW
LORA = 64
RWKV_COLS = 3 * GW + 4 * LORA + 128
GDN_QKV = 3 * GW
GDN_COLS = 4 * GW + 4 * HEADS
IN_COLS = ATTN_COLS + RWKV_COLS + GDN_COLS + ATTN_COLS
COL_A = 0
COL_B = ATTN_COLS
COL_C = COL_B + RWKV_COLS
COL_D = COL_C + GDN_COLS
KT = D // P
WCHUNK = 466
NCHUNKS = IN_COLS // WCHUNK
WIN_H, WIN_W = 8, 16
C = 64
CHUNKS = TOK // C
CTX_CHUNKS = CTX // C
LEVELS = (1, 2, 4, 8, 16, 32)
PH, PK, TOPK = 8, 128, 16
EXPERTS = PK * PK
SLOTS = PH * TOPK
ALPHA = (2 * DEPTH) ** 0.25
LN_EPS = 1e-5
GN_EPS = 64e-5
NORM_EPS = 1e-6
NEG = -1e30
DECAY = -float(np.exp(-0.5))


def constants():
    c = {}
    i = np.arange(P)
    same = (i[:, None] // C) == (i[None, :] // C)
    low = i[:, None] >= i[None, :]
    c["k_sums"] = np.stack([same & low.T, same & low, same]).astype(np.float32).transpose(1, 0, 2)
    c["k_ident"] = np.eye(P, dtype=np.float32)
    both = lambda m: np.stack([m, m, m.T, m.T]).astype(np.float32)
    strict = same & (i[:, None] > i[None, :])
    incl = same & low
    masks = [both(strict.T), both(incl.T)]
    for s in LEVELS:
        off = ((i[:, None] // (2 * s)) == (i[None, :] // (2 * s))) & ((i[:, None] // s) > (i[None, :] // s))
        masks += [both(off), both(off.T)]
    c["k_masks"] = np.stack(masks).transpose(2, 0, 1, 3).astype(np.float32).copy()
    c["k_rows"] = np.stack([(i // 64 == 0), (i // 64 == 1)] + [(i // 32 == g) for g in range(4)]).T.astype(np.float32).copy()
    e = np.ones((TILES, P, 2), np.float32)
    e[0, 0, 0] = e[CTX_TILES, 0, 0] = 0
    e[CTX_TILES - 1, P - 1, 1] = e[TILES - 1, P - 1, 1] = 0
    c["k_edges"] = e
    t = np.arange(SEQ)
    inv = (10000.0 ** (-np.arange(8, dtype=np.float32) / 8)).astype(np.float32)
    rope = np.zeros((2, TOK, HD), np.float32)
    rope[0] = 1
    for part, pos in ((0, t // GRID_W), (1, t % GRID_W)):
        ang = pos.astype(np.float32)[:, None] * inv
        for half in (0, 1):
            o = 32 * half + 16 * part
            rope[0, CTX:, o:o + 8] = rope[0, CTX:, o + 8:o + 16] = np.cos(ang)
            rope[1, CTX:, o:o + 8] = -np.sin(ang)
            rope[1, CTX:, o + 8:o + 16] = np.sin(ang)
    rope = np.broadcast_to(rope.reshape(2, TILES, P, 1, HD), (2, TILES, P, 8, HD))
    c["k_rope"] = np.ascontiguousarray(rope.transpose(1, 2, 0, 3, 4))
    c["k_iota"] = np.broadcast_to(np.arange(TOPK, dtype=np.float32), (P, TOPK)).copy()
    c["k_zero"] = np.zeros((2, IN_COLS), np.float32)
    lam = [0.8 - 0.6 * float(np.exp(-0.3 * l)) for l in range(DEPTH)]
    c["k_layer"] = np.stack([np.broadcast_to(np.array([lam[l], 1.0 - lam[l], l * EXPERTS, 0.0], np.float32), (P, 4))
                             for l in range(DEPTH)]).copy()
    return c


def window_bias(rpb):
    q = np.arange(SEQ)
    r, cq = q // GRID_W, q % GRID_W
    start = np.clip(cq - WIN_W // 2, 0, GRID_W - WIN_W)
    ok = (cq[None, :] >= start[:, None]) & (cq[None, :] < start[:, None] + WIN_W)
    dr = r[None, :] - r[:, None] + WIN_H - 1
    dc = np.clip(cq[None, :] - cq[:, None], -(WIN_W - 1), WIN_W - 1) + WIN_W - 1
    laid = np.asarray(rpb)[:, :, dr, dc]
    laid = np.where(ok[None, None], laid, np.float32(NEG)).astype(np.float32)
    return np.ascontiguousarray(laid.reshape(DEPTH, HEADS, SEQ // P, P, SEQ).transpose(0, 2, 3, 1, 4))


@contextmanager
def stage(nc, *names, pool_dmas=False):
    with ExitStack() as es:
        sems = [es.enter_context(nc.semaphore(n)) for n in names]
        with nc.Block() as block:
            yield (block, *sems)
        with nc.Block() as clear:
            if pool_dmas:
                @clear.gpsimd
                def _(pool):
                    pool.dma_reset()
                    for s in sems:
                        pool.sem_clear(s)
            else:
                @clear.sync
                def _(sp):
                    for s in sems:
                        sp.sem_clear(s)


def chained(eng, sem):
    count = [0]

    def link(ins):
        count[0] += 1
        ins.then_inc(sem, 1)
        eng.wait_ge(sem, count[0])
        return ins

    return link


def over_rows(row, *shape):
    return row.unsqueeze(0).to_broadcast([P] + list(row.shape))


def ln_first(v, link, x, stats, mv, var_ready):
    for k in range(2):
        link(v.bn_stats(stats[:, k, :], x[:, k * 512:(k + 1) * 512]))
    link(v.bn_aggr(mv[:, 0:2], stats[:, :, :].rearrange("p a b -> p (a b)")))
    v.tensor_scalar(mv[:, 2:3], mv[:, 1:2], LN_EPS, None, ALU.add).then_inc(var_ready, 1)


def ln_last(v, link, out, x, mv, std_ready, n):
    v.wait_ge(std_ready, n)
    link(v.reciprocal(mv[:, 4:5], mv[:, 3:4]))
    link(v.tensor_scalar(out, x, mv[:, 0:1], mv[:, 4:5], ALU.subtract, ALU.mult))


def ada_stage(nc, l, t, mods, consts):
    n_chunks, bufs = 6 * D // 512, 4
    with ExitStack() as es:
        cc = es.enter_context(nc.sbuf_tensor("cond", [P, KT, 2], F32))
        sc = es.enter_context(nc.sbuf_tensor("cond_silu", [P, KT, 2], F32))
        w = es.enter_context(nc.sbuf_tensor("ada_w", [P, bufs, KT, 512], F32))
        b = es.enter_context(nc.sbuf_tensor("ada_b", [2, 6 * D], F32))
        row = es.enter_context(nc.sbuf_tensor("ada_rows", [2, 6 * D], F32))
        ps = es.enter_context(nc.psum_tensor("ada_ps", [2, 2, 512], F32))
        wait = es.enter_context(stage(nc, "cond_in", "bias_in", "silu_done", "chunk_done", "row_done", "rows_out",
                                      "dve_step", *[f"w_in{k}" for k in range(bufs)]))
        block, cond_in, bias_in, silu_done, chunk_done, row_done, rows_out, dve_step, *w_in = wait
        wv = t["w_ada"][l].rearrange("(k p) n -> p k n", p=P)

        @block.sync
        def _(sp):
            sp.dma_start(cc[:], t["cond"]).then_inc(cond_in, 16)
            sp.dma_start(b[:], t["b_ada"][l].unsqueeze(0).to_broadcast([2, 6 * D])).then_inc(bias_in, 16)
            for n in range(n_chunks):
                if n >= bufs:
                    sp.wait_ge(chunk_done, n - bufs + 1)
                sp.dma_start(w[:, n % bufs], wv[:, :, n * 512:(n + 1) * 512]).then_inc(w_in[n % bufs], 16)
            sp.wait_ge(row_done, n_chunks)
            for i in range(TILES):
                r = 1 if i < CTX_TILES else 0
                sp.dma_start(mods[i:i + 1, :], row[r:r + 1, :]).then_inc(rows_out, 16)
            sp.wait_ge(rows_out, 16 * TILES)

        @block.scalar
        def _(act):
            act.wait_ge(cond_in, 16)
            act.activation(sc[:], cc[:], ACT.Silu).then_inc(silu_done, 1)

        @block.tensor
        def _(pe):
            pe.wait_ge(silu_done, 1)
            for n in range(n_chunks):
                pe.wait_ge(w_in[n % bufs], 16 * (n // bufs + 1))
                if n >= 2:
                    pe.wait_ge(row_done, n - 1)
                for k in range(KT):
                    mm = pe.matmul(ps[:, n % 2, :], sc[:, k, :], w[:, n % bufs, k, :], start=(k == 0), stop=(k == KT - 1))
                mm.then_inc(chunk_done, 1)

        @block.vector
        def _(v):
            v.wait_ge(bias_in, 16)
            for n in range(n_chunks):
                cols = slice(n * 512, (n + 1) * 512)
                v.wait_ge(chunk_done, n + 1)
                one = 1.0 if n // 2 in (1, 4) else 0.0
                v.scalar_tensor_tensor(row[:, cols], ps[:, n % 2, :], one, b[:, cols], ALU.add, ALU.add).then_inc(row_done, 1)


def norm_stage(nc, l, t, h_dram, mods, consts, uT):
    with ExitStack() as es:
        h = es.enter_context(nc.sbuf_tensor("n_h", [P, D], F32))
        m = es.enter_context(nc.sbuf_tensor("n_mod", [P, 2, D], F32))
        stats = es.enter_context(nc.sbuf_tensor("n_stats", [P, 2, 6], F32))
        mv = es.enter_context(nc.sbuf_tensor("n_mv", [P, 8], F32))
        ps = es.enter_context(nc.psum_tensor("n_ps", [P, 2, 4, P], F32))
        with nc.Fori(0, TILES) as i:
            with stage(nc, "h_in", "mod_in", "var_ready", "std_ready", "dve_step", "u_ready", "tr_done", "copied") as \
                    (block, h_in, mod_in, var_ready, std_ready, dve_step, u_ready, tr_done, copied):

                @block.sync
                def _(sp):
                    sp.dma_start(h[:], h_dram[i]).then_inc(h_in, 16)
                    sp.dma_start(m[:], over_rows(mods[i, 0:2 * D]).rearrange("p (a n) -> p a n", a=2)).then_inc(mod_in, 16)

                @block.vector
                def _(v):
                    link = chained(v, dve_step)
                    v.wait_ge(h_in, 16)
                    ln_first(v, link, h, stats, mv, var_ready)
                    ln_last(v, link, h[:], h[:], mv, std_ready, 1)
                    v.wait_ge(mod_in, 16)
                    link(v.tensor_tensor(h[:], h[:], m[:, 1, :], ALU.mult))
                    v.tensor_tensor(h[:], h[:], m[:, 0, :], ALU.add).then_inc(u_ready, 1)

                @block.scalar
                def _(act):
                    act.wait_ge(var_ready, 1)
                    act.activation(mv[:, 3:4], mv[:, 2:3], ACT.Sqrt).then_inc(std_ready, 1)
                    for half in range(2):
                        act.wait_ge(tr_done, half + 1)
                        act.activation(uT[:, 4 * half:4 * half + 4, bass.ds(i * P, P)], ps[:, half], ACT.Copy).then_inc(copied, 1)

                @block.tensor
                def _(pe):
                    pe.wait_ge(u_ready, 1)
                    for half in range(2):
                        for k in range(4):
                            kk = 4 * half + k
                            tr = pe.transpose(ps[:, half, k, :], h[:, kk * P:(kk + 1) * P], consts["ident"][:])
                        tr.then_inc(tr_done, 1)


def project_stage(nc, l, t, p_dram, uT):
    with ExitStack() as es:
        w = es.enter_context(nc.sbuf_tensor("p_w", [P, 2, KT, WCHUNK], F32))
        o = es.enter_context(nc.sbuf_tensor("p_out", [P, 4, WCHUNK], F32))
        ps = es.enter_context(nc.psum_tensor("p_ps", [P, 4, 512], F32))
        wv = t["w_in"][l].rearrange("(k p) n -> p k n", p=P)
        with stage(nc, "first_in") as (block, first_in):
            @block.sync
            def _(sp):
                sp.dma_start(w[:, 0], wv[:, :, 0:WCHUNK]).then_inc(first_in, 16)
                sp.wait_ge(first_in, 16)
        with nc.Fori(0, NCHUNKS // 2) as j:
            with stage(nc, "w0_in", "w1_in", "mm_done", "out_ready", "gone0", "gone1", "gone2", "gone3") as \
                    (block, w0_in, w1_in, mm_done, out_ready, *gone):

                @block.sync
                def _(sp):
                    sp.dma_start(w[:, 1], wv[:, :, bass.ds(j * 2 * WCHUNK + WCHUNK, WCHUNK)]).then_inc(w1_in, 16)
                    sp.wait_ge(mm_done, TILES)
                    nxt = sp.snap((j + 1) % (NCHUNKS // 2))
                    sp.dma_start(w[:, 0], wv[:, :, bass.ds(nxt * 2 * WCHUNK, WCHUNK)]).then_inc(w0_in, 16)
                    sp.wait_ge(w0_in, 16)

                @block.tensor
                def _(pe):
                    for q in range(2 * TILES):
                        ch, i = q // TILES, q % TILES
                        if q == TILES:
                            pe.wait_ge(w1_in, 16)
                        if q >= 4:
                            pe.wait_ge(out_ready, q - 3)
                        for k in range(KT):
                            mm = pe.matmul(ps[:, q % 4, 0:WCHUNK], uT[:, k, i * P:(i + 1) * P], w[:, ch, k, :],
                                           start=(k == 0), stop=(k == KT - 1))
                        mm.then_inc(mm_done, 1)

                @block.vector
                def _(v):
                    for q in range(2 * TILES):
                        v.wait_ge(mm_done, q + 1)
                        if q >= 4:
                            v.wait_ge(gone[q % 4], 16 * (q // 4))
                        v.tensor_copy(o[:, q % 4, :], ps[:, q % 4, 0:WCHUNK]).then_inc(out_ready, 1)

                @block.scalar
                def _(act):
                    for q in range(2 * TILES):
                        ch, i = q // TILES, q % TILES
                        act.wait_ge(out_ready, q + 1)
                        dst = p_dram[1 + i * P:1 + (i + 1) * P, bass.ds(j * 2 * WCHUNK + ch * WCHUNK, WCHUNK)]
                        act.dma_start(dst, o[:, q % 4, :]).then_inc(gone[q % 4], 16)
                    for g in gone:
                        act.wait_ge(g, 16 * 2 * TILES // 4)


def attention_stages(nc, l, t, s, consts):
    with ExitStack() as es:
        sb = lambda n, sh: es.enter_context(nc.sbuf_tensor(n, sh, F32))
        b = {"qA": sb("at_qA", [P, 2, TOK]), "kA": sb("at_kA", [P, 2, TOK]), "qD": sb("at_qD", [P, 2, TOK]),
             "kD": sb("at_kD", [P, 2, TOK]), "vA": sb("at_vA", [P, TILES, GW]), "vD": sb("at_vD", [P, TILES, GW]),
             "lam": sb("at_lam", [P, 8]), "g": sb("at_g", [P, HD])}
        v_src = lambda col: s["p"][1:1 + TOK, col + 2 * GW:col + 3 * GW].rearrange("(i p) n -> p i n", p=P)
        load_once(nc, [(b["vA"][:], v_src(COL_A)), (b["vD"][:], v_src(COL_D))])
        lambda_stage(nc, l, t, b, consts)
        qk_stage(nc, t, s, b, consts)
        attend_stage(nc, s, b, consts, "A", CTX_TILES, TILES, TILES, None)
        attend_stage(nc, s, b, consts, "A", 0, CTX_TILES, CTX_TILES, None)
        attend_stage(nc, s, b, consts, "D", CTX_TILES, TILES, TILES, t["bias"][l])
        attend_stage(nc, s, b, consts, "D", 0, CTX_TILES, CTX_TILES, None)


def lambda_stage(nc, l, t, b, consts):
    with ExitStack() as es:
        lv = es.enter_context(nc.sbuf_tensor("lv", [P, 4, 32], F32))
        pr = es.enter_context(nc.sbuf_tensor("lv_prod", [P, 2, 32], F32))
        lam = b["lam"]
        with stage(nc, "lv_in", "g_in", "dots_ready", "exps_ready", "dve_step") as (block, lv_in, g_in, dots_ready, exps_ready, dve_step):
            @block.sync
            def _(sp):
                sp.dma_start(lv[:].rearrange("p a b -> p (a b)"), over_rows(t["diff_lam"][l])).then_inc(lv_in, 16)
                sp.dma_start(b["g"][:], over_rows(t["diff_norm_g"][l])).then_inc(g_in, 16)

            @block.vector
            def _(v):
                link = chained(v, dve_step)
                v.wait_ge(lv_in, 16)
                for k in range(2):
                    link(v.tensor_tensor(pr[:, k, :], lv[:, 2 * k, :], lv[:, 2 * k + 1, :], ALU.mult))
                v.tensor_reduce(lam[:, 2:4], pr[:], X, ALU.add).then_inc(dots_ready, 1)
                v.wait_ge(exps_ready, 1)
                link(v.tensor_tensor(lam[:, 6:7], lam[:, 4:5], lam[:, 5:6], ALU.subtract))
                link(v.tensor_tensor(lam[:, 0:1], lam[:, 6:7], consts["layer"][:, 0:1], ALU.add))
                v.wait_ge(g_in, 16)
                link(v.tensor_scalar(b["g"][:], b["g"][:], consts["layer"][:, 1:2], None, ALU.mult))

            @block.scalar
            def _(act):
                act.wait_ge(dots_ready, 1)
                act.activation(lam[:, 4:6], lam[:, 2:4], ACT.Exp).then_inc(exps_ready, 1)


def qk_stage(nc, t, s, b, consts):
    with ExitStack() as es:
        sb = lambda n, sh: es.enter_context(nc.sbuf_tensor(n, sh, F32))
        a, d, tab, rot, t2 = sb("qk_a", [P, 512]), sb("qk_d", [P, 512]), sb("qk_tab", [P, 2, 512]), sb("qk_rot", [P, 512]), sb("qk_t2", [P, 512])
        ps = es.enter_context(nc.psum_tensor("qk_ps", [P, 2, 4, P], F32))
        pairs = lambda x: x.rearrange("p (g two e) -> p g two e", two=2, e=8)
        with nc.Fori(0, TILES) as i:
            with stage(nc, "a_in", "d_in", "tab_in", "dve_step", "rot_ready", "tr_done", "copied") as \
                    (block, a_in, d_in, tab_in, dve_step, rot_ready, tr_done, copied):
                @block.sync
                def _(sp):
                    rows = bass.ds(i * P + 1, P)
                    sp.dma_start(a[:], s["p"][rows, COL_A:COL_A + 512]).then_inc(a_in, 16)
                    sp.dma_start(tab[:], t["k_rope"][i].rearrange("p a h e -> p a (h e)")).then_inc(tab_in, 16)
                    sp.dma_start(d[:], s["p"][rows, COL_D:COL_D + 512]).then_inc(d_in, 16)

                @block.vector
                def _(v):
                    link = chained(v, dve_step)
                    v.wait_ge(a_in, 16)
                    v.wait_ge(tab_in, 16)
                    v.tensor_tensor(rot[:], a[:], tab[:, 0], ALU.mult)
                    for x in range(2):
                        mul = v.tensor_tensor(pairs(t2[:])[:, :, x], pairs(a[:])[:, :, 1 - x], pairs(tab[:, 1])[:, :, x], ALU.mult)
                    link(mul)
                    v.tensor_tensor(rot[:], rot[:], t2[:], ALU.add).then_inc(rot_ready, 1)

                @block.tensor
                def _(pe):
                    pe.wait_ge(d_in, 16)
                    for k in range(4):
                        tr = pe.transpose(ps[:, 1, k, :], d[:, k * P:(k + 1) * P], consts["ident"][:])
                    tr.then_inc(tr_done, 1)
                    pe.wait_ge(rot_ready, 1)
                    for k in range(4):
                        tr = pe.transpose(ps[:, 0, k, :], rot[:, k * P:(k + 1) * P], consts["ident"][:])
                    tr.then_inc(tr_done, 1)

                @block.scalar
                def _(act):
                    cols = bass.ds(i * P, P)
                    for n, (bank, q, k) in enumerate(((1, "qD", "kD"), (0, "qA", "kA"))):
                        act.wait_ge(tr_done, n + 1)
                        act.activation(b[q][:, :, cols], ps[:, bank, 0:2], ACT.Copy).then_inc(copied, 1)
                        act.activation(b[k][:, :, cols], ps[:, bank, 2:4], ACT.Copy).then_inc(copied, 1)


def attend_stage(nc, s, b, consts, group, first, last, key_tiles, bias_dram):
    diff = group == "A"
    parts = 2 if diff else 1
    units = HEADS * parts
    nk = key_tiles * P
    scale = 32 ** -0.5 if diff else HD ** -0.5
    qT, kT, vt = b["q" + group], b["k" + group], b["v" + group]
    col = 0 if diff else 3 * GW
    nm = f"at{group}{first}_"
    with ExitStack() as es:
        sb = lambda n, sh: es.enter_context(nc.sbuf_tensor(nm + n, sh, F32))
        q = sb("q", [P, units, P])
        e = sb("e", [P, 4, nk])
        pr = sb("p", [P, 2, nk])
        pt = sb("pt", [P, 2, key_tiles, P])
        st = sb("st", [P, 4, units])
        sx = sb("sx", [P, 2, nk])
        bias = sb("bias", [P, HEADS, SEQ]) if bias_dram is not None else None
        o = sb("o", [P, HEADS, HD])
        sq = sb("sq", [P, HEADS, HD])
        r = sb("r", [P, 3, HEADS])
        ps = es.enter_context(nc.psum_tensor(nm + "ps", [P, 2, 1024], F32))
        pst = es.enter_context(nc.psum_tensor(nm + "pst", [P, 8, P], F32))
        pso = es.enter_context(nc.psum_tensor(nm + "pso", [P, 512], F32))
        with nc.Fori(first, last) as i:
            with stage(nc, "q_ready", "bias_in", "scores_done", "scores_read", "max_ready", "exp_done", "probs_ready", "tr_done",
                       "pt_ready", "av_done", "dve_step", "sq_ready", "sqrt_done", "o_ready", "o_gone") as \
                    (block, q_ready, bias_in, scores_done, scores_read, max_ready, exp_done, probs_ready, tr_done,
                     pt_ready, av_done, dve_step, sq_ready, sqrt_done, o_ready, o_gone):

                @block.sync
                def _(sp):
                    if bias_dram is not None:
                        sp.dma_start(bias[:], bias_dram[i - first]).then_inc(bias_in, 16)
                    sp.wait_ge(o_ready, 1)
                    sp.dma_start(s["y"][bass.ds(i * P, P), col:col + GW], o[:].rearrange("p h e -> p (h e)")).then_inc(o_gone, 16)
                    sp.wait_ge(o_gone, 16)

                @block.tensor
                def _(pe):
                    def score(u):
                        h = u // parts
                        if u >= 2:
                            pe.wait_ge(scores_read, u - 1)
                        for c0 in range(0, nk, 512):
                            c1 = min(nk, c0 + 512)
                            mm = pe.matmul(ps[:, u % 2, c0:c1], q[:, u, :], kT[:, h // 2, c0:c1], start=True, stop=True)
                        mm.then_inc(scores_done, 1)

                    pe.wait_ge(q_ready, 1)
                    for u in range(parts):
                        score(u)
                    for h in range(HEADS):
                        if h + 1 < HEADS:
                            for u in range(parts * (h + 1), parts * (h + 2)):
                                score(u)
                        pe.wait_ge(probs_ready, h + 1)
                        if h >= 1:
                            pe.wait_ge(pt_ready, h)
                        for k in range(key_tiles):
                            tr = pe.transpose(pst[:, k, :], pr[:, h % 2, k * P:(k + 1) * P], consts["ident"][:])
                        tr.then_inc(tr_done, 1)
                        pe.wait_ge(pt_ready, h + 1)
                        for k in range(key_tiles):
                            mm = pe.matmul(pso[:, h * HD:(h + 1) * HD], pt[:, h % 2, k, :], vt[:, k, h * HD:(h + 1) * HD],
                                           start=(k == 0), stop=(k == key_tiles - 1))
                        mm.then_inc(av_done, 1)

                @block.scalar
                def _(act):
                    for h in range(HEADS + 1):
                        if h < HEADS:
                            for u in range(parts * h, parts * (h + 1)):
                                act.wait_ge(max_ready, u + 1)
                                if u >= 4:
                                    act.wait_ge(probs_ready, (u - 4) // parts + 1)
                                src = sx[:, u % 2, :] if bias is not None else ps[:, u % 2, 0:nk]
                                act.activation(e[:, u % 4, :], src, ACT.Exp, bias=st[:, 1, u:u + 1],
                                               scale=1.0 if bias is not None else scale,
                                               accum_out=st[:, 2, u:u + 1]).then_inc(exp_done, 1)
                                if bias is None:
                                    act.wait_ge(exp_done, u + 1)
                                    act.sem_inc(scores_read, 1)
                        if h >= 1:
                            act.wait_ge(tr_done, h)
                            if h >= 3:
                                act.wait_ge(av_done, h - 2)
                            act.activation(pt[:, (h - 1) % 2], pst[:, 0:key_tiles, :], ACT.Copy).then_inc(pt_ready, 1)
                    if diff:
                        act.wait_ge(sq_ready, 1)
                        act.activation(r[:, 1, :], r[:, 0, :], ACT.Sqrt).then_inc(sqrt_done, 1)

                @block.vector
                def _(v):
                    link = chained(v, dve_step)
                    for u in range(units):
                        h = u // parts
                        row = 2 + (h % 2) * 2 + u % 2 if diff else h % 2
                        mask = v.tensor_scalar(q[:, u, :], qT[:, h // 2, bass.ds(i * P, P)], consts["rows"][:, row:row + 1], None, ALU.mult)
                    mask.then_inc(q_ready, 1)
                    if bias is not None:
                        v.wait_ge(bias_in, 16)

                    def maximum(u):
                        v.wait_ge(scores_done, u + 1)
                        src = ps[:, u % 2, 0:nk]
                        if bias is not None:
                            if u >= 2:
                                v.wait_ge(exp_done, u - 1)
                            link(v.tensor_scalar(sx[:, u % 2, 0:CTX], ps[:, u % 2, 0:CTX], scale, None, ALU.mult))
                            ins = link(v.scalar_tensor_tensor(sx[:, u % 2, CTX:nk], ps[:, u % 2, CTX:nk], scale, bias[:, u, :], ALU.mult, ALU.add))
                            v.sem_inc(scores_read, 1)
                            src = sx[:, u % 2, :]
                        link(v.tensor_reduce(st[:, 0, u:u + 1], src, X, ALU.max))
                        v.tensor_scalar(st[:, 1, u:u + 1], st[:, 0, u:u + 1], -1.0 if bias is not None else -scale, None, ALU.mult).then_inc(max_ready, 1)

                    for u in range(parts):
                        maximum(u)
                    for h in range(HEADS):
                        if h + 1 < HEADS:
                            for u in range(parts * (h + 1), parts * (h + 2)):
                                maximum(u)
                        u = parts * h
                        v.wait_ge(exp_done, u + parts)
                        if h >= 2:
                            v.wait_ge(tr_done, h - 1)
                        link(v.reciprocal(st[:, 3, u:u + parts], st[:, 2, u:u + parts]))
                        if diff:
                            x1, x2 = u, u + 1
                            link(v.tensor_scalar(e[:, x2 % 4, :], e[:, x2 % 4, :], st[:, 3, x2:x2 + 1], b["lam"][:, 0:1], ALU.mult, ALU.mult))
                            v.scalar_tensor_tensor(pr[:, h % 2, :], e[:, x1 % 4, :], st[:, 3, x1:x1 + 1], e[:, x2 % 4, :],
                                                   ALU.mult, ALU.subtract).then_inc(probs_ready, 1)
                        else:
                            v.tensor_scalar(pr[:, h % 2, :], e[:, u % 4, :], st[:, 3, u:u + 1], None, ALU.mult).then_inc(probs_ready, 1)
                    v.wait_ge(av_done, HEADS)
                    out = v.tensor_copy(o[:].rearrange("p h e -> p (h e)"), pso[:, 0:GW])
                    if not diff:
                        out.then_inc(o_ready, 1)
                        return
                    link(out)
                    link(v.tensor_tensor(sq[:], o[:], o[:], ALU.mult))
                    link(v.tensor_reduce(r[:, 2, :], sq[:], X, ALU.add))
                    v.tensor_scalar(r[:, 0, :], r[:, 2, :], 1.0 / HD, NORM_EPS, ALU.mult, ALU.add).then_inc(sq_ready, 1)
                    v.wait_ge(sqrt_done, 1)
                    link(v.reciprocal(r[:, 2, :], r[:, 1, :]))
                    link(v.tensor_tensor(o[:], o[:], r[:, 2, :].unsqueeze(2).to_broadcast([P, HEADS, HD]), ALU.mult))
                    v.tensor_tensor(o[:], o[:], b["g"][:].unsqueeze(1).to_broadcast([P, HEADS, HD]), ALU.mult).then_inc(o_ready, 1)


def head_bc(x):
    return x.unsqueeze(2).to_broadcast(list(x.shape) + [HD])


def by_head(x):
    return x.rearrange("p (h e) -> p h e", e=HD)


def scan_stages(nc, l, t, s, consts):
    rwkv_prep_stage(nc, l, t, s, consts)
    gdn_prep_stage(nc, l, t, s, consts)
    chunk_stage(nc, t, s, consts)
    scan_post_stage(nc, l, t, s, consts)


def store_chunks(eng, dst, src, i, sem):
    n = 0
    nq = src.shape[2]
    for d in range(2):
        for half in range(2):
            for tile in ([i] if d == 0 else [i, i + TILES]):
                eng.dma_start(dst[tile, half, d].rearrange("q a b t e -> t (q a b) e"),
                              src[half * C:(half + 1) * C, d].rearrange("t q (h e) -> t (q h) e", e=HD)).then_inc(sem, 16)
                n += 16
    return n


def rwkv_prep_stage(nc, l, t, s, consts):
    W = RWKV_COLS
    with ExitStack() as es:
        sb = lambda n, sh: es.enter_context(nc.sbuf_tensor("rp_" + n, sh, F32))
        mu, w2, a2, g2 = sb("mu", [P, 3, W]), sb("w2", [P, 2, GW]), sb("a2", [P, 2, GW]), sb("g2", [P, GW])
        w0, a0, kk_g, ka_g, rk_g = sb("w0", [P, 2 * GW]), sb("a0", [P, 2 * GW]), sb("kkg", [P, GW]), sb("kag", [P, GW]), sb("rkg", [P, GW])
        f, fp, fn, edge = sb("f", [P, W]), sb("fp", [P, W]), sb("fn", [P, W]), sb("edge", [P, 2])
        low, lowT = sb("low", [P, 2, P]), sb("lowT", [P, 3, P])
        wr, ar, sg, ex, av = [sb(n, [P, 2, GW]) for n in ("wr", "ar", "sg", "ex", "av")]
        e_in, e_neg, e_ex, dec = [sb(n, [P, 2, GW]) for n in ("ein", "eneg", "eex", "dec")]
        kk, sq, kd, kka = sb("kk", [P, GW]), sb("sq", [P, GW]), sb("kd", [P, 2, GW]), sb("kka", [P, 2, GW])
        n4 = sb("n4", [P, 4, HEADS])
        out, post, rks = sb("out", [P, 2, 5, GW]), sb("post", [P, 2, GW]), sb("rks", [P, 2, GW])
        ps = es.enter_context(nc.psum_tensor("rp_ps", [P, 6, 512], F32))
        flat = lambda x: x[:].rearrange("p a b -> p (a b)")
        over_dir = lambda x: x.unsqueeze(1).to_broadcast([P, 2, GW])

        with stage(nc, "zeroed", "params_in", "mid") as (block, zeroed, params_in, mid):
            @block.gpsimd
            def _(pool):
                pool.memset(w2[:], 0.0).then_inc(zeroed, 1)
                pool.memset(a2[:], 0.0).then_inc(zeroed, 1)

            @block.sync
            def _(sp):
                loads = [(mu[:, 0], over_rows(t["rwkv_mu"][l, 0])), (mu[:, 2], over_rows(t["rwkv_mu"][l, 1])), (g2[:], t["rwkv_g2"][l]),
                         (w0[:], over_rows(t["rwkv_w0"][l])), (a0[:], over_rows(t["rwkv_a0"][l])), (kk_g[:], over_rows(t["rwkv_kk"][l])),
                         (ka_g[:], over_rows(t["rwkv_ka"][l])), (rk_g[:], over_rows(t["rwkv_rk"][l]))]
                sp.wait_ge(zeroed, 2)
                for d in range(2):
                    for dst, src in ((w2, "rwkv_w2"), (a2, "rwkv_a2")):
                        loads.append((dst[d * LORA:(d + 1) * LORA, d, :], t[src][l, d]))
                for dst, src in loads:
                    sp.dma_start(dst, src).then_inc(params_in, 16)
                sp.wait_ge(params_in, 16 * len(loads))

            @block.vector
            def _(v):
                v.wait_ge(params_in, 16 * 12)
                v.tensor_tensor(mu[:, 1], mu[:, 0], mu[:, 2], ALU.add).then_inc(mid, 1)
                v.wait_ge(mid, 1)
                v.tensor_scalar(mu[:, 1], mu[:, 1], -1.0, 1.0, ALU.mult, ALU.add)

        with nc.Fori(0, TILES) as i:
            with stage(nc, "f_in", "sides_in", "sides_ready", "f_ready", "low_ready", "low_done", "lowT_ready", "raw_done", "raw_ready",
                       "gates_ready", "g_copied", "sums_done", "ex_ready", "exps_ready", "sq_ready", "root_ready", "dve_step", "out_ready",
                       "stored") as \
                    (block, f_in, sides_in, sides_ready, f_ready, low_ready, low_done, lowT_ready, raw_done, raw_ready,
                     gates_ready, g_copied, sums_done, ex_ready, exps_ready, sq_ready, root_ready, dve_step, out_ready, stored):
                @block.sync
                def _(sp):
                    cols = slice(COL_B, COL_B + W)
                    sp.dma_start(f[:], s["p"][bass.ds(i * P + 1, P), cols]).then_inc(f_in, 16)
                    sp.dma_start(edge[:], t["k_edges"][i]).then_inc(f_in, 16)
                    sp.dma_start(fp[:], s["p"][bass.ds(i * P, P), cols]).then_inc(sides_in, 16)
                    sp.dma_start(fn[:], s["p"][bass.ds(i * P + 2, P), cols]).then_inc(sides_in, 16)
                    sp.wait_ge(out_ready, 1)
                    n = store_chunks(sp, s["rw"], out[:], i, stored)
                    for tile in (i, i + TILES):
                        sp.dma_start(s["rwdec"][bass.ds(tile * 2, 2)].rearrange("c d g -> c (d g)"),
                                     dec[0:C + 1:C].rearrange("c d g -> c (d g)")).then_inc(stored, 16)
                        n += 16
                    sp.dma_start(s["rwpost"][i], post[:]).then_inc(stored, 16)
                    sp.wait_ge(stored, n + 16)

                @block.gpsimd
                def _(pool):
                    pool.wait_ge(sides_in, 32)
                    pool.tensor_tensor(fp[:], fp[:], mu[:, 0], ALU.mult).then_inc(sides_ready, 1)
                    pool.tensor_tensor(fn[:], fn[:], mu[:, 2], ALU.mult).then_inc(sides_ready, 1)

                @block.vector
                def _(v):
                    link = chained(v, dve_step)
                    r, k, val = f[:, 0:GW], f[:, GW:2 * GW], f[:, 2 * GW:3 * GW]
                    v.wait_ge(f_in, 32)
                    link(v.tensor_tensor(f[:], f[:], mu[:, 1], ALU.mult))
                    v.wait_ge(sides_ready, 1)
                    link(v.scalar_tensor_tensor(f[:], fp[:], edge[:, 0:1], f[:], ALU.mult, ALU.add))
                    v.wait_ge(sides_ready, 2)
                    link(v.scalar_tensor_tensor(f[:], fn[:], edge[:, 1:2], f[:], ALU.mult, ALU.add))
                    v.sem_inc(f_ready, 1)
                    link(v.tensor_tensor(kk[:], k, kk_g[:], ALU.mult))
                    link(v.tensor_tensor(sq[:], kk[:], kk[:], ALU.mult))
                    link(v.tensor_reduce(n4[:, 0, :], by_head(sq[:]), X, ALU.add))
                    v.tensor_scalar(n4[:, 1, :], n4[:, 0, :], NORM_EPS, None, ALU.add).then_inc(sq_ready, 1)
                    v.wait_ge(raw_done, 1)
                    v.tensor_tensor(flat(wr), ps[:, 1, :], w0[:], ALU.add).then_inc(raw_ready, 1)
                    v.wait_ge(raw_done, 2)
                    v.tensor_tensor(flat(ar), ps[:, 2, :], a0[:], ALU.add).then_inc(raw_ready, 1)
                    v.wait_ge(root_ready, 1)
                    link(v.reciprocal(n4[:, 3, :], n4[:, 2, :]))
                    link(v.tensor_tensor(by_head(kk[:]), by_head(kk[:]), head_bc(n4[:, 3, :]), ALU.mult))
                    v.wait_ge(gates_ready, 2)
                    link(v.tensor_tensor(kka[:], av[:], over_dir(kk[:]), ALU.mult))
                    link(v.scalar_tensor_tensor(kd[:], av[:], -1.0, over_dir(ka_g[:]), ALU.add, ALU.mult))
                    link(v.scalar_tensor_tensor(kd[:], kd[:], 1.0, over_dir(k), ALU.add, ALU.mult))
                    v.wait_ge(sums_done, 1)
                    v.tensor_tensor(flat(ex), ps[:, 4, :], flat(sg), ALU.subtract).then_inc(ex_ready, 1)
                    link(v.tensor_tensor(rks[:, 0], r, rk_g[:], ALU.mult))
                    link(v.tensor_tensor(sq[:], kd[:, 0], kd[:, 1], ALU.add))
                    link(v.tensor_tensor(rks[:, 1], rks[:, 0], sq[:], ALU.mult))
                    link(v.tensor_reduce(n4[:, 0, :], by_head(rks[:, 1]), X, ALU.add))
                    link(v.tensor_tensor(by_head(post[:, 0]), by_head(val), head_bc(n4[:, 0, :]), ALU.mult))
                    v.tensor_copy(out[:, :, 4], over_dir(val))
                    v.wait_ge(exps_ready, 4)
                    v.tensor_tensor(out[:, :, 0], e_ex[:], over_dir(kk[:]), ALU.mult)
                    v.tensor_tensor(out[:, :, 1], e_neg[:], kka[:], ALU.mult)
                    v.tensor_tensor(out[:, :, 2], e_neg[:], kd[:], ALU.mult)
                    v.wait_ge(g_copied, 1)
                    link(v.tensor_tensor(out[:, :, 3], e_in[:], over_dir(r), ALU.mult))
                    v.sem_inc(out_ready, 1)

                @block.scalar
                def _(act):
                    act.wait_ge(f_ready, 1)
                    act.activation(low[:, 0], f[:, 3 * GW:3 * GW + P], ACT.Tanh).then_inc(low_ready, 1)
                    act.activation(low[:, 1], f[:, 3 * GW + 2 * P:3 * GW + 3 * P], ACT.Sigmoid).then_inc(low_ready, 1)
                    act.wait_ge(low_done, 1)
                    act.activation(lowT[:], ps[:, 0, 0:3 * P].rearrange("p (a b) -> p a b", a=3), ACT.Copy).then_inc(lowT_ready, 1)
                    act.wait_ge(raw_ready, 1)
                    act.activation(flat(sg), flat(wr), ACT.Sigmoid).then_inc(gates_ready, 1)
                    act.wait_ge(raw_ready, 2)
                    act.activation(flat(av), flat(ar), ACT.Sigmoid).then_inc(gates_ready, 1)
                    act.wait_ge(raw_done, 3)
                    act.activation(post[:, 1], ps[:, 3, 0:GW], ACT.Copy).then_inc(g_copied, 1)
                    act.wait_ge(sq_ready, 1)
                    act.activation(n4[:, 2, :], n4[:, 1, :], ACT.Sqrt).then_inc(root_ready, 1)
                    act.wait_ge(ex_ready, 1)
                    act.activation(flat(e_in), ps[:, 4, :], ACT.Exp, scale=DECAY).then_inc(exps_ready, 1)
                    act.activation(flat(e_neg), ps[:, 4, :], ACT.Exp, scale=-DECAY).then_inc(exps_ready, 1)
                    act.activation(flat(e_ex), flat(ex), ACT.Exp, scale=DECAY).then_inc(exps_ready, 1)
                    act.wait_ge(sums_done, 2)
                    act.activation(flat(dec), ps[:, 5, :], ACT.Exp, scale=DECAY).then_inc(exps_ready, 1)

                @block.tensor
                def _(pe):
                    pe.wait_ge(low_ready, 2)
                    for n, src in enumerate((low[:, 0], f[:, 3 * GW + P:3 * GW + 2 * P], low[:, 1])):
                        tr = pe.transpose(ps[:, 0, n * P:(n + 1) * P], src, consts["ident"][:])
                    tr.then_inc(low_done, 1)
                    pe.wait_ge(lowT_ready, 1)
                    pe.matmul(ps[:, 1, :], lowT[:, 0], flat(w2), start=True, stop=True).then_inc(raw_done, 1)
                    pe.matmul(ps[:, 2, :], lowT[:, 1], flat(a2), start=True, stop=True).then_inc(raw_done, 1)
                    pe.matmul(ps[:, 3, 0:GW], lowT[:, 2], g2[:], start=True, stop=True).then_inc(raw_done, 1)
                    pe.wait_ge(gates_ready, 1)
                    for d in range(2):
                        mm = pe.matmul(ps[:, 4, d * GW:(d + 1) * GW], consts["sums"][:, d, :], sg[:, d], start=True, stop=True)
                    mm.then_inc(sums_done, 1)
                    pe.matmul(ps[:, 5, :], consts["sums"][:, 2, :], flat(sg), start=True, stop=True).then_inc(sums_done, 1)


def gdn_prep_stage(nc, l, t, s, consts):
    W = GDN_QKV
    ND = 2 * HEADS
    with ExitStack() as es:
        sb = lambda n, sh: es.enter_context(nc.sbuf_tensor("gp_" + n, sh, F32))
        cw, alog, dtb = sb("cw", [P, 3, W]), sb("alog", [P, ND]), sb("dtb", [P, ND])
        f, fp, fn, edge = sb("f", [P, GDN_COLS]), sb("fp", [P, W]), sb("fn", [P, W]), sb("edge", [P, 2])
        qkv, sq, n8 = sb("qkv", [P, W]), sb("sq", [P, 2 * GW]), sb("n8", [P, 5, ND])
        x8 = sb("x8", [P, 16, ND])
        cols = sb("cols", [P, 2, ND])
        cols_b = sb("cols_b", [P, 2, 2 * ND // 2])
        out, post = sb("out", [P, 2, 7, GW]), sb("post", [P, GW])
        ps = es.enter_context(nc.psum_tensor("gp_ps", [P, 512], F32))
        with stage(nc, "params_in", "exp_done") as (block, params_in, exp_done):
            @block.sync
            def _(sp):
                loads = [(cw[:, k], over_rows(t["gdn_conv"][l, k])) for k in range(3)]
                loads += [(alog[:], over_rows(t["gdn_a_log"][l])), (dtb[:], over_rows(t["gdn_dt_bias"][l]))]
                for dst, src in loads:
                    sp.dma_start(dst, src).then_inc(params_in, 16)
                sp.wait_ge(params_in, 16 * len(loads))

            @block.scalar
            def _(act):
                act.wait_ge(params_in, 16 * 5)
                act.activation(alog[:], alog[:], ACT.Exp).then_inc(exp_done, 1)

        with nc.Fori(0, TILES) as i:
            with stage(nc, "f_in", "sides_in", "sides_ready", "conv_ready", "qkv_ready", "gate_ready", "beta_ready", "abs_ready", "exp_ready",
                       "sq_ready", "root_ready", "g_ready", "sums_done", "dec_ready", "exps_ready", "dve_step", "out_ready", "stored") as \
                    (block, f_in, sides_in, sides_ready, conv_ready, qkv_ready, gate_ready, beta_ready, abs_ready, exp_ready,
                     sq_ready, root_ready, g_ready, sums_done, dec_ready, exps_ready, dve_step, out_ready, stored):
                @block.sync
                def _(sp):
                    sp.dma_start(f[:], s["p"][bass.ds(i * P + 1, P), COL_C:COL_C + GDN_COLS]).then_inc(f_in, 16)
                    sp.dma_start(edge[:], t["k_edges"][i]).then_inc(f_in, 16)
                    sp.dma_start(fp[:], s["p"][bass.ds(i * P, P), COL_C:COL_C + W]).then_inc(sides_in, 16)
                    sp.dma_start(fn[:], s["p"][bass.ds(i * P + 2, P), COL_C:COL_C + W]).then_inc(sides_in, 16)
                    sp.wait_ge(out_ready, 1)
                    n = store_chunks(sp, s["gd"], out[:], i, stored)
                    for tile in (i, i + TILES):
                        for half in range(2):
                            sp.dma_start(s["gdcol"][tile * 2 + half].rearrange("b t m -> t b m"),
                                         cols_b[half * C:(half + 1) * C]).then_inc(stored, 16)
                            n += 16
                    sp.dma_start(s["gdpost"][i], post[:]).then_inc(stored, 16)
                    sp.wait_ge(stored, n + 16)

                @block.gpsimd
                def _(pool):
                    pool.wait_ge(sides_in, 32)
                    pool.tensor_tensor(fp[:], fp[:], cw[:, 0], ALU.mult).then_inc(sides_ready, 1)
                    pool.tensor_tensor(fn[:], fn[:], cw[:, 2], ALU.mult).then_inc(sides_ready, 1)

                @block.vector
                def _(v):
                    link = chained(v, dve_step)
                    v.wait_ge(f_in, 32)
                    x, neg, ax, u, den, z, z2, acc, top, g = [x8[:, k, :] for k in range(10)]
                    link(v.tensor_tensor(x, f[:, 4 * GW:4 * GW + ND], dtb[:], ALU.add))
                    link(v.tensor_scalar(neg, x, -1.0, None, ALU.mult))
                    v.tensor_tensor(ax, x, neg, ALU.max).then_inc(abs_ready, 1)
                    link(v.tensor_scalar(top, x, 0.0, None, ALU.max))
                    link(v.tensor_tensor(qkv[:], f[:, 0:W], cw[:, 1], ALU.mult))
                    v.wait_ge(sides_ready, 1)
                    link(v.scalar_tensor_tensor(qkv[:], fp[:], edge[:, 0:1], qkv[:], ALU.mult, ALU.add))
                    v.wait_ge(sides_ready, 2)
                    v.scalar_tensor_tensor(qkv[:], fn[:], edge[:, 1:2], qkv[:], ALU.mult, ALU.add).then_inc(conv_ready, 1)
                    v.wait_ge(exp_ready, 1)
                    link(v.tensor_scalar(den, u, 2.0, None, ALU.add))
                    link(v.reciprocal(z2, den))
                    link(v.tensor_tensor(z, u, z2, ALU.mult))
                    link(v.tensor_tensor(z2, z, z, ALU.mult))
                    link(v.tensor_scalar(acc, z2, 2.0 / 19, 2.0 / 17, ALU.mult, ALU.add))
                    for k in (15, 13, 11, 9, 7, 5, 3, 1):
                        link(v.tensor_tensor(acc, acc, z2, ALU.mult))
                        link(v.tensor_scalar(acc, acc, 2.0 / k, None, ALU.add))
                    link(v.tensor_tensor(acc, acc, z, ALU.mult))
                    link(v.tensor_tensor(acc, acc, top, ALU.add))
                    v.scalar_tensor_tensor(g, acc, -1.0, alog[:], ALU.mult, ALU.mult).then_inc(g_ready, 1)
                    v.wait_ge(qkv_ready, 1)
                    link(v.tensor_tensor(sq[:], qkv[:, 0:2 * GW], qkv[:, 0:2 * GW], ALU.mult))
                    link(v.tensor_reduce(n8[:, 0, :], by_head(sq[:]), X, ALU.add))
                    v.tensor_scalar(n8[:, 1, :], n8[:, 0, :], NORM_EPS, None, ALU.add).then_inc(sq_ready, 1)
                    v.wait_ge(sums_done, 1)
                    gc, gap = cols[:, 0], x8[:, 10, :]
                    link(v.tensor_copy(cols[:], ps[:, 0:2 * ND].rearrange("p (a n) -> p a n", a=2)))
                    for b in range(2):
                        v.tensor_copy(cols_b[:, b], cols[:].rearrange("p w (m b) -> p (w m) b", b=2)[:, :, b])
                    v.tensor_tensor(gap, cols[:, 1], gc, ALU.subtract).then_inc(dec_ready, 1)
                    v.wait_ge(root_ready, 1)
                    link(v.reciprocal(n8[:, 3, :], n8[:, 2, :]))
                    link(v.tensor_scalar(n8[:, 3, 0:HEADS], n8[:, 3, 0:HEADS], HD ** -0.5, None, ALU.mult))
                    link(v.tensor_tensor(by_head(qkv[:, 0:2 * GW]), by_head(qkv[:, 0:2 * GW]), head_bc(n8[:, 3, :]), ALU.mult))
                    v.wait_ge(exps_ready, 2)
                    v.wait_ge(beta_ready, 1)
                    beta, egc, egap, bg = x8[:, 11, :], x8[:, 12, :], x8[:, 13, :], x8[:, 14, :]
                    link(v.tensor_tensor(bg, beta, egc, ALU.mult))
                    q, k, val = [qkv[:, a * GW:(a + 1) * GW] for a in range(3)]
                    for d in range(2):
                        hs = slice(d * HEADS, (d + 1) * HEADS)
                        for n, (src, by) in enumerate(((k, bg), (k, beta), (k, None), (q, None), (q, egc), (k, egap), (val, beta))):
                            if by is None:
                                last = v.tensor_copy(out[:, d, n], src)
                            else:
                                last = v.tensor_tensor(by_head(out[:, d, n]), by_head(src), head_bc(by[:, hs]), ALU.mult)
                    link(last)
                    v.wait_ge(gate_ready, 1)
                    v.sem_inc(out_ready, 1)

                @block.scalar
                def _(act):
                    act.wait_ge(f_in, 32)
                    act.activation(post[:], f[:, 3 * GW:4 * GW], ACT.Silu).then_inc(gate_ready, 1)
                    act.wait_ge(conv_ready, 1)
                    act.activation(qkv[:], qkv[:], ACT.Silu).then_inc(qkv_ready, 1)
                    act.activation(x8[:, 11, :], f[:, 4 * GW + ND:4 * GW + 2 * ND], ACT.Sigmoid).then_inc(beta_ready, 1)
                    act.wait_ge(abs_ready, 1)
                    act.activation(x8[:, 3, :], x8[:, 2, :], ACT.Exp, scale=-1.0).then_inc(exp_ready, 1)
                    act.wait_ge(sq_ready, 1)
                    act.activation(n8[:, 2, :], n8[:, 1, :], ACT.Sqrt).then_inc(root_ready, 1)
                    act.wait_ge(dec_ready, 1)
                    act.activation(x8[:, 12, :], cols[:, 0], ACT.Exp).then_inc(exps_ready, 1)
                    act.activation(x8[:, 13, :], x8[:, 10, :], ACT.Exp).then_inc(exps_ready, 1)

                @block.tensor
                def _(pe):
                    pe.wait_ge(g_ready, 1)
                    g = x8[:, 9, :]
                    for d in range(2):
                        pe.matmul(ps[:, d * HEADS:(d + 1) * HEADS], consts["sums"][:, d, :], g[:, d * HEADS:(d + 1) * HEADS], start=True, stop=True)
                    pe.matmul(ps[:, ND:2 * ND], consts["sums"][:, 2, :], g, start=True, stop=True).then_inc(sums_done, 1)


def chunk_stage(nc, t, s, consts):
    NQ = (4, 6)
    NT = (4, 5)
    N4 = 4
    with ExitStack() as es:
        sb = lambda n, sh: es.enter_context(nc.sbuf_tensor("ch_" + n, sh, F32))
        masks = sb("masks", [P, 14, N4, P])
        bd = [sb(f"bd{k}", [P, 2, NQ[k], 2, P]) for k in range(2)]
        val = [sb(f"val{k}", [P, 2, 2, HD]) for k in range(2)]
        tq = [sb(f"tq{k}", [P, NT[k], N4, P]) for k in range(2)]
        am = [sb(f"am{k}", [P, 2, N4, P]) for k in range(2)]
        m = [sb(f"m{k}", [P, 6, 2, N4, P]) for k in range(2)]
        x = [sb(f"x{k}", [P, 2, N4, P]) for k in range(2)]
        y = [sb(f"y{k}", [P, N4, P]) for k in range(2)]
        akt, rk, rb, qk = [sb(n, [P, N4, P]) for n in ("akt", "rk", "rb", "qk")]
        diag, du, dd = sb("diag", [P, N4, P]), sb("du", [P, 2, N4, P]), sb("dd", [P, 2, N4, P])
        st = [sb(f"st{k}", [P, N4, HD]) for k in range(2)]
        rhs = [sb(f"rhs{k}", [P, N4, HD]) for k in range(2)]
        nn = [sb(f"nn{k}", [P, N4, HD]) for k in range(2)]
        oo = [sb(f"oo{k}", [P, N4, HD]) for k in range(2)]
        col = sb("col", [P, 2, 2, 2])
        dec = [sb(f"dec{k}", [P, N4]) for k in range(2)]
        ones = sb("ones", [P, P])
        ps = es.enter_context(nc.psum_tensor("ch_ps", [P, 8, N4, P], F32))
        prob = lambda n: (n // 2, n % 2)
        src_dram = (s["rw"], s["gd"])

        with stage(nc, "masks_in") as (block, masks_in):
            @block.sync
            def _(sp):
                sp.dma_start(masks[:], t["k_masks"]).then_inc(masks_in, 16)
                sp.wait_ge(masks_in, 16)

            @block.gpsimd
            def _(pool):
                for k in range(2):
                    pool.memset(bd[k][:], 0.0)
                    pool.memset(st[k][:], 0.0)
                pool.memset(ones[:], 1.0)

        names = ["rw_in", "gd_in", "col_in", "dec_in", "diag_ready", "diffs_done", "du_ready", "dd_ready", "ddm_ready", "tr_done",
                 "tr_copied", "gram_done", "gram_ready", "m_ready", "x_ready", "y_done", "y_ready", "z_done", "z_read", "rhs_done", "rhs_ready0",
                 "rhs_ready1", "n_done", "n_ready", "o_done", "o_ready", "ds_done", "dve_step", "gdec_ready", "stored", "state_step"]
        with nc.Fori(0, CHUNKS) as c:
            with stage(nc, *names) as (block, rw_in, gd_in, col_in, dec_in, diag_ready, diffs_done, du_ready, dd_ready, ddm_ready, tr_done,
                                       tr_copied, gram_done, gram_ready, m_ready, x_ready, y_done, y_ready, z_done, z_read, rhs_done, rhs_ready0,
                                       rhs_ready1, n_done, n_ready, o_done, o_ready, ds_done, dve_step, gdec_ready, stored, state_step):
                fwd, bwd = c, 15 - c

                @block.sync
                def _(sp):
                    def load(k, d, at, sem):
                        src = src_dram[k].rearrange("i c d q a b t e -> (i c) d q a b t e")[at, d]
                        for b in range(2):
                            sp.dma_start(bd[k][b * C:(b + 1) * C, d, :, :, b * C:(b + 1) * C].rearrange("t q a e -> t (q a) e"),
                                         src[0:NQ[k], :, b].rearrange("q a t e -> t (q a) e")).then_inc(sem, 16)
                        sp.dma_start(val[k][:, d], src[NQ[k]].rearrange("a b t e -> (b t) a e")).then_inc(sem, 16)

                    for d, at in enumerate((fwd, bwd)):
                        sp.dma_start(col[:, :, d], s["gdcol"][at].rearrange("b t (w d a) -> d (b t) w a", w=2, d=2)[d]).then_inc(col_in, 16)
                    for k, sem in enumerate((rw_in, gd_in)):
                        for d, at in enumerate((fwd, bwd)):
                            load(k, d, at, sem)
                    for d, at in enumerate((fwd, bwd)):
                        sp.dma_start(dec[0][:, 2 * d:2 * d + 2], s["rwdec"][at, d].rearrange("(a p) -> p a", p=P),
                                     allow_slow_non_contiguous=True).then_inc(dec_in, 16)
                    n = 0
                    for k in range(2):
                        sp.wait_ge(o_ready, k + 1)
                        for b in range(2):
                            for d, at in ((0, c), (1, 23 - c), (1, 11 - c)):
                                sp.dma_start(s["scan"][k, d, at].rearrange("t (a b e) -> b t a e", a=2, b=2)[b],
                                             oo[k][b * C:(b + 1) * C, 2 * d:2 * d + 2]).then_inc(stored, 16)
                                n += 16
                    sp.wait_ge(stored, n)

                @block.gpsimd
                def _(pool):
                    for lev in range(6):
                        for k in range(2):
                            for w in range(2):
                                if lev == 0:
                                    pool.wait_ge(gram_ready, 2 * k + w + 1)
                                pool.tensor_tensor(m[k][:, lev, w], am[k][:, w], masks[:, 2 + 2 * lev + w], ALU.mult).then_inc(m_ready, 1)

                @block.tensor
                def _(pe):
                    pe.wait_ge(diag_ready, 1)
                    pe.matmul(ps[:, 7].rearrange("p a b -> p (a b)"), ones[:], diag[:].rearrange("p a b -> p (a b)"), start=True, stop=True).then_inc(diffs_done, 1)
                    g = 0
                    for k, sem in ((0, rw_in), (1, gd_in)):
                        pe.wait_ge(sem, 16 * 6)
                        for q in range(NT[k]):
                            if g >= 4:
                                pe.wait_ge(tr_copied, g - 3)
                            for n in range(N4):
                                d, a = prob(n)
                                tr = pe.transpose(ps[:, g % 4, n, :], bd[k][:, d, q, a, :], consts["ident"][:])
                            tr.then_inc(tr_done, 1)
                            g += 1
                    grams = [(0, 0, 1), (0, 1, 0), (1, 1, 2), (1, 2, 1), (0, 2, 0), (0, 2, 3), (0, 1, 3), (1, 2, 3)]
                    for g, (k, left, right) in enumerate(grams):
                        pe.wait_ge(tr_copied, 4 if k == 0 else 9)
                        if g >= 3:
                            pe.wait_ge(gram_ready, g - 2)
                        for n in range(N4):
                            mm = pe.matmul(ps[:, 4 + g % 3, n, :], tq[k][:, left, n, :], tq[k][:, right, n, :], start=True, stop=True)
                        mm.then_inc(gram_done, 1)
                    pe.wait_ge(gram_ready, 8)
                    for lev in range(1, 6):
                        for k in range(2):
                            pe.wait_ge(x_ready, 2 * (lev - 1) + k + 1)
                            pe.wait_ge(m_ready, 4 * lev + 2 * k + 2)
                            for n in range(N4):
                                mm = pe.matmul(ps[:, k, n, :], m[k][:, lev, 1, n, :], x[k][:, 0, n, :], start=True, stop=True)
                            mm.then_inc(y_done, 1)
                        for k in range(2):
                            pe.wait_ge(y_ready, 2 * (lev - 1) + k + 1)
                            if lev < 5:
                                for n in range(N4):
                                    pe.matmul(ps[:, 2 + k, n, :], x[k][:, 1, n, :], y[k][:, n, :], start=True, stop=True)
                            for n in range(N4):
                                mm = pe.matmul(ps[:, 4 + k, n, :], y[k][:, n, :], x[k][:, 1, n, :], start=True, stop=True)
                            mm.then_inc(z_done, 1)
                    for n in range(N4):
                        pe.matmul(ps[:, 6, n, 0:HD], tq[0][:, 0, n, :], st[0][:, n, :], start=True, stop=False)
                        mm = pe.matmul(ps[:, 6, n, 0:HD], akt[:, n, :], val[0][:, n // 2, n % 2, :], start=False, stop=True)
                    mm.then_inc(rhs_done, 1)
                    for n in range(N4):
                        mm = pe.matmul(ps[:, 7, n, 0:HD], tq[1][:, 0, n, :], st[1][:, n, :], start=True, stop=True)
                    mm.then_inc(rhs_done, 1)
                    for k in range(2):
                        pe.wait_ge((rhs_ready0, rhs_ready1)[k], 1)
                        pe.wait_ge(x_ready, 11 + k)
                        for n in range(N4):
                            mm = pe.matmul(ps[:, k, n, 0:HD], x[k][:, 1, n, :], rhs[k][:, n, :], start=True, stop=True)
                        mm.then_inc(n_done, 1)
                    for k in range(2):
                        pe.wait_ge(n_ready, k + 1)
                        for n in range(N4):
                            d, a = prob(n)
                            if k == 0:
                                pe.matmul(ps[:, 4, n, 0:HD], bd[0][:, d, 2, a, :], val[0][:, d, a, :], start=True, stop=False)
                                mm = pe.matmul(ps[:, 4, n, 0:HD], bd[0][:, d, 1, a, :], nn[0][:, n, :], start=False, stop=True)
                            else:
                                mm = pe.matmul(ps[:, 5, n, 0:HD], bd[1][:, d, 5, a, :], nn[1][:, n, :], start=True, stop=True)
                        mm.then_inc(ds_done, 1)
                        for n in range(N4):
                            d, a = prob(n)
                            if k == 0:
                                pe.matmul(ps[:, 2, n, 0:HD], tq[0][:, 3, n, :], st[0][:, n, :], start=True, stop=False)
                                pe.matmul(ps[:, 2, n, 0:HD], rk[:, n, :], val[0][:, d, a, :], start=False, stop=False)
                                mm = pe.matmul(ps[:, 2, n, 0:HD], rb[:, n, :], nn[0][:, n, :], start=False, stop=True)
                            else:
                                pe.matmul(ps[:, 3, n, 0:HD], tq[1][:, 4, n, :], st[1][:, n, :], start=True, stop=False)
                                mm = pe.matmul(ps[:, 3, n, 0:HD], qk[:, n, :], nn[1][:, n, :], start=False, stop=True)
                        mm.then_inc(o_done, 1)

                @block.scalar
                def _(act):
                    act.wait_ge(du_ready, 2)
                    for w, sign in ((0, -1.0), (1, 1.0)):
                        act.activation(dd[:, w], du[:, w], ACT.Exp, scale=sign).then_inc(dd_ready, 1)
                    act.activation(dec[1][:], col[:, 1].rearrange("p d a -> p (d a)"), ACT.Exp).then_inc(gdec_ready, 1)
                    g = 0
                    for k in range(2):
                        for q in range(NT[k]):
                            act.wait_ge(tr_done, g + 1)
                            act.activation(tq[k][:, q], ps[:, g % 4], ACT.Copy).then_inc(tr_copied, 1)
                            g += 1
                    for lev in range(1, 6):
                        for k in range(2):
                            act.wait_ge(y_done, 2 * (lev - 1) + k + 1)
                            act.activation(y[k][:], ps[:, k], ACT.Copy).then_inc(y_ready, 1)
                    act.wait_ge(rhs_done, 1)
                    act.activation(rhs[0][:], ps[:, 6, :, 0:HD], ACT.Copy).then_inc(rhs_ready0, 1)
                    for k in range(2):
                        act.wait_ge(n_done, k + 1)
                        act.activation(nn[k][:], ps[:, k, :, 0:HD], ACT.Copy, scale=-1.0 if k == 0 else 1.0).then_inc(n_ready, 1)
                    for k in range(2):
                        act.wait_ge(o_done, k + 1)
                        act.activation(oo[k][:], ps[:, 2 + k, :, 0:HD], ACT.Copy).then_inc(o_ready, 1)

                @block.vector
                def _(v):
                    link = chained(v, dve_step)
                    v.wait_ge(col_in, 32)
                    for n in range(N4):
                        d, a = prob(n)
                        ins = v.tensor_scalar(diag[:, n, :], consts["ident"][:], col[:, 0, d, a:a + 1], None, ALU.mult)
                    ins.then_inc(diag_ready, 1)
                    v.wait_ge(diffs_done, 1)
                    for w, op in ((0, ALU.max), (1, ALU.min)):
                        for n in range(N4):
                            d, a = prob(n)
                            ins = v.tensor_scalar(du[:, w, n, :], ps[:, 7, n, :], col[:, 0, d, a:a + 1], 0.0, ALU.subtract, op)
                        ins.then_inc(du_ready, 1)
                    evac = [(am[0][:, 0], None), (am[0][:, 1], None), (am[1][:, 0], dd[:, 0]), (am[1][:, 1], dd[:, 1]),
                            (akt[:], masks[:, 0]), (rk[:], masks[:, 1]), (rb[:], masks[:, 1]), (qk[:], dd[:, 1])]
                    for g, (dst, by) in enumerate(evac):
                        v.wait_ge(gram_done, g + 1)
                        if g == 2:
                            v.wait_ge(dd_ready, 2)
                        if by is None:
                            v.tensor_copy(dst, ps[:, 4 + g % 3]).then_inc(gram_ready, 1)
                        elif g == 7:
                            link(v.tensor_tensor(dst, ps[:, 4 + g % 3], by, ALU.mult))
                            v.tensor_tensor(dst, dst, masks[:, 1], ALU.mult).then_inc(gram_ready, 1)
                        else:
                            v.tensor_tensor(dst, ps[:, 4 + g % 3], by, ALU.mult).then_inc(gram_ready, 1)
                    eye = consts["ident"][:].unsqueeze(1).to_broadcast([P, N4, P])
                    for k in range(2):
                        v.wait_ge(m_ready, 2 * k + 2)
                        v.tensor_tensor(x[k][:, 0], eye, m[k][:, 0, 0], ALU.subtract)
                        v.tensor_tensor(x[k][:, 1], eye, m[k][:, 0, 1], ALU.subtract).then_inc(x_ready, 1)
                    for lev in range(1, 6):
                        for k in range(2):
                            v.wait_ge(z_done, 2 * (lev - 1) + k + 1)
                            v.wait_ge(x_ready, 2 * (lev - 1) + k + 1)
                            if lev < 5:
                                v.tensor_tensor(x[k][:, 0], x[k][:, 0], ps[:, 2 + k], ALU.subtract)
                            v.tensor_tensor(x[k][:, 1], x[k][:, 1], ps[:, 4 + k], ALU.subtract).then_inc(x_ready, 1)
                    v.wait_ge(rhs_done, 2)
                    v.tensor_tensor(rhs[1][:], val[1][:].rearrange("p d a e -> p (d a) e"), ps[:, 7, :, 0:HD], ALU.subtract).then_inc(rhs_ready1, 1)
                    v.wait_ge(dec_in, 32)
                    v.wait_ge(ds_done, 1)
                    v.wait_ge(o_done, 1)
                    link(v.tensor_tensor(st[0][:], st[0][:], ps[:, 4, :, 0:HD], ALU.add))
                    link(v.tensor_tensor(st[0][:], st[0][:], head_bc(dec[0][:]), ALU.mult))
                    v.wait_ge(gdec_ready, 1)
                    v.wait_ge(ds_done, 2)
                    v.wait_ge(o_done, 2)
                    link(v.tensor_tensor(st[1][:], st[1][:], head_bc(dec[1][:]), ALU.mult))
                    link(v.tensor_tensor(st[1][:], st[1][:], ps[:, 5, :, 0:HD], ALU.add))


def scan_post_stage(nc, l, t, s, consts):
    with ExitStack() as es:
        sb = lambda n, sh: es.enter_context(nc.sbuf_tensor("po_" + n, sh, F32))
        lg, lb, gg = sb("lg", [P, GW]), sb("lb", [P, GW]), sb("gg", [P, HD])
        load_once(nc, [(lg[:], over_rows(t["rwkv_ln_g"][l])), (lb[:], over_rows(t["rwkv_ln_b"][l])), (gg[:], over_rows(t["gdn_norm_g"][l]))])
        y = sb("y", [P, 2, 2, GW])
        sq = sb("sq", [P, 2, GW])
        rp, gp = sb("rp", [P, 2, GW]), sb("gp", [P, GW])
        r = sb("r", [P, 6, 2 * HEADS])
        with nc.Fori(0, TILES) as i:
            with stage(nc, "y_in", "post_in", "var_ready", "root_ready", "dve_step", "out_ready", "stored") as \
                    (block, y_in, post_in, var_ready, root_ready, dve_step, out_ready, stored):
                @block.sync
                def _(sp):
                    for k in range(2):
                        for d in range(2):
                            src = s["scan"][k, d].rearrange("c t g -> (c t) g")[bass.ds(i * P + (0 if d == 0 else 8 * C), P), :]
                            sp.dma_start(y[:, k, d], src).then_inc(y_in, 16)
                    sp.dma_start(rp[:], s["rwpost"][i]).then_inc(post_in, 16)
                    sp.dma_start(gp[:], s["gdpost"][i]).then_inc(post_in, 16)
                    sp.wait_ge(out_ready, 1)
                    sp.dma_start(s["y"][bass.ds(i * P, P), GW:3 * GW].rearrange("p (k g) -> p k g", k=2), y[:, :, 0]).then_inc(stored, 16)
                    sp.wait_ge(stored, 16)

                @block.scalar
                def _(act):
                    act.wait_ge(var_ready, 1)
                    act.activation(r[:, 3, :], r[:, 2, :], ACT.Sqrt).then_inc(root_ready, 1)

                @block.vector
                def _(v):
                    link = chained(v, dve_step)
                    yb, yc = y[:, 0, 0], y[:, 1, 0]
                    v.wait_ge(y_in, 64)
                    link(v.tensor_tensor(y[:, :, 0], y[:, :, 0], y[:, :, 1], ALU.add))
                    link(v.tensor_reduce(r[:, 0, 0:HEADS], by_head(yb), X, ALU.add))
                    link(v.tensor_scalar(r[:, 0, 0:HEADS], r[:, 0, 0:HEADS], 1.0 / HD, None, ALU.mult))
                    link(v.tensor_tensor(by_head(yb), by_head(yb), head_bc(r[:, 0, 0:HEADS]), ALU.subtract))
                    link(v.tensor_tensor(sq[:], y[:, :, 0], y[:, :, 0], ALU.mult))
                    link(v.tensor_reduce(r[:, 1, :], sq[:].rearrange("p k (h e) -> p (k h) e", e=HD), X, ALU.add))
                    link(v.tensor_scalar(r[:, 2, 0:HEADS], r[:, 1, 0:HEADS], 1.0 / HD, GN_EPS, ALU.mult, ALU.add))
                    v.tensor_scalar(r[:, 2, HEADS:], r[:, 1, HEADS:], 1.0 / HD, NORM_EPS, ALU.mult, ALU.add).then_inc(var_ready, 1)
                    v.wait_ge(root_ready, 1)
                    link(v.reciprocal(r[:, 4, :], r[:, 3, :]))
                    link(v.tensor_tensor(y[:, :, 0].rearrange("p k (h e) -> p k h e", e=HD), y[:, :, 0].rearrange("p k (h e) -> p k h e", e=HD),
                                         r[:, 4, :].rearrange("p (k h) -> p k h", k=2).unsqueeze(3).to_broadcast([P, 2, HEADS, HD]), ALU.mult))
                    v.wait_ge(post_in, 32)
                    link(v.tensor_tensor(yb, yb, lg[:], ALU.mult))
                    link(v.tensor_tensor(yb, yb, lb[:], ALU.add))
                    link(v.tensor_tensor(yb, yb, rp[:, 0], ALU.add))
                    link(v.tensor_tensor(yb, yb, rp[:, 1], ALU.mult))
                    link(v.tensor_tensor(by_head(yc), by_head(yc), gg[:].unsqueeze(1).to_broadcast([P, HEADS, HD]), ALU.mult))
                    v.tensor_tensor(yc, yc, gp[:], ALU.mult).then_inc(out_ready, 1)


def post_norm(v, link, z, y, h, gate, g, b, stats, mv, var_ready, std_ready):
    link(v.tensor_tensor(z[:], y, gate, ALU.mult))
    link(v.scalar_tensor_tensor(z[:], h[:], ALPHA, z[:], ALU.mult, ALU.add))
    ln_first(v, link, z, stats, mv, var_ready)
    ln_last(v, link, z[:], z[:], mv, std_ready, 1)
    link(v.tensor_tensor(z[:], z[:], g[:], ALU.mult))
    return v.tensor_tensor(z[:], z[:], b[:], ALU.add)


def mix_stage(nc, l, t, s, consts):
    with ExitStack() as es:
        sb = lambda n, sh: es.enter_context(nc.sbuf_tensor("mx_" + n, sh, F32))
        w, g, b = sb("w", [P, KT, D]), sb("g", [P, D]), sb("b", [P, D])
        load_once(nc, [(w[:], t["w_out"][l].rearrange("(k p) n -> p k n", p=P)), (g[:], over_rows(t["ln_mix_g"][l])), (b[:], over_rows(t["ln_mix_b"][l]))])
        y, yT, h, gate, z = sb("y", [P, D]), sb("yT", [P, KT, P]), sb("h", [P, D]), sb("gate", [P, D]), sb("z", [P, D])
        stats, mv = sb("stats", [P, 2, 6]), sb("mv", [P, 8])
        ps = es.enter_context(nc.psum_tensor("mx_ps", [P, 4, 512], F32))
        with nc.Fori(0, TILES) as i:
            with stage(nc, "y_in", "h_in", "gate_in", "tr_done", "copied", "mm_done", "var_ready", "std_ready", "dve_step", "z_ready", "stored") as \
                    (block, y_in, h_in, gate_in, tr_done, copied, mm_done, var_ready, std_ready, dve_step, z_ready, stored):
                @block.sync
                def _(sp):
                    sp.dma_start(y[:], s["y"][bass.ds(i * P, P), :]).then_inc(y_in, 16)
                    sp.dma_start(h[:], s["h"][i]).then_inc(h_in, 16)
                    sp.dma_start(gate[:], over_rows(s["mods"][i, 2 * D:3 * D])).then_inc(gate_in, 16)
                    sp.wait_ge(z_ready, 1)
                    sp.dma_start(s["h"][i], z[:]).then_inc(stored, 16)
                    sp.wait_ge(stored, 16)

                @block.tensor
                def _(pe):
                    pe.wait_ge(y_in, 16)
                    for half in range(2):
                        for k in range(4):
                            kk = 4 * half + k
                            tr = pe.transpose(ps[:, half, k * P:(k + 1) * P], y[:, kk * P:(kk + 1) * P], consts["ident"][:])
                        tr.then_inc(tr_done, 1)
                    pe.wait_ge(copied, 2)
                    for half in range(2):
                        for k in range(KT):
                            mm = pe.matmul(ps[:, 2 + half, :], yT[:, k, :], w[:, k, half * 512:(half + 1) * 512], start=(k == 0), stop=(k == KT - 1))
                        mm.then_inc(mm_done, 1)

                @block.scalar
                def _(act):
                    for half in range(2):
                        act.wait_ge(tr_done, half + 1)
                        act.activation(yT[:, 4 * half:4 * half + 4, :].rearrange("p k n -> p (k n)"), ps[:, half], ACT.Copy).then_inc(copied, 1)
                    act.wait_ge(var_ready, 1)
                    act.activation(mv[:, 3:4], mv[:, 2:3], ACT.Sqrt).then_inc(std_ready, 1)

                @block.vector
                def _(v):
                    link = chained(v, dve_step)
                    v.wait_ge(h_in, 16)
                    v.wait_ge(gate_in, 16)
                    v.wait_ge(mm_done, 2)
                    post_norm(v, link, z, ps[:, 2:4].rearrange("p a b -> p (a b)"), h, gate[:], g, b, stats, mv, var_ready, std_ready).then_inc(z_ready, 1)


GROUP = 16
RING = 8


def peer_stages(nc, l, t, s, consts):
    with ExitStack() as es:
        sb = lambda n, sh, dt=F32: es.enter_context(nc.sbuf_tensor("pe_" + n, sh, dt))
        keys, g, b = sb("keys", [P, PH * 2 * PK]), sb("g", [P, D]), sb("b", [P, D])
        wq = sb("wq", [P, KT, PH * 2 * P])
        iota = sb("iota", [P, TOPK])
        load_once(nc, [(keys[:], t["keys"][l]), (g[:], over_rows(t["ln_ffn_g"][l])), (b[:], over_rows(t["ln_ffn_b"][l])),
                       (wq[:], t["peer_wq"][l].rearrange("(k p) n -> p k n", p=P)), (iota[:], t["k_iota"])])
        tb, y = sb("tb", [P, D]), sb("y", [P, D])
        slot, act_raw, gates, wts = sb("slot", [P, SLOTS], U32), sb("act", [P, SLOTS]), sb("gates", [P, SLOTS]), sb("wts", [P, SLOTS])
        with nc.Fori(l * CTX_TILES, TILES) as i:
            route_stage(nc, l, i, t, s, consts, keys, wq, iota, tb, slot, gates)
            with ExitStack() as inner:
                buf = {"ring": inner.enter_context(nc.sbuf_tensor("pe_ring", [P, RING, D], F32)),
                       "idx": inner.enter_context(nc.sbuf_tensor("pe_idx", [P, GROUP], U32)),
                       "w": inner.enter_context(nc.sbuf_tensor("pe_w", [P, GROUP], F32)),
                       "junk": inner.enter_context(nc.sbuf_tensor("pe_junk", [P, D], F32))}
                with nc.Fori(0, SLOTS // GROUP) as j:
                    gather_stage(nc, t["peer_u"], j, buf, slot, act_raw, tb, None)
                with stage(nc, "gelu_done", "w_ready", "y_zero") as (block, gelu_done, w_ready, y_zero):
                    @block.scalar
                    def _(act):
                        act.activation(wts[:], act_raw[:], ACT.Gelu).then_inc(gelu_done, 1)

                    @block.gpsimd
                    def _(pool):
                        pool.memset(y[:], 0.0).then_inc(y_zero, 1)

                    @block.vector
                    def _(v):
                        v.wait_ge(gelu_done, 1)
                        v.tensor_tensor(wts[:], wts[:], gates[:], ALU.mult).then_inc(w_ready, 1)
                with nc.Fori(0, SLOTS // GROUP) as j:
                    gather_stage(nc, t["peer_v"], j, buf, slot, wts, tb, y)
            ffn_norm_stage(nc, i, s, y, g, b)


def gather_stage(nc, table, j, buf, slot, col, tb, y):
    ring, idx, w, junk = buf["ring"], buf["idx"], buf["w"], buf["junk"]
    with stage(nc, "idx_ready", "dve_step", "row_used", *[f"row_in{k}" for k in range(RING)], pool_dmas=True) as (block, idx_ready, dve_step, row_used, *row_in):
        @block.gpsimd
        def _(pool):
            pool.wait_ge(idx_ready, 1)
            for k in range(GROUP):
                if k >= RING:
                    pool.wait_ge(row_used, k - RING + 1)
                pool.indirect_dma_start(ring[:, k % RING, :], None, table, bass.IndirectOffsetOnAxis(ap=idx[:, k:k + 1], axis=0)).then_inc(row_in[k % RING], 16)

        @block.vector
        def _(v):
            link = chained(v, dve_step)
            cols = bass.ds(j * GROUP, GROUP)
            v.tensor_copy(idx[:], slot[:, cols]).then_inc(idx_ready, 1)
            if y is not None:
                link(v.tensor_copy(w[:], col[:, cols]))
            for k in range(GROUP):
                v.wait_ge(row_in[k % RING], 16 * (k // RING + 1))
                row = ring[:, k % RING, :]
                if y is None:
                    v.scalar_tensor_tensor(junk[:], row, 1.0, tb[:], ALU.mult, ALU.mult, accum_out=w[:, k:k + 1]).then_inc(row_used, 1)
                    v.wait_ge(row_used, k + 1)
                else:
                    v.scalar_tensor_tensor(y[:], row, w[:, k:k + 1], y[:], ALU.mult, ALU.add).then_inc(row_used, 1)
                    v.wait_ge(row_used, k + 1)
            if y is None:
                v.tensor_copy(col[:, cols], w[:])


def route_stage(nc, l, i, t, s, consts, keys, wq, iota, tb, slot, gates):
    NS = 2 * PH
    with ExitStack() as es:
        sb = lambda n, sh, dt=F32: es.enter_context(nc.sbuf_tensor("ro_" + n, sh, dt))
        m, tbT, qT, sc, sc2 = sb("m", [P, 2, D]), sb("tbT", [P, KT, P]), sb("qT", [P, NS, P]), sb("sc", [P, NS, PK]), sb("sc2", [P, 2, TOPK * TOPK])
        stats, mv = sb("stats", [P, 2, 6]), sb("mv", [P, 8])
        top, topi, topf = sb("top", [P, NS, TOPK]), sb("topi", [P, NS, TOPK], U32), sb("topf", [P, NS, TOPK])
        cand = sb("cand", [P, PH, TOPK, TOPK])
        best, pos = sb("best", [P, PH, TOPK]), sb("pos", [P, PH, TOPK], U32)
        hi, lo, hif, lof = sb("hi", [P, PH, TOPK], U32), sb("lo", [P, PH, TOPK], U32), sb("hif", [P, PH, TOPK]), sb("lof", [P, PH, TOPK])
        eq = sb("eq", [P, SLOTS, TOPK])
        i0, i1, r8 = sb("i0", [P, PH, TOPK]), sb("i1", [P, PH, TOPK]), sb("r8", [P, 2, PH])
        ps = es.enter_context(nc.psum_tensor("ro_ps", [P, 8, 512], F32))
        with stage(nc, "h_in", "m_in", "var_ready", "std_ready", "tb_ready", "tr_done", "tbT_ready", "q_done", "q_ready", "s_done", "s_ready",
                   "gap_ready", "exp_ready", "dve_step") as \
                (block, h_in, m_in, var_ready, std_ready, tb_ready, tr_done, tbT_ready, q_done, q_ready, s_done, s_ready,
                 gap_ready, exp_ready, dve_step):
            @block.sync
            def _(sp):
                sp.dma_start(tb[:], s["h"][i]).then_inc(h_in, 16)
                sp.dma_start(m[:], over_rows(s["mods"][i, 3 * D:5 * D]).rearrange("p (a n) -> p a n", a=2)).then_inc(m_in, 16)

            @block.tensor
            def _(pe):
                pe.wait_ge(tb_ready, 1)
                for half in range(2):
                    for k in range(4):
                        kk = 4 * half + k
                        tr = pe.transpose(ps[:, half, k * P:(k + 1) * P], tb[:, kk * P:(kk + 1) * P], consts["ident"][:])
                    tr.then_inc(tr_done, 1)
                pe.wait_ge(tbT_ready, 2)
                for q in range(NS // 4):
                    if q >= 2:
                        pe.wait_ge(q_ready, q - 1)
                    for n in range(4):
                        hp = 4 * q + n
                        for k in range(KT):
                            mm = pe.matmul(ps[:, 2 + q % 2, n * P:(n + 1) * P], wq[:, k, hp * P:(hp + 1) * P], tbT[:, k, :], start=(k == 0), stop=(k == KT - 1))
                    mm.then_inc(q_done, 1)
                for q in range(NS // 4):
                    pe.wait_ge(q_ready, q + 1)
                    for n in range(4):
                        hp = 4 * q + n
                        mm = pe.matmul(ps[:, 4 + q, n * P:(n + 1) * P], qT[:, hp, :], keys[:, hp * PK:(hp + 1) * PK], start=True, stop=True)
                    mm.then_inc(s_done, 1)

            @block.scalar
            def _(act):
                act.wait_ge(var_ready, 1)
                act.activation(mv[:, 3:4], mv[:, 2:3], ACT.Sqrt).then_inc(std_ready, 1)
                for half in range(2):
                    act.wait_ge(tr_done, half + 1)
                    act.activation(tbT[:, 4 * half:4 * half + 4, :].rearrange("p k n -> p (k n)"), ps[:, half], ACT.Copy).then_inc(tbT_ready, 1)
                for q in range(NS // 4):
                    act.wait_ge(q_done, q + 1)
                    act.activation(qT[:, 4 * q:4 * q + 4, :].rearrange("p k n -> p (k n)"), ps[:, 2 + q % 2], ACT.Copy).then_inc(q_ready, 1)
                for q in range(NS // 4):
                    act.wait_ge(s_done, q + 1)
                    act.activation(sc[:, 4 * q:4 * q + 4, :].rearrange("p k n -> p (k n)"), ps[:, 4 + q], ACT.Copy).then_inc(s_ready, 1)
                act.wait_ge(gap_ready, 1)
                act.activation(hif[:], best[:], ACT.Exp).then_inc(exp_ready, 1)

            @block.vector
            def _(v):
                link = chained(v, dve_step)
                v.wait_ge(h_in, 16)
                ln_first(v, link, tb, stats, mv, var_ready)
                ln_last(v, link, tb[:], tb[:], mv, std_ready, 1)
                v.wait_ge(m_in, 16)
                link(v.tensor_tensor(tb[:], tb[:], m[:, 1, :], ALU.mult))
                v.tensor_tensor(tb[:], tb[:], m[:, 0, :], ALU.add).then_inc(tb_ready, 1)

                def top16(src, spare, vals, inds):
                    link(v.max(vals[:, 0:8], src))
                    link(v.max_index(inds[:, 0:8], vals[:, 0:8], src))
                    link(v.match_replace(out=spare, in_to_replace=vals[:, 0:8], in_values=src, imm_value=-3e38))
                    link(v.max(vals[:, 8:16], spare))
                    link(v.max_index(inds[:, 8:16], vals[:, 8:16], spare))

                for hp in range(NS):
                    v.wait_ge(s_ready, hp // 4 + 1)
                    top16(sc[:, hp, :], sc2[:, hp % 2, 0:PK], top[:, hp, :], topi[:, hp, :])
                halves = lambda x: x[:].rearrange("p (h two) k -> p h two k", two=2)
                link(v.tensor_tensor(cand[:], halves(top)[:, :, 0].unsqueeze(3).to_broadcast([P, PH, TOPK, TOPK]),
                                     halves(top)[:, :, 1].unsqueeze(2).to_broadcast([P, PH, TOPK, TOPK]), ALU.add))
                for h in range(PH):
                    top16(cand[:, h].rearrange("p a b -> p (a b)"), sc2[:, h % 2, :], best[:, h, :], pos[:, h, :])
                link(v.tensor_scalar(hi[:], pos[:], 4, None, ALU.logical_shift_right))
                link(v.tensor_scalar(lo[:], pos[:], 15, None, ALU.bitwise_and))
                link(v.tensor_copy(hif[:], hi[:]))
                link(v.tensor_copy(lof[:], lo[:]))
                link(v.tensor_copy(topf[:], topi[:]))
                for out, at, half in ((i0, hif, 0), (i1, lof, 1)):
                    a = at[:].rearrange("p h k -> p (h k)").unsqueeze(2).to_broadcast([P, SLOTS, TOPK])
                    link(v.tensor_tensor(eq[:], a, iota[:].unsqueeze(1).to_broadcast([P, SLOTS, TOPK]), ALU.is_equal))
                    e4 = eq[:].rearrange("p (h k) n -> p h k n", h=PH)
                    link(v.tensor_tensor(e4, e4, halves(topf)[:, :, half].unsqueeze(2).to_broadcast([P, PH, TOPK, TOPK]), ALU.mult))
                    link(v.tensor_reduce(out[:].rearrange("p h k -> p (h k)"), eq[:], X, ALU.add))
                link(v.scalar_tensor_tensor(i0[:], i0[:], float(PK), i1[:], ALU.mult, ALU.add))
                link(v.tensor_scalar(i0[:], i0[:], consts["layer"][:, 2:3], None, ALU.add))
                link(v.tensor_copy(slot[:], i0[:].rearrange("p h k -> p (h k)")))
                link(v.tensor_copy(r8[:, 0, :], best[:, :, 0]))
                v.tensor_tensor(best[:], best[:], r8[:, 0, :].unsqueeze(2).to_broadcast([P, PH, TOPK]), ALU.subtract).then_inc(gap_ready, 1)
                v.wait_ge(exp_ready, 1)
                link(v.tensor_reduce(r8[:, 0, :], hif[:], X, ALU.add))
                link(v.reciprocal(r8[:, 1, :], r8[:, 0, :]))
                link(v.tensor_tensor(gates[:].rearrange("p (h k) -> p h k", h=PH), hif[:], r8[:, 1, :].unsqueeze(2).to_broadcast([P, PH, TOPK]), ALU.mult))


def ffn_norm_stage(nc, i, s, y, g, b):
    with ExitStack() as es:
        sb = lambda n, sh: es.enter_context(nc.sbuf_tensor("fn_" + n, sh, F32))
        h, gate, z, stats, mv = sb("h", [P, D]), sb("gate", [P, D]), sb("z", [P, D]), sb("stats", [P, 2, 6]), sb("mv", [P, 8])
        with stage(nc, "h_in", "gate_in", "var_ready", "std_ready", "dve_step", "z_ready", "stored") as \
                (block, h_in, gate_in, var_ready, std_ready, dve_step, z_ready, stored):
            @block.sync
            def _(sp):
                sp.dma_start(h[:], s["h"][i]).then_inc(h_in, 16)
                sp.dma_start(gate[:], over_rows(s["mods"][i, 5 * D:6 * D])).then_inc(gate_in, 16)
                sp.wait_ge(z_ready, 1)
                sp.dma_start(s["h"][i], z[:]).then_inc(stored, 16)
                sp.wait_ge(stored, 16)

            @block.scalar
            def _(act):
                act.wait_ge(var_ready, 1)
                act.activation(mv[:, 3:4], mv[:, 2:3], ACT.Sqrt).then_inc(std_ready, 1)

            @block.vector
            def _(v):
                link = chained(v, dve_step)
                v.wait_ge(h_in, 16)
                v.wait_ge(gate_in, 16)
                post_norm(v, link, z, y[:], h, gate[:], g, b, stats, mv, var_ready, std_ready).then_inc(z_ready, 1)


def load_once(nc, pairs):
    with stage(nc, "once_in") as (block, once_in):
        @block.sync
        def _(sp):
            for dst, src in pairs:
                sp.dma_start(dst, src).then_inc(once_in, 16)
            sp.wait_ge(once_in, 16 * len(pairs))


def build(nc, t, out, upto=99):
    with ExitStack() as es:
        dram = lambda n, s: nc.dram_tensor(n, s, F32, kind="Internal").ap()
        s = {
            "h": dram("h_dram", (TILES, P, D)),
            "mods": dram("mods_dram", (TILES, 6 * D)),
            "p": dram("p_dram", (TOK + 2, IN_COLS)),
            "y": dram("y_dram", (TOK, D)),
            "rw": dram("rw_dram", (2 * TILES, 2, 2, 5, 2, 2, C, HD)),
            "rwdec": dram("rwdec_dram", (2 * TILES * 2, 2, GW)),
            "rwpost": dram("rwpost_dram", (TILES, P, 2, GW)),
            "gd": dram("gd_dram", (2 * TILES, 2, 2, 7, 2, 2, C, HD)),
            "gdcol": dram("gdcol_dram", (2 * TILES * 2, 2, C, 2 * HEADS)),
            "gdpost": dram("gdpost_dram", (TILES, P, GW)),
            "scan": dram("scan_dram", (2, 2, 24, C, GW)),
        }
        consts = {}
        for name, key in (("ident", "k_ident"), ("sums", "k_sums"), ("rows", "k_rows")):
            ap = t[key]
            consts[name] = es.enter_context(nc.sbuf_tensor("c_" + name, list(ap.shape), F32))
        layer = es.enter_context(nc.sbuf_tensor("c_layer", [P, 4], F32))
        consts["layer"] = layer
        load_once(nc, [(consts["ident"][:], t["k_ident"]), (consts["sums"][:], t["k_sums"]), (consts["rows"][:], t["k_rows"]),
                       (s["h"][0:CTX_TILES].rearrange("i p n -> (i p) n"), t["ctx"]),
                       (s["h"][CTX_TILES:TILES].rearrange("i p n -> (i p) n"), t["x"]),
                       (s["p"][0:1, :], t["k_zero"][0:1, :]), (s["p"][TOK + 1:TOK + 2, :], t["k_zero"][1:2, :])])
        with nc.Fori(0, DEPTH) as l:
            load_once(nc, [(layer[:], t["k_layer"][l])])
            ada_stage(nc, l, t, s["mods"], consts)
            with nc.sbuf_tensor("uT", [P, KT, TOK], F32) as uT:
                norm_stage(nc, l, t, s["h"], s["mods"], consts, uT)
                project_stage(nc, l, t, s["p"], uT)
            if upto >= 2:
                attention_stages(nc, l, t, s, consts)
            if upto >= 3:
                scan_stages(nc, l, t, s, consts)
            if upto >= 5:
                mix_stage(nc, l, t, s, consts)
            if upto >= 6:
                peer_stages(nc, l, t, s, consts)
        load_once(nc, [(out, s["h"][CTX_TILES:TILES].rearrange("i p n -> (i p) n"))])


def laid_out(inputs):
    a = {k: np.asarray(v) for k, v in inputs.items()}
    r = {n: a[n] for n in ("w_ada", "b_ada", "w_in", "w_out", "ln_mix_g", "ln_mix_b", "ln_ffn_g", "ln_ffn_b", "diff_norm_g",
                           "rwkv_mu", "rwkv_kk", "rwkv_ka", "rwkv_ln_g", "rwkv_ln_b", "rwkv_g2", "gdn_conv", "gdn_norm_g",
                           "peer_wq")}
    r["x"] = a["x"].reshape(SEQ, D)
    r["ctx"] = a["ctx"].reshape(CTX, D)
    r["cond"] = np.ascontiguousarray(np.stack([a["c"][0], a["c_ctx"]]).reshape(2, KT, P).transpose(2, 1, 0))
    r["diff_lam"] = a["diff_lam"].reshape(DEPTH, -1)
    r["rwkv_w0"] = a["rwkv_w0"].reshape(DEPTH, -1)
    r["rwkv_a0"] = a["rwkv_a0"].reshape(DEPTH, -1)
    r["rwkv_w2"] = a["rwkv_w2"]
    r["rwkv_a2"] = a["rwkv_a2"]
    r["rwkv_rk"] = a["rwkv_rk"].reshape(DEPTH, -1)
    r["gdn_a_log"] = a["gdn_a_log"].reshape(DEPTH, -1)
    r["gdn_dt_bias"] = a["gdn_dt_bias"].reshape(DEPTH, -1)
    r["bias"] = window_bias(a["nat_rpb"])
    r["keys"] = np.ascontiguousarray(a["peer_keys"].transpose(0, 4, 1, 2, 3).reshape(DEPTH, P, PH * 2 * PK))
    r["peer_u"] = a["peer_u"].reshape(DEPTH * EXPERTS, D)
    r["peer_v"] = a["peer_v"].reshape(DEPTH * EXPERTS, D)
    r.update(constants())
    return {"in_" + k: np.ascontiguousarray(v) for k, v in r.items()}


def kernel(**inputs):
    import concourse.bacc as bacc
    from concourse.bass_utils import run_bass_kernel_spmd

    nc = bacc.Bacc("TRN2", target_bir_lowering=False, num_devices=1)
    arrays = laid_out(inputs)
    t = {}
    for name, a in arrays.items():
        t[name[3:]] = nc.dram_tensor(name, a.shape, mybir.dt.from_np(a.dtype), kind="ExternalInput").ap()
    out = nc.dram_tensor("out", (SEQ, D), F32, kind="ExternalOutput").ap()
    build(nc, t, out)
    r = run_bass_kernel_spmd(nc, [arrays], core_ids=[0])
    return r.results[0]["out"].reshape(1, SEQ, D)
```

```python
from contextlib import ExitStack, contextmanager

import numpy as np

import concourse.bass as bass
import concourse.mybir as mybir

F32 = mybir.dt.float32
U32 = mybir.dt.uint32
ALU = mybir.AluOpType
ACT = mybir.ActivationFunctionType
X = mybir.AxisListType.X
P = 128

D = 1024
SEQ = 512
CTX = 256
TOK = CTX + SEQ
TILES = TOK // P
CTX_TILES = CTX // P
DEPTH = 2
GRID_W = 64
HD = 64
HEADS = 4
GW = HEADS * HD
ATTN_COLS = 3 * GW
LORA = 64
RWKV_COLS = 3 * GW + 4 * LORA + 128
GDN_QKV = 3 * GW
GDN_COLS = 4 * GW + 4 * HEADS
IN_COLS = ATTN_COLS + RWKV_COLS + GDN_COLS + ATTN_COLS
COL_A = 0
COL_B = ATTN_COLS
COL_C = COL_B + RWKV_COLS
COL_D = COL_C + GDN_COLS
KT = D // P
WCHUNK = 466
NCHUNKS = IN_COLS // WCHUNK
WIN_H, WIN_W = 8, 16
C = 64
CHUNKS = TOK // C
CTX_CHUNKS = CTX // C
LEVELS = (1, 2, 4, 8, 16, 32)
PH, PK, TOPK = 8, 128, 16
EXPERTS = PK * PK
SLOTS = PH * TOPK
ALPHA = (2 * DEPTH) ** 0.25
LN_EPS = 1e-5
GN_EPS = 64e-5
NORM_EPS = 1e-6
NEG = -1e30
DECAY = -float(np.exp(-0.5))


def constants():
    c = {}
    i = np.arange(P)
    same = (i[:, None] // C) == (i[None, :] // C)
    low = i[:, None] >= i[None, :]
    c["k_sums"] = np.stack([same & low.T, same & low, same]).astype(np.float32).transpose(1, 0, 2)
    c["k_ident"] = np.eye(P, dtype=np.float32)
    both = lambda m: np.stack([m, m, m.T, m.T]).astype(np.float32)
    strict = same & (i[:, None] > i[None, :])
    incl = same & low
    masks = [both(strict.T), both(incl.T)]
    for s in LEVELS:
        off = ((i[:, None] // (2 * s)) == (i[None, :] // (2 * s))) & ((i[:, None] // s) > (i[None, :] // s))
        masks += [both(off), both(off.T)]
    c["k_masks"] = np.stack(masks).transpose(2, 0, 1, 3).astype(np.float32).copy()
    c["k_rows"] = np.stack([(i // 64 == 0), (i // 64 == 1)] + [(i // 32 == g) for g in range(4)]).T.astype(np.float32).copy()
    e = np.ones((TILES, P, 2), np.float32)
    e[0, 0, 0] = e[CTX_TILES, 0, 0] = 0
    e[CTX_TILES - 1, P - 1, 1] = e[TILES - 1, P - 1, 1] = 0
    c["k_edges"] = e
    t = np.arange(SEQ)
    inv = (10000.0 ** (-np.arange(8, dtype=np.float32) / 8)).astype(np.float32)
    rope = np.zeros((2, TOK, HD), np.float32)
    rope[0] = 1
    for part, pos in ((0, t // GRID_W), (1, t % GRID_W)):
        ang = pos.astype(np.float32)[:, None] * inv
        for half in (0, 1):
            o = 32 * half + 16 * part
            rope[0, CTX:, o:o + 8] = rope[0, CTX:, o + 8:o + 16] = np.cos(ang)
            rope[1, CTX:, o:o + 8] = -np.sin(ang)
            rope[1, CTX:, o + 8:o + 16] = np.sin(ang)
    rope = np.broadcast_to(rope.reshape(2, TILES, P, 1, HD), (2, TILES, P, 8, HD))
    c["k_rope"] = np.ascontiguousarray(rope.transpose(1, 2, 0, 3, 4))
    c["k_iota"] = np.broadcast_to(np.arange(TOPK, dtype=np.float32), (P, TOPK)).copy()
    c["k_zero"] = np.zeros((2, IN_COLS), np.float32)
    lam = [0.8 - 0.6 * float(np.exp(-0.3 * l)) for l in range(DEPTH)]
    c["k_layer"] = np.stack([np.broadcast_to(np.array([lam[l], 1.0 - lam[l], l * EXPERTS, 0.0], np.float32), (P, 4))
                             for l in range(DEPTH)]).copy()
    return c


def window_bias(rpb):
    q = np.arange(SEQ)
    r, cq = q // GRID_W, q % GRID_W
    start = np.clip(cq - WIN_W // 2, 0, GRID_W - WIN_W)
    ok = (cq[None, :] >= start[:, None]) & (cq[None, :] < start[:, None] + WIN_W)
    dr = r[None, :] - r[:, None] + WIN_H - 1
    dc = np.clip(cq[None, :] - cq[:, None], -(WIN_W - 1), WIN_W - 1) + WIN_W - 1
    laid = np.asarray(rpb)[:, :, dr, dc]
    laid = np.where(ok[None, None], laid, np.float32(NEG)).astype(np.float32)
    return np.ascontiguousarray(laid.reshape(DEPTH, HEADS, SEQ // P, P, SEQ).transpose(0, 2, 3, 1, 4))


@contextmanager
def stage(nc, *names, pool_dmas=False):
    with ExitStack() as es:
        sems = [es.enter_context(nc.semaphore(n)) for n in names]
        with nc.Block() as block:
            yield (block, *sems)
        with nc.Block() as clear:
            if pool_dmas:
                @clear.gpsimd
                def _(pool):
                    pool.dma_reset()
                    for s in sems:
                        pool.sem_clear(s)
            else:
                @clear.sync
                def _(sp):
                    for s in sems:
                        sp.sem_clear(s)


def chained(eng, sem):
    count = [0]

    def link(ins):
        count[0] += 1
        ins.then_inc(sem, 1)
        eng.wait_ge(sem, count[0])
        return ins

    return link


def over_rows(row, *shape):
    return row.unsqueeze(0).to_broadcast([P] + list(row.shape))


def ln_first(v, link, x, stats, mv, var_ready):
    for k in range(2):
        link(v.bn_stats(stats[:, k, :], x[:, k * 512:(k + 1) * 512]))
    link(v.bn_aggr(mv[:, 0:2], stats[:, :, :].rearrange("p a b -> p (a b)")))
    v.tensor_scalar(mv[:, 2:3], mv[:, 1:2], LN_EPS, None, ALU.add).then_inc(var_ready, 1)


def ln_last(v, link, out, x, mv, std_ready, n):
    v.wait_ge(std_ready, n)
    link(v.reciprocal(mv[:, 4:5], mv[:, 3:4]))
    link(v.tensor_scalar(out, x, mv[:, 0:1], mv[:, 4:5], ALU.subtract, ALU.mult))


def ada_stage(nc, l, t, mods, consts):
    n_chunks, bufs = 6 * D // 512, 4
    with ExitStack() as es:
        cc = es.enter_context(nc.sbuf_tensor("cond", [P, KT, 2], F32))
        sc = es.enter_context(nc.sbuf_tensor("cond_silu", [P, KT, 2], F32))
        w = es.enter_context(nc.sbuf_tensor("ada_w", [P, bufs, KT, 512], F32))
        b = es.enter_context(nc.sbuf_tensor("ada_b", [2, 6 * D], F32))
        row = es.enter_context(nc.sbuf_tensor("ada_rows", [2, 6 * D], F32))
        ps = es.enter_context(nc.psum_tensor("ada_ps", [2, 2, 512], F32))
        wait = es.enter_context(stage(nc, "cond_in", "bias_in", "silu_done", "chunk_done", "row_done", "rows_out",
                                      "dve_step", *[f"w_in{k}" for k in range(bufs)]))
        block, cond_in, bias_in, silu_done, chunk_done, row_done, rows_out, dve_step, *w_in = wait
        wv = t["w_ada"][l].rearrange("(k p) n -> p k n", p=P)

        @block.sync
        def _(sp):
            sp.dma_start(cc[:], t["cond"]).then_inc(cond_in, 16)
            sp.dma_start(b[:], t["b_ada"][l].unsqueeze(0).to_broadcast([2, 6 * D])).then_inc(bias_in, 16)
            for n in range(n_chunks):
                if n >= bufs:
                    sp.wait_ge(chunk_done, n - bufs + 1)
                sp.dma_start(w[:, n % bufs], wv[:, :, n * 512:(n + 1) * 512]).then_inc(w_in[n % bufs], 16)
            sp.wait_ge(row_done, n_chunks)
            for i in range(TILES + 1):
                r = 1 if i < CTX_TILES else 0
                sp.dma_start(mods[i:i + 1, :], row[r:r + 1, :]).then_inc(rows_out, 16)
            sp.wait_ge(rows_out, 16 * (TILES + 1))

        @block.scalar
        def _(act):
            act.wait_ge(cond_in, 16)
            act.activation(sc[:], cc[:], ACT.Silu).then_inc(silu_done, 1)

        @block.tensor
        def _(pe):
            pe.wait_ge(silu_done, 1)
            for n in range(n_chunks):
                pe.wait_ge(w_in[n % bufs], 16 * (n // bufs + 1))
                if n >= 2:
                    pe.wait_ge(row_done, n - 1)
                for k in range(KT):
                    mm = pe.matmul(ps[:, n % 2, :], sc[:, k, :], w[:, n % bufs, k, :], start=(k == 0), stop=(k == KT - 1))
                mm.then_inc(chunk_done, 1)

        @block.vector
        def _(v):
            v.wait_ge(bias_in, 16)
            for n in range(n_chunks):
                cols = slice(n * 512, (n + 1) * 512)
                v.wait_ge(chunk_done, n + 1)
                one = 1.0 if n // 2 in (1, 4) else 0.0
                v.scalar_tensor_tensor(row[:, cols], ps[:, n % 2, :], one, b[:, cols], ALU.add, ALU.add).then_inc(row_done, 1)


def norm_stage(nc, l, t, h_dram, mods, consts, uT):
    with ExitStack() as es:
        h = es.enter_context(nc.sbuf_tensor("n_h", [P, D], F32))
        m = es.enter_context(nc.sbuf_tensor("n_mod", [P, 2, D], F32))
        stats = es.enter_context(nc.sbuf_tensor("n_stats", [P, 2, 6], F32))
        mv = es.enter_context(nc.sbuf_tensor("n_mv", [P, 8], F32))
        ps = es.enter_context(nc.psum_tensor("n_ps", [P, 2, 4, P], F32))
        with nc.Fori(0, TILES) as i:
            with stage(nc, "h_in", "mod_in", "var_ready", "std_ready", "dve_step", "u_ready", "tr_done", "copied") as \
                    (block, h_in, mod_in, var_ready, std_ready, dve_step, u_ready, tr_done, copied):

                @block.sync
                def _(sp):
                    sp.dma_start(h[:], h_dram[i]).then_inc(h_in, 16)
                    sp.dma_start(m[:], over_rows(mods[i, 0:2 * D]).rearrange("p (a n) -> p a n", a=2)).then_inc(mod_in, 16)

                @block.vector
                def _(v):
                    link = chained(v, dve_step)
                    v.wait_ge(h_in, 16)
                    ln_first(v, link, h, stats, mv, var_ready)
                    ln_last(v, link, h[:], h[:], mv, std_ready, 1)
                    v.wait_ge(mod_in, 16)
                    link(v.tensor_tensor(h[:], h[:], m[:, 1, :], ALU.mult))
                    v.tensor_tensor(h[:], h[:], m[:, 0, :], ALU.add).then_inc(u_ready, 1)

                @block.scalar
                def _(act):
                    act.wait_ge(var_ready, 1)
                    act.activation(mv[:, 3:4], mv[:, 2:3], ACT.Sqrt).then_inc(std_ready, 1)
                    for half in range(2):
                        act.wait_ge(tr_done, half + 1)
                        act.activation(uT[:, 4 * half:4 * half + 4, bass.ds(i * P, P)], ps[:, half], ACT.Copy).then_inc(copied, 1)

                @block.tensor
                def _(pe):
                    pe.wait_ge(u_ready, 1)
                    for half in range(2):
                        for k in range(4):
                            kk = 4 * half + k
                            tr = pe.transpose(ps[:, half, k, :], h[:, kk * P:(kk + 1) * P], consts["ident"][:])
                        tr.then_inc(tr_done, 1)


def project_stage(nc, l, t, p_dram, uT):
    with ExitStack() as es:
        w = es.enter_context(nc.sbuf_tensor("p_w", [P, 2, KT, WCHUNK], F32))
        o = es.enter_context(nc.sbuf_tensor("p_out", [P, 4, WCHUNK], F32))
        ps = es.enter_context(nc.psum_tensor("p_ps", [P, 4, 512], F32))
        wv = t["w_in"][l].rearrange("(k p) n -> p k n", p=P)
        with stage(nc, "first_in") as (block, first_in):
            @block.sync
            def _(sp):
                sp.dma_start(w[:, 0], wv[:, :, 0:WCHUNK]).then_inc(first_in, 16)
                sp.wait_ge(first_in, 16)
        with nc.Fori(0, NCHUNKS // 2) as j:
            with stage(nc, "w0_in", "w1_in", "mm_done", "out_ready", "gone0", "gone1", "gone2", "gone3") as \
                    (block, w0_in, w1_in, mm_done, out_ready, *gone):

                @block.sync
                def _(sp):
                    sp.dma_start(w[:, 1], wv[:, :, bass.ds(j * 2 * WCHUNK + WCHUNK, WCHUNK)]).then_inc(w1_in, 16)
                    sp.wait_ge(mm_done, TILES)
                    nxt = sp.snap((j + 1) % (NCHUNKS // 2))
                    sp.dma_start(w[:, 0], wv[:, :, bass.ds(nxt * 2 * WCHUNK, WCHUNK)]).then_inc(w0_in, 16)
                    sp.wait_ge(w0_in, 16)

                @block.tensor
                def _(pe):
                    for q in range(2 * TILES):
                        ch, i = q // TILES, q % TILES
                        if q == TILES:
                            pe.wait_ge(w1_in, 16)
                        if q >= 4:
                            pe.wait_ge(out_ready, q - 3)
                        for k in range(KT):
                            mm = pe.matmul(ps[:, q % 4, 0:WCHUNK], uT[:, k, i * P:(i + 1) * P], w[:, ch, k, :],
                                           start=(k == 0), stop=(k == KT - 1))
                        mm.then_inc(mm_done, 1)

                @block.vector
                def _(v):
                    for q in range(2 * TILES):
                        v.wait_ge(mm_done, q + 1)
                        if q >= 4:
                            v.wait_ge(gone[q % 4], 16 * (q // 4))
                        v.tensor_copy(o[:, q % 4, :], ps[:, q % 4, 0:WCHUNK]).then_inc(out_ready, 1)

                @block.scalar
                def _(act):
                    for q in range(2 * TILES):
                        ch, i = q // TILES, q % TILES
                        act.wait_ge(out_ready, q + 1)
                        dst = p_dram[1 + i * P:1 + (i + 1) * P, bass.ds(j * 2 * WCHUNK + ch * WCHUNK, WCHUNK)]
                        act.dma_start(dst, o[:, q % 4, :]).then_inc(gone[q % 4], 16)
                    for g in gone:
                        act.wait_ge(g, 16 * 2 * TILES // 4)


def attention_stages(nc, l, t, s, consts):
    with ExitStack() as es:
        sb = lambda n, sh: es.enter_context(nc.sbuf_tensor(n, sh, F32))
        b = {"qA": sb("at_qA", [P, 2, TOK]), "kA": sb("at_kA", [P, 2, TOK]), "qD": sb("at_qD", [P, 2, TOK]),
             "kD": sb("at_kD", [P, 2, TOK]), "vA": sb("at_vA", [P, TILES, GW]), "vD": sb("at_vD", [P, TILES, GW]),
             "lam": sb("at_lam", [P, 8]), "g": sb("at_g", [P, HD])}
        v_src = lambda col: s["p"][1:1 + TOK, col + 2 * GW:col + 3 * GW].rearrange("(i p) n -> p i n", p=P)
        load_once(nc, [(b["vA"][:], v_src(COL_A)), (b["vD"][:], v_src(COL_D))])
        lambda_stage(nc, l, t, b, consts)
        qk_stage(nc, t, s, b, consts)
        attend_stage(nc, s, b, consts, "A", CTX_TILES, TILES, TILES, None)
        attend_stage(nc, s, b, consts, "A", 0, CTX_TILES, CTX_TILES, None)
        attend_stage(nc, s, b, consts, "D", CTX_TILES, TILES, TILES, t["bias"][l])
        attend_stage(nc, s, b, consts, "D", 0, CTX_TILES, CTX_TILES, None)


def lambda_stage(nc, l, t, b, consts):
    with ExitStack() as es:
        lv = es.enter_context(nc.sbuf_tensor("lv", [P, 4, 32], F32))
        pr = es.enter_context(nc.sbuf_tensor("lv_prod", [P, 2, 32], F32))
        lam = b["lam"]
        with stage(nc, "lv_in", "g_in", "dots_ready", "exps_ready", "dve_step") as (block, lv_in, g_in, dots_ready, exps_ready, dve_step):
            @block.sync
            def _(sp):
                sp.dma_start(lv[:].rearrange("p a b -> p (a b)"), over_rows(t["diff_lam"][l])).then_inc(lv_in, 16)
                sp.dma_start(b["g"][:], over_rows(t["diff_norm_g"][l])).then_inc(g_in, 16)

            @block.vector
            def _(v):
                link = chained(v, dve_step)
                v.wait_ge(lv_in, 16)
                for k in range(2):
                    link(v.tensor_tensor(pr[:, k, :], lv[:, 2 * k, :], lv[:, 2 * k + 1, :], ALU.mult))
                v.tensor_reduce(lam[:, 2:4], pr[:], X, ALU.add).then_inc(dots_ready, 1)
                v.wait_ge(exps_ready, 1)
                link(v.tensor_tensor(lam[:, 6:7], lam[:, 4:5], lam[:, 5:6], ALU.subtract))
                link(v.tensor_tensor(lam[:, 0:1], lam[:, 6:7], consts["layer"][:, 0:1], ALU.add))
                v.wait_ge(g_in, 16)
                link(v.tensor_scalar(b["g"][:], b["g"][:], consts["layer"][:, 1:2], None, ALU.mult))

            @block.scalar
            def _(act):
                act.wait_ge(dots_ready, 1)
                act.activation(lam[:, 4:6], lam[:, 2:4], ACT.Exp).then_inc(exps_ready, 1)


def qk_stage(nc, t, s, b, consts):
    with ExitStack() as es:
        sb = lambda n, sh: es.enter_context(nc.sbuf_tensor(n, sh, F32))
        a, d, tab, rot, t2 = sb("qk_a", [P, 512]), sb("qk_d", [P, 512]), sb("qk_tab", [P, 2, 512]), sb("qk_rot", [P, 512]), sb("qk_t2", [P, 512])
        ps = es.enter_context(nc.psum_tensor("qk_ps", [P, 2, 4, P], F32))
        pairs = lambda x: x.rearrange("p (g two e) -> p g two e", two=2, e=8)
        with nc.Fori(0, TILES) as i:
            with stage(nc, "a_in", "d_in", "tab_in", "dve_step", "rot_ready", "tr_done", "copied") as \
                    (block, a_in, d_in, tab_in, dve_step, rot_ready, tr_done, copied):
                @block.sync
                def _(sp):
                    rows = bass.ds(i * P + 1, P)
                    sp.dma_start(a[:], s["p"][rows, COL_A:COL_A + 512]).then_inc(a_in, 16)
                    sp.dma_start(tab[:], t["k_rope"][i].rearrange("p a h e -> p a (h e)")).then_inc(tab_in, 16)
                    sp.dma_start(d[:], s["p"][rows, COL_D:COL_D + 512]).then_inc(d_in, 16)

                @block.vector
                def _(v):
                    link = chained(v, dve_step)
                    v.wait_ge(a_in, 16)
                    v.wait_ge(tab_in, 16)
                    v.tensor_tensor(rot[:], a[:], tab[:, 0], ALU.mult)
                    for x in range(2):
                        mul = v.tensor_tensor(pairs(t2[:])[:, :, x], pairs(a[:])[:, :, 1 - x], pairs(tab[:, 1])[:, :, x], ALU.mult)
                    link(mul)
                    v.tensor_tensor(rot[:], rot[:], t2[:], ALU.add).then_inc(rot_ready, 1)

                @block.tensor
                def _(pe):
                    pe.wait_ge(d_in, 16)
                    for k in range(4):
                        tr = pe.transpose(ps[:, 1, k, :], d[:, k * P:(k + 1) * P], consts["ident"][:])
                    tr.then_inc(tr_done, 1)
                    pe.wait_ge(rot_ready, 1)
                    for k in range(4):
                        tr = pe.transpose(ps[:, 0, k, :], rot[:, k * P:(k + 1) * P], consts["ident"][:])
                    tr.then_inc(tr_done, 1)

                @block.scalar
                def _(act):
                    cols = bass.ds(i * P, P)
                    for n, (bank, q, k) in enumerate(((1, "qD", "kD"), (0, "qA", "kA"))):
                        act.wait_ge(tr_done, n + 1)
                        act.activation(b[q][:, :, cols], ps[:, bank, 0:2], ACT.Copy).then_inc(copied, 1)
                        act.activation(b[k][:, :, cols], ps[:, bank, 2:4], ACT.Copy).then_inc(copied, 1)


def attend_stage(nc, s, b, consts, group, first, last, key_tiles, bias_dram):
    diff = group == "A"
    parts = 2 if diff else 1
    per_tile = HEADS * parts
    jobs = 2 * HEADS
    nk = key_tiles * P
    scale = 32 ** -0.5 if diff else HD ** -0.5
    qT, kT, vt = b["q" + group], b["k" + group], b["v" + group]
    col = 0 if diff else 3 * GW
    nm = f"at{group}{first}_"
    with ExitStack() as es:
        sb = lambda n, sh: es.enter_context(nc.sbuf_tensor(nm + n, sh, F32))
        q = sb("q", [P, 2 * per_tile, P])
        e = sb("e", [P, 4, nk])
        pr = sb("p", [P, 2, nk])
        pt = sb("pt", [P, 2, key_tiles, P])
        st = sb("st", [P, 4, 2 * per_tile])
        sx = sb("sx", [P, 2, nk])
        bias = sb("bias", [P, 2, HEADS, SEQ]) if bias_dram is not None else None
        o = sb("o", [P, 2 * HEADS, HD])
        sq = sb("sq", [P, 2 * HEADS, HD])
        r = sb("r", [P, 3, 2 * HEADS])
        ps = es.enter_context(nc.psum_tensor(nm + "ps", [P, 2, 1024], F32))
        pst = es.enter_context(nc.psum_tensor(nm + "pst", [P, 8, P], F32))
        pso = es.enter_context(nc.psum_tensor(nm + "pso", [P, 2, 512], F32))
        with nc.Fori(first // 2, last // 2) as pair:
            i = pair * 2
            with stage(nc, "q_ready", "bias0_in", "bias1_in", "scores_done", "scores_read", "max_ready", "exp_done", "probs_ready", "tr_done",
                       "pt_ready", "av_done", "dve_step", "sq_ready", "sqrt_done", "o_ready", "o_gone") as \
                    (block, q_ready, bias0_in, bias1_in, scores_done, scores_read, max_ready, exp_done, probs_ready, tr_done,
                     pt_ready, av_done, dve_step, sq_ready, sqrt_done, o_ready, o_gone):

                @block.sync
                def _(sp):
                    if bias_dram is not None:
                        for tt in range(2):
                            sp.dma_start(bias[:, tt], bias_dram[i - first + tt]).then_inc((bias0_in, bias1_in)[tt], 16)
                    sp.wait_ge(o_ready, 1)
                    for tt in range(2):
                        sp.dma_start(s["y"][bass.ds((i + tt) * P, P), col:col + GW],
                                     o[:, tt * HEADS:(tt + 1) * HEADS].rearrange("p h e -> p (h e)")).then_inc(o_gone, 16)
                    sp.wait_ge(o_gone, 32)

                @block.tensor
                def _(pe):
                    def score(u):
                        h = u // parts % HEADS
                        if u % per_tile == 0:
                            pe.wait_ge(q_ready, u // per_tile + 1)
                        if u >= 2:
                            pe.wait_ge(scores_read, u - 1)
                        for c0 in range(0, nk, 512):
                            c1 = min(nk, c0 + 512)
                            mm = pe.matmul(ps[:, u % 2, c0:c1], q[:, u, :], kT[:, h // 2, c0:c1], start=True, stop=True)
                        mm.then_inc(scores_done, 1)

                    def weighted(j):
                        h = j % HEADS
                        pe.wait_ge(pt_ready, j + 1)
                        for k in range(key_tiles):
                            mm = pe.matmul(pso[:, j // HEADS, h * HD:(h + 1) * HD], pt[:, j % 2, k, :], vt[:, k, h * HD:(h + 1) * HD],
                                           start=(k == 0), stop=(k == key_tiles - 1))
                        mm.then_inc(av_done, 1)

                    for u in range(2):
                        score(u)
                    for j in range(jobs):
                        for u in range(parts * j + 2, parts * (j + 1) + 2):
                            if u < parts * jobs:
                                score(u)
                        pe.wait_ge(probs_ready, j + 1)
                        if j >= 1:
                            pe.wait_ge(pt_ready, j)
                        for k in range(key_tiles):
                            tr = pe.transpose(pst[:, k, :], pr[:, j % 2, k * P:(k + 1) * P], consts["ident"][:])
                        tr.then_inc(tr_done, 1)
                        if j >= 1:
                            weighted(j - 1)
                    weighted(jobs - 1)

                @block.scalar
                def _(act):
                    for j in range(jobs + 1):
                        if j < jobs:
                            for u in range(parts * j, parts * (j + 1)):
                                act.wait_ge(max_ready, u + 1)
                                if u >= 4:
                                    act.wait_ge(probs_ready, (u - 4) // parts + 1)
                                src = sx[:, u % 2, :] if bias is not None else ps[:, u % 2, 0:nk]
                                act.activation(e[:, u % 4, :], src, ACT.Exp, bias=st[:, 1, u:u + 1],
                                               scale=1.0 if bias is not None else scale,
                                               accum_out=st[:, 2, u:u + 1]).then_inc(exp_done, 1)
                                if bias is None:
                                    act.wait_ge(exp_done, u + 1)
                                    act.sem_inc(scores_read, 1)
                        if j >= 1:
                            act.wait_ge(tr_done, j)
                            if j >= 3:
                                act.wait_ge(av_done, j - 2)
                            act.activation(pt[:, (j - 1) % 2], pst[:, 0:key_tiles, :], ACT.Copy).then_inc(pt_ready, 1)
                    if diff:
                        act.wait_ge(sq_ready, 1)
                        act.activation(r[:, 1, :], r[:, 0, :], ACT.Sqrt).then_inc(sqrt_done, 1)

                @block.vector
                def _(v):
                    link = chained(v, dve_step)

                    def masked_queries(tt):
                        for x in range(per_tile):
                            h = x // parts
                            row = 2 + (h % 2) * 2 + x % 2 if diff else h % 2
                            mask = v.tensor_scalar(q[:, tt * per_tile + x, :], qT[:, h // 2, bass.ds((i + tt) * P, P)], consts["rows"][:, row:row + 1], None, ALU.mult)
                        mask.then_inc(q_ready, 1)

                    def maximum(u):
                        v.wait_ge(scores_done, u + 1)
                        src = ps[:, u % 2, 0:nk]
                        if bias is not None:
                            if u % HEADS == 0:
                                v.wait_ge((bias0_in, bias1_in)[u // HEADS], 16)
                            if u >= 2:
                                v.wait_ge(exp_done, u - 1)
                            v.tensor_scalar(sx[:, u % 2, 0:CTX], ps[:, u % 2, 0:CTX], scale, None, ALU.mult)
                            link(v.scalar_tensor_tensor(sx[:, u % 2, CTX:nk], ps[:, u % 2, CTX:nk], scale, bias[:, u // HEADS, u % HEADS, :], ALU.mult, ALU.add))
                            v.sem_inc(scores_read, 1)
                            src = sx[:, u % 2, :]
                        link(v.tensor_reduce(st[:, 0, u:u + 1], src, X, ALU.max))
                        v.tensor_scalar(st[:, 1, u:u + 1], st[:, 0, u:u + 1], -1.0 if bias is not None else -scale, None, ALU.mult).then_inc(max_ready, 1)

                    masked_queries(0)
                    for u in range(parts):
                        maximum(u)
                    masked_queries(1)
                    for j in range(jobs):
                        if not diff and j + 1 < jobs:
                            maximum(j + 1)
                        u = parts * j
                        v.wait_ge(exp_done, u + parts)
                        if j >= 2:
                            v.wait_ge(tr_done, j - 1)
                        link(v.reciprocal(st[:, 3, u:u + parts], st[:, 2, u:u + parts]))
                        if diff:
                            x1, x2 = u, u + 1
                            link(v.tensor_scalar(e[:, x2 % 4, :], e[:, x2 % 4, :], st[:, 3, x2:x2 + 1], b["lam"][:, 0:1], ALU.mult, ALU.mult))
                            v.scalar_tensor_tensor(pr[:, j % 2, :], e[:, x1 % 4, :], st[:, 3, x1:x1 + 1], e[:, x2 % 4, :],
                                                   ALU.mult, ALU.subtract).then_inc(probs_ready, 1)
                        else:
                            v.tensor_scalar(pr[:, j % 2, :], e[:, u % 4, :], st[:, 3, u:u + 1], None, ALU.mult).then_inc(probs_ready, 1)
                        if diff and j + 1 < jobs:
                            for u in range(parts * (j + 1), parts * (j + 2)):
                                maximum(u)
                    v.wait_ge(av_done, jobs)
                    out = v.tensor_copy(o[:].rearrange("p (t h) e -> p t (h e)", t=2), pso[:, :, 0:GW])
                    if not diff:
                        out.then_inc(o_ready, 1)
                        return
                    link(out)
                    link(v.tensor_tensor(sq[:], o[:], o[:], ALU.mult))
                    link(v.tensor_reduce(r[:, 2, :], sq[:], X, ALU.add))
                    v.tensor_scalar(r[:, 0, :], r[:, 2, :], 1.0 / HD, NORM_EPS, ALU.mult, ALU.add).then_inc(sq_ready, 1)
                    v.wait_ge(sqrt_done, 1)
                    link(v.reciprocal(r[:, 2, :], r[:, 1, :]))
                    link(v.tensor_tensor(o[:], o[:], r[:, 2, :].unsqueeze(2).to_broadcast([P, 2 * HEADS, HD]), ALU.mult))
                    v.tensor_tensor(o[:], o[:], b["g"][:].unsqueeze(1).to_broadcast([P, 2 * HEADS, HD]), ALU.mult).then_inc(o_ready, 1)


def head_bc(x):
    return x.unsqueeze(2).to_broadcast(list(x.shape) + [HD])


def by_head(x):
    return x.rearrange("p (h e) -> p h e", e=HD)


def scan_stages(nc, l, t, s, consts):
    prep_stage(nc, l, t, s, consts)
    chunk_stage(nc, t, s, consts)
    scan_post_stage(nc, l, t, s, consts)


def store_chunks(eng, dst, src, i, back, sem):
    for d, tile in ((0, i), (1, back)):
        for half in range(2):
            eng.dma_start(dst[tile, half, d].rearrange("b t q a e -> t b (q a e)"),
                          src[half * C:(half + 1) * C, d].rearrange("t b q a e -> t b (q a e)")).then_inc(sem, 16)


def heads_of(x):
    return x.rearrange("p (a b e) -> p a b e", a=2, b=2)


def heads_bc(x):
    return x.rearrange("p (a b) -> p a b", a=2).unsqueeze(3).to_broadcast([P, 2, 2, HD])


def prep_stage(nc, l, t, s, consts):
    W, V = RWKV_COLS, GDN_QKV
    ND = 2 * HEADS
    with ExitStack() as es:
        sb = lambda n, sh: es.enter_context(nc.sbuf_tensor("pp_" + n, sh, F32))
        mu, w2, a2, g2 = sb("mu", [P, 3, W]), sb("w2", [P, 2, GW]), sb("a2", [P, 2, GW]), sb("g2", [P, GW])
        w0, a0, kk_g, ka_g, rk_g = sb("w0", [P, 2 * GW]), sb("a0", [P, 2 * GW]), sb("kkg", [P, GW]), sb("kag", [P, GW]), sb("rkg", [P, GW])
        f, fp, fn, edge = sb("f", [P, W]), sb("fp", [P, W]), sb("fn", [P, W]), sb("edge", [P, 2])
        low, lowT = sb("low", [P, 2, P]), sb("lowT", [P, 3, P])
        wr, ar, sg, ex, av = [sb(n, [P, 2, GW]) for n in ("wr", "ar", "sg", "ex", "av")]
        e_in, e_neg, e_ex, dec = [sb(n, [P, 2, GW]) for n in ("ein", "eneg", "eex", "dec")]
        kk, sq, kd, kka = sb("kk", [P, GW]), sb("sq", [P, GW]), sb("kd", [P, 2, GW]), sb("kka", [P, 2, GW])
        n4 = sb("n4", [P, 4, HEADS])
        out, post, rks = sb("out", [P, 2, 2, 5, 2, HD]), sb("post", [P, 2, GW]), sb("rks", [P, 2, GW])
        cw, alog, dtb = sb("cw", [P, 3, V]), sb("alog", [P, ND]), sb("dtb", [P, ND])
        gf, gfp, gfn = sb("gf", [P, GDN_COLS]), sb("gfp", [P, V]), sb("gfn", [P, V])
        qkv, gsq, n8 = sb("qkv", [P, V]), sb("gsq", [P, 2 * GW]), sb("n8", [P, 4, ND])
        x8, cols, cols_b = sb("x8", [P, 16, ND]), sb("cols", [P, 2, ND]), sb("cols_b", [P, 2, ND])
        gout, gpost = sb("gout", [P, 2, 2, 7, 2, HD]), sb("gpost", [P, GW])
        ps = es.enter_context(nc.psum_tensor("pp_ps", [P, 7, 512], F32))
        flat = lambda x: x[:].rearrange("p a b -> p (a b)")
        over_dir = lambda x: x.unsqueeze(1).to_broadcast([P, 2, GW])
        quantity = lambda o, d, n: o[:, d, :, n].rearrange("p b a e -> p a b e")
        x, neg, ax, u, den, z, z2, acc, top, g, gap, beta, egc, egap, bg = [x8[:, k, :] for k in range(15)]

        with stage(nc, "zeroed", "params_in", "mid", "exp_done") as (block, zeroed, params_in, mid, exp_done):
            @block.gpsimd
            def _(pool):
                pool.memset(w2[:], 0.0).then_inc(zeroed, 1)
                pool.memset(a2[:], 0.0).then_inc(zeroed, 1)

            @block.sync
            def _(sp):
                loads = [(mu[:, 0], over_rows(t["rwkv_mu"][l, 0])), (mu[:, 2], over_rows(t["rwkv_mu"][l, 1])), (g2[:], t["rwkv_g2"][l]),
                         (w0[:], over_rows(t["rwkv_w0"][l])), (a0[:], over_rows(t["rwkv_a0"][l])), (kk_g[:], over_rows(t["rwkv_kk"][l])),
                         (ka_g[:], over_rows(t["rwkv_ka"][l])), (rk_g[:], over_rows(t["rwkv_rk"][l]))]
                loads += [(cw[:, k], over_rows(t["gdn_conv"][l, k])) for k in range(3)]
                loads += [(alog[:], over_rows(t["gdn_a_log"][l])), (dtb[:], over_rows(t["gdn_dt_bias"][l]))]
                sp.wait_ge(zeroed, 2)
                for d in range(2):
                    for dst, src in ((w2, "rwkv_w2"), (a2, "rwkv_a2")):
                        loads.append((dst[d * LORA:(d + 1) * LORA, d, :], t[src][l, d]))
                for dst, src in loads:
                    sp.dma_start(dst, src).then_inc(params_in, 16)
                sp.wait_ge(params_in, 16 * 17)

            @block.vector
            def _(v):
                v.wait_ge(params_in, 16 * 17)
                v.tensor_tensor(mu[:, 1], mu[:, 0], mu[:, 2], ALU.add).then_inc(mid, 1)
                v.wait_ge(mid, 1)
                v.tensor_scalar(mu[:, 1], mu[:, 1], -1.0, 1.0, ALU.mult, ALU.add)

            @block.scalar
            def _(act):
                act.wait_ge(params_in, 16 * 17)
                act.activation(alog[:], alog[:], ACT.Exp).then_inc(exp_done, 1)

        with nc.Fori(0, TILES) as i:
            with stage(nc, "f_in", "sides_in", "gf_in", "gsides_in", "sides_ready", "gsides_ready", "f_ready", "low_ready", "low_done", "lowT_ready",
                       "raw_done", "raw_ready", "gates_ready", "g_copied", "sums_done", "ex_ready", "exps_ready", "sq_ready", "root_ready",
                       "dve_step", "out_ready", "stored", "abs_ready", "exp_ready", "g_ready", "gsums_done", "conv_ready", "qkv_ready",
                       "gate_ready", "beta_ready", "gsq_ready", "groot_ready", "dec_ready", "gexps_ready", "gout_ready", "gstored") as \
                    (block, f_in, sides_in, gf_in, gsides_in, sides_ready, gsides_ready, f_ready, low_ready, low_done, lowT_ready,
                     raw_done, raw_ready, gates_ready, g_copied, sums_done, ex_ready, exps_ready, sq_ready, root_ready,
                     dve_step, out_ready, stored, abs_ready, exp_ready, g_ready, gsums_done, conv_ready, qkv_ready,
                     gate_ready, beta_ready, gsq_ready, groot_ready, dec_ready, gexps_ready, gout_ready, gstored):
                @block.sync
                def _(sp):
                    cols_r = slice(COL_B, COL_B + W)
                    sp.dma_start(gf[:], s["p"][bass.ds(i * P + 1, P), COL_C:COL_C + GDN_COLS]).then_inc(gf_in, 16)
                    sp.dma_start(f[:], s["p"][bass.ds(i * P + 1, P), cols_r]).then_inc(f_in, 16)
                    sp.dma_start(edge[:], t["k_edges"][i]).then_inc(f_in, 16)
                    sp.dma_start(fp[:], s["p"][bass.ds(i * P, P), cols_r]).then_inc(sides_in, 16)
                    sp.dma_start(fn[:], s["p"][bass.ds(i * P + 2, P), cols_r]).then_inc(sides_in, 16)
                    sp.dma_start(gfp[:], s["p"][bass.ds(i * P, P), COL_C:COL_C + V]).then_inc(gsides_in, 16)
                    sp.dma_start(gfn[:], s["p"][bass.ds(i * P + 2, P), COL_C:COL_C + V]).then_inc(gsides_in, 16)
                    back = sp.snap((i + 4) % TILES + CTX_TILES)
                    sp.wait_ge(out_ready, 1)
                    store_chunks(sp, s["rw"], out, i, back, stored)
                    for d, tile in ((0, i), (1, back)):
                        sp.dma_start(s["rwdec"][bass.ds(tile * 2, 2), d], dec[0:C + 1:C, d, :]).then_inc(stored, 16)
                    sp.dma_start(s["rwpost"][i], post[:]).then_inc(stored, 16)
                    sp.wait_ge(gout_ready, 1)
                    store_chunks(sp, s["gd"], gout, i, back, gstored)
                    for d, tile in ((0, i), (1, back)):
                        for half in range(2):
                            sp.dma_start(s["gdcol"][tile * 2 + half, d].rearrange("b t m -> t b m"),
                                         cols_b[half * C:(half + 1) * C, :, 4 * d:4 * d + 4]).then_inc(gstored, 16)
                    sp.dma_start(s["gdpost"][i], gpost[:]).then_inc(gstored, 16)
                    sp.wait_ge(stored, 16 * 7)
                    sp.wait_ge(gstored, 16 * 9)

                @block.gpsimd
                def _(pool):
                    pool.wait_ge(sides_in, 32)
                    pool.tensor_tensor(fp[:], fp[:], mu[:, 0], ALU.mult).then_inc(sides_ready, 1)
                    pool.tensor_tensor(fn[:], fn[:], mu[:, 2], ALU.mult).then_inc(sides_ready, 1)
                    pool.wait_ge(gsides_in, 32)
                    pool.tensor_tensor(gfp[:], gfp[:], cw[:, 0], ALU.mult).then_inc(gsides_ready, 1)
                    pool.tensor_tensor(gfn[:], gfn[:], cw[:, 2], ALU.mult).then_inc(gsides_ready, 1)

                @block.vector
                def _(v):
                    link = chained(v, dve_step)
                    r, k, val = f[:, 0:GW], f[:, GW:2 * GW], f[:, 2 * GW:3 * GW]

                    v.wait_ge(gf_in, 16)
                    link(v.tensor_tensor(x, gf[:, 4 * GW:4 * GW + ND], dtb[:], ALU.add))
                    link(v.tensor_scalar(neg, x, -1.0, None, ALU.mult))
                    v.tensor_tensor(ax, x, neg, ALU.max).then_inc(abs_ready, 1)
                    v.tensor_scalar(top, x, 0.0, None, ALU.max)
                    v.wait_ge(f_in, 32)
                    link(v.tensor_tensor(f[:], f[:], mu[:, 1], ALU.mult))
                    v.wait_ge(sides_ready, 1)
                    link(v.scalar_tensor_tensor(f[:], fp[:], edge[:, 0:1], f[:], ALU.mult, ALU.add))
                    v.wait_ge(sides_ready, 2)
                    link(v.scalar_tensor_tensor(f[:], fn[:], edge[:, 1:2], f[:], ALU.mult, ALU.add))
                    v.sem_inc(f_ready, 1)
                    link(v.tensor_tensor(qkv[:], gf[:, 0:V], cw[:, 1], ALU.mult))
                    v.wait_ge(gsides_ready, 1)
                    link(v.scalar_tensor_tensor(qkv[:], gfp[:], edge[:, 0:1], qkv[:], ALU.mult, ALU.add))
                    v.wait_ge(gsides_ready, 2)
                    v.scalar_tensor_tensor(qkv[:], gfn[:], edge[:, 1:2], qkv[:], ALU.mult, ALU.add).then_inc(conv_ready, 1)
                    link(v.tensor_tensor(kk[:], k, kk_g[:], ALU.mult))
                    link(v.tensor_tensor(sq[:], kk[:], kk[:], ALU.mult))
                    link(v.tensor_reduce(n4[:, 0, :], by_head(sq[:]), X, ALU.add))
                    v.tensor_scalar(n4[:, 1, :], n4[:, 0, :], NORM_EPS, None, ALU.add).then_inc(sq_ready, 1)
                    v.wait_ge(exp_ready, 1)
                    link(v.tensor_scalar(den, u, 2.0, None, ALU.add))
                    link(v.reciprocal(z2, den))
                    link(v.tensor_tensor(z, u, z2, ALU.mult))
                    link(v.tensor_tensor(z2, z, z, ALU.mult))
                    link(v.tensor_scalar(acc, z2, 2.0 / 19, 2.0 / 17, ALU.mult, ALU.add))
                    for odd in (15, 13, 11, 9, 7, 5, 3, 1):
                        link(v.tensor_tensor(acc, acc, z2, ALU.mult))
                        link(v.tensor_scalar(acc, acc, 2.0 / odd, None, ALU.add))
                    link(v.tensor_tensor(acc, acc, z, ALU.mult))
                    link(v.tensor_tensor(acc, acc, top, ALU.add))
                    v.scalar_tensor_tensor(g, acc, -1.0, alog[:], ALU.mult, ALU.mult).then_inc(g_ready, 1)
                    v.wait_ge(raw_done, 1)
                    v.tensor_tensor(flat(wr), ps[:, 1, :], w0[:], ALU.add).then_inc(raw_ready, 1)
                    v.wait_ge(raw_done, 2)
                    v.tensor_tensor(flat(ar), ps[:, 2, :], a0[:], ALU.add).then_inc(raw_ready, 1)
                    v.wait_ge(qkv_ready, 1)
                    link(v.tensor_tensor(gsq[:], qkv[:, 0:2 * GW], qkv[:, 0:2 * GW], ALU.mult))
                    link(v.tensor_reduce(n8[:, 0, :], by_head(gsq[:]), X, ALU.add))
                    v.tensor_scalar(n8[:, 1, :], n8[:, 0, :], NORM_EPS, None, ALU.add).then_inc(gsq_ready, 1)
                    v.wait_ge(gsums_done, 1)
                    link(v.tensor_copy(cols[:], ps[:, 6, 0:2 * ND].rearrange("p (a n) -> p a n", a=2)))
                    for w in range(2):
                        for b in range(2):
                            v.tensor_copy(cols_b[:, b].rearrange("p (d w a) -> p d w a", d=2, w=2)[:, :, w, :],
                                          cols[:, w].rearrange("p (d a b) -> p d a b", d=2, a=2)[:, :, :, b])
                    v.tensor_tensor(gap, cols[:, 1], cols[:, 0], ALU.subtract).then_inc(dec_ready, 1)
                    v.wait_ge(root_ready, 1)
                    link(v.reciprocal(n4[:, 3, :], n4[:, 2, :]))
                    link(v.tensor_tensor(by_head(kk[:]), by_head(kk[:]), head_bc(n4[:, 3, :]), ALU.mult))
                    v.wait_ge(sums_done, 1)
                    v.wait_ge(gates_ready, 2)
                    v.tensor_tensor(flat(ex), ps[:, 4, :], flat(sg), ALU.subtract).then_inc(ex_ready, 1)
                    v.tensor_tensor(kka[:], av[:], over_dir(kk[:]), ALU.mult)
                    link(v.scalar_tensor_tensor(kd[:], av[:], -1.0, over_dir(ka_g[:]), ALU.add, ALU.mult))
                    link(v.scalar_tensor_tensor(kd[:], kd[:], 1.0, over_dir(k), ALU.add, ALU.mult))
                    v.tensor_tensor(rks[:, 0], r, rk_g[:], ALU.mult)
                    link(v.tensor_tensor(sq[:], kd[:, 0], kd[:, 1], ALU.add))
                    link(v.tensor_tensor(rks[:, 1], rks[:, 0], sq[:], ALU.mult))
                    link(v.tensor_reduce(n4[:, 0, :], by_head(rks[:, 1]), X, ALU.add))
                    v.tensor_tensor(by_head(post[:, 0]), by_head(val), head_bc(n4[:, 0, :]), ALU.mult)
                    for d in range(2):
                        v.tensor_copy(quantity(out, d, 4), heads_of(val))
                    v.wait_ge(exps_ready, 4)
                    for d in range(2):
                        v.tensor_tensor(quantity(out, d, 0), heads_of(e_ex[:, d]), heads_of(kk[:]), ALU.mult)
                        v.tensor_tensor(quantity(out, d, 1), heads_of(e_neg[:, d]), heads_of(kka[:, d]), ALU.mult)
                        v.tensor_tensor(quantity(out, d, 2), heads_of(e_neg[:, d]), heads_of(kd[:, d]), ALU.mult)
                        last = v.tensor_tensor(quantity(out, d, 3), heads_of(e_in[:, d]), heads_of(r), ALU.mult)
                    v.wait_ge(g_copied, 1)
                    link(last)
                    v.sem_inc(out_ready, 1)
                    v.wait_ge(groot_ready, 1)
                    link(v.reciprocal(n8[:, 3, :], n8[:, 2, :]))
                    link(v.tensor_scalar(n8[:, 3, 0:HEADS], n8[:, 3, 0:HEADS], HD ** -0.5, None, ALU.mult))
                    link(v.tensor_tensor(by_head(qkv[:, 0:2 * GW]), by_head(qkv[:, 0:2 * GW]), head_bc(n8[:, 3, :]), ALU.mult))
                    v.wait_ge(gexps_ready, 2)
                    v.wait_ge(beta_ready, 1)
                    link(v.tensor_tensor(bg, beta, egc, ALU.mult))
                    gq, gk, gval = [qkv[:, m * GW:(m + 1) * GW] for m in range(3)]
                    for d in range(2):
                        hs = slice(d * HEADS, (d + 1) * HEADS)
                        for n, (src, by) in enumerate(((gk, bg), (gk, beta), (gk, None), (gq, None), (gq, egc), (gk, egap), (gval, beta))):
                            if by is None:
                                last = v.tensor_copy(quantity(gout, d, n), heads_of(src))
                            else:
                                last = v.tensor_tensor(quantity(gout, d, n), heads_of(src), heads_bc(by[:, hs]), ALU.mult)
                    link(last)
                    v.wait_ge(gate_ready, 1)
                    v.sem_inc(gout_ready, 1)

                @block.scalar
                def _(act):
                    act.wait_ge(abs_ready, 1)
                    act.activation(u, ax, ACT.Exp, scale=-1.0).then_inc(exp_ready, 1)
                    act.wait_ge(f_ready, 1)
                    act.activation(low[:, 0], f[:, 3 * GW:3 * GW + P], ACT.Tanh).then_inc(low_ready, 1)
                    act.activation(low[:, 1], f[:, 3 * GW + 2 * P:3 * GW + 3 * P], ACT.Sigmoid).then_inc(low_ready, 1)
                    act.wait_ge(gf_in, 16)
                    act.activation(beta, gf[:, 4 * GW + ND:4 * GW + 2 * ND], ACT.Sigmoid).then_inc(beta_ready, 1)
                    act.wait_ge(low_done, 1)
                    act.activation(lowT[:], ps[:, 0, 0:3 * P].rearrange("p (a b) -> p a b", a=3), ACT.Copy).then_inc(lowT_ready, 1)
                    act.wait_ge(conv_ready, 1)
                    act.activation(qkv[:], qkv[:], ACT.Silu).then_inc(qkv_ready, 1)
                    act.activation(gpost[:], gf[:, 3 * GW:4 * GW], ACT.Silu).then_inc(gate_ready, 1)
                    act.wait_ge(raw_ready, 1)
                    act.activation(flat(sg), flat(wr), ACT.Sigmoid).then_inc(gates_ready, 1)
                    act.wait_ge(raw_ready, 2)
                    act.activation(flat(av), flat(ar), ACT.Sigmoid).then_inc(gates_ready, 1)
                    act.wait_ge(raw_done, 3)
                    act.activation(post[:, 1], ps[:, 3, 0:GW], ACT.Copy).then_inc(g_copied, 1)
                    act.wait_ge(sq_ready, 1)
                    act.activation(n4[:, 2, :], n4[:, 1, :], ACT.Sqrt).then_inc(root_ready, 1)
                    act.wait_ge(gsq_ready, 1)
                    act.activation(n8[:, 2, :], n8[:, 1, :], ACT.Sqrt).then_inc(groot_ready, 1)
                    act.wait_ge(ex_ready, 1)
                    act.activation(flat(e_in), ps[:, 4, :], ACT.Exp, scale=DECAY).then_inc(exps_ready, 1)
                    act.activation(flat(e_neg), ps[:, 4, :], ACT.Exp, scale=-DECAY).then_inc(exps_ready, 1)
                    act.activation(flat(e_ex), flat(ex), ACT.Exp, scale=DECAY).then_inc(exps_ready, 1)
                    act.wait_ge(sums_done, 2)
                    act.activation(flat(dec), ps[:, 5, :], ACT.Exp, scale=DECAY).then_inc(exps_ready, 1)
                    act.wait_ge(dec_ready, 1)
                    act.activation(egc, cols[:, 0], ACT.Exp).then_inc(gexps_ready, 1)
                    act.activation(egap, gap, ACT.Exp).then_inc(gexps_ready, 1)

                @block.tensor
                def _(pe):
                    pe.wait_ge(low_ready, 2)
                    for n, src in enumerate((low[:, 0], f[:, 3 * GW + P:3 * GW + 2 * P], low[:, 1])):
                        tr = pe.transpose(ps[:, 0, n * P:(n + 1) * P], src, consts["ident"][:])
                    tr.then_inc(low_done, 1)
                    pe.wait_ge(lowT_ready, 1)
                    pe.matmul(ps[:, 1, :], lowT[:, 0], flat(w2), start=True, stop=True).then_inc(raw_done, 1)
                    pe.matmul(ps[:, 2, :], lowT[:, 1], flat(a2), start=True, stop=True).then_inc(raw_done, 1)
                    pe.matmul(ps[:, 3, 0:GW], lowT[:, 2], g2[:], start=True, stop=True).then_inc(raw_done, 1)
                    pe.wait_ge(g_ready, 1)
                    for d in range(2):
                        pe.matmul(ps[:, 6, d * HEADS:(d + 1) * HEADS], consts["sums"][:, d, :], g[:, d * HEADS:(d + 1) * HEADS], start=True, stop=True)
                    pe.matmul(ps[:, 6, ND:2 * ND], consts["sums"][:, 2, :], g, start=True, stop=True).then_inc(gsums_done, 1)
                    pe.wait_ge(gates_ready, 1)
                    for d in range(2):
                        mm = pe.matmul(ps[:, 4, d * GW:(d + 1) * GW], consts["sums"][:, d, :], sg[:, d], start=True, stop=True)
                    mm.then_inc(sums_done, 1)
                    pe.matmul(ps[:, 5, :], consts["sums"][:, 2, :], flat(sg), start=True, stop=True).then_inc(sums_done, 1)


def chunk_stage(nc, t, s, consts):
    NQ = (4, 6)
    NT = (4, 5)
    N4 = 4
    with ExitStack() as es:
        sb = lambda n, sh: es.enter_context(nc.sbuf_tensor("ch_" + n, sh, F32))
        masks = sb("masks", [P, 14, N4, P])
        bd = [sb(f"bd{k}", [P, 2, NQ[k], 2, P]) for k in range(2)]
        val = [sb(f"val{k}", [P, 2, 2, HD]) for k in range(2)]
        tq = [sb(f"tq{k}", [P, NT[k], N4, P]) for k in range(2)]
        am = [sb(f"am{k}", [P, 2, N4, P]) for k in range(2)]
        m = [sb(f"m{k}", [P, 6, 2, N4, P]) for k in range(2)]
        x = [sb(f"x{k}", [P, 2, N4, P]) for k in range(2)]
        y = [sb(f"y{k}", [P, N4, P]) for k in range(2)]
        akt, rk, rb, qk = [sb(n, [P, N4, P]) for n in ("akt", "rk", "rb", "qk")]
        diag, du, dd = sb("diag", [P, N4, P]), sb("du", [P, 2, N4, P]), sb("dd", [P, 2, N4, P])
        st = [sb(f"st{k}", [P, N4, HD]) for k in range(2)]
        rhs = [sb(f"rhs{k}", [P, N4, HD]) for k in range(2)]
        nn = [sb(f"nn{k}", [P, N4, HD]) for k in range(2)]
        oo = [sb(f"oo{k}", [P, N4, HD]) for k in range(2)]
        col = sb("col", [P, 2, 2, 2])
        dec = [sb(f"dec{k}", [P, N4]) for k in range(2)]
        ones = sb("ones", [P, P])
        ps = es.enter_context(nc.psum_tensor("ch_ps", [P, 8, N4, P], F32))
        prob = lambda n: (n // 2, n % 2)
        src_dram = (s["rw"], s["gd"])

        with stage(nc, "masks_in") as (block, masks_in):
            @block.sync
            def _(sp):
                sp.dma_start(masks[:], t["k_masks"]).then_inc(masks_in, 16)
                sp.wait_ge(masks_in, 16)

            @block.gpsimd
            def _(pool):
                for k in range(2):
                    pool.memset(bd[k][:], 0.0)
                    pool.memset(st[k][:], 0.0)
                pool.memset(ones[:], 1.0)

        names = ["rw_in", "gd_in", "col_in", "dec_in", "diag_ready", "diffs_done", "du_ready", "dd_ready", "ddm_ready", "tr_done",
                 "tr_copied", "gram_done", "gram_ready", "m_ready", "x_ready", "y_done", "y_ready", "z_done", "z_read", "rhs_done", "rhs_ready0",
                 "rhs_ready1", "n_done", "n_ready", "o_done", "o_ready", "ds_done", "dve_step", "gdec_ready", "stored", "state_step"]
        with nc.Fori(0, CHUNKS) as c:
            with stage(nc, *names) as (block, rw_in, gd_in, col_in, dec_in, diag_ready, diffs_done, du_ready, dd_ready, ddm_ready, tr_done,
                                       tr_copied, gram_done, gram_ready, m_ready, x_ready, y_done, y_ready, z_done, z_read, rhs_done, rhs_ready0,
                                       rhs_ready1, n_done, n_ready, o_done, o_ready, ds_done, dve_step, gdec_ready, stored, state_step):
                fwd, bwd = c, 15 - c

                @block.sync
                def _(sp):
                    def load(k, d, at, sem):
                        src = src_dram[k].rearrange("i c d b t q a e -> (i c) d b t q a e")[at, d]
                        for b in range(2):
                            sp.dma_start(bd[k][b * C:(b + 1) * C, d, :, :, b * C:(b + 1) * C].rearrange("t q a e -> t (q a) e"),
                                         src[b, :, 0:NQ[k]].rearrange("t q a e -> t (q a) e")).then_inc(sem, 16)
                        sp.dma_start(val[k][:, d], src[:, :, NQ[k]].rearrange("b t a e -> (b t) a e")).then_inc(sem, 16)

                    for d, at in enumerate((fwd, bwd)):
                        sp.dma_start(col[:, :, d], s["gdcol"][at, d].rearrange("b t (w a) -> (b t) w a", w=2)).then_inc(col_in, 16)
                    for k, sem in enumerate((rw_in, gd_in)):
                        for d, at in enumerate((fwd, bwd)):
                            load(k, d, at, sem)
                    for d, at in enumerate((fwd, bwd)):
                        sp.dma_start(dec[0][:, 2 * d:2 * d + 2], s["rwdec"][at, d].rearrange("(a p) -> p a", p=P),
                                     allow_slow_non_contiguous=True).then_inc(dec_in, 16)
                    n = 0
                    for k in range(2):
                        sp.wait_ge(o_ready, k + 1)
                        for b in range(2):
                            for d, at in ((0, c), (1, 23 - c), (1, 11 - c)):
                                sp.dma_start(s["scan"][k, d, at].rearrange("t (a b e) -> b t a e", a=2, b=2)[b],
                                             oo[k][b * C:(b + 1) * C, 2 * d:2 * d + 2]).then_inc(stored, 16)
                                n += 16
                    sp.wait_ge(stored, n)

                @block.gpsimd
                def _(pool):
                    for lev in range(6):
                        for k in range(2):
                            for w in range(2):
                                if lev == 0:
                                    pool.wait_ge(gram_ready, 2 * k + w + 1)
                                pool.tensor_tensor(m[k][:, lev, w], am[k][:, w], masks[:, 2 + 2 * lev + w], ALU.mult).then_inc(m_ready, 1)

                @block.tensor
                def _(pe):
                    pe.wait_ge(diag_ready, 1)
                    pe.matmul(ps[:, 7].rearrange("p a b -> p (a b)"), ones[:], diag[:].rearrange("p a b -> p (a b)"), start=True, stop=True).then_inc(diffs_done, 1)
                    g = 0
                    for k, sem in ((0, rw_in), (1, gd_in)):
                        pe.wait_ge(sem, 16 * 6)
                        for q in range(NT[k]):
                            if g >= 4:
                                pe.wait_ge(tr_copied, g - 3)
                            for n in range(N4):
                                d, a = prob(n)
                                tr = pe.transpose(ps[:, g % 4, n, :], bd[k][:, d, q, a, :], consts["ident"][:])
                            tr.then_inc(tr_done, 1)
                            g += 1
                    grams = [(0, 0, 1), (0, 1, 0), (1, 1, 2), (1, 2, 1), (0, 2, 0), (0, 2, 3), (0, 1, 3), (1, 2, 3)]
                    for g, (k, left, right) in enumerate(grams):
                        pe.wait_ge(tr_copied, 4 if k == 0 else 9)
                        if g >= 3:
                            pe.wait_ge(gram_ready, g - 2)
                        for n in range(N4):
                            mm = pe.matmul(ps[:, 4 + g % 3, n, :], tq[k][:, left, n, :], tq[k][:, right, n, :], start=True, stop=True)
                        mm.then_inc(gram_done, 1)
                    pe.wait_ge(gram_ready, 8)
                    for lev in range(1, 6):
                        for k in range(2):
                            pe.wait_ge(x_ready, 2 * (lev - 1) + k + 1)
                            pe.wait_ge(m_ready, 4 * lev + 2 * k + 2)
                            for n in range(N4):
                                mm = pe.matmul(ps[:, k, n, :], m[k][:, lev, 1, n, :], x[k][:, 0, n, :], start=True, stop=True)
                            mm.then_inc(y_done, 1)
                        for k in range(2):
                            pe.wait_ge(y_ready, 2 * (lev - 1) + k + 1)
                            if lev < 5:
                                for n in range(N4):
                                    pe.matmul(ps[:, 2 + k, n, :], x[k][:, 1, n, :], y[k][:, n, :], start=True, stop=True)
                            for n in range(N4):
                                mm = pe.matmul(ps[:, 4 + k, n, :], y[k][:, n, :], x[k][:, 1, n, :], start=True, stop=True)
                            mm.then_inc(z_done, 1)
                    for n in range(N4):
                        pe.matmul(ps[:, 6, n, 0:HD], tq[0][:, 0, n, :], st[0][:, n, :], start=True, stop=False)
                        mm = pe.matmul(ps[:, 6, n, 0:HD], akt[:, n, :], val[0][:, n // 2, n % 2, :], start=False, stop=True)
                    mm.then_inc(rhs_done, 1)
                    for n in range(N4):
                        mm = pe.matmul(ps[:, 7, n, 0:HD], tq[1][:, 0, n, :], st[1][:, n, :], start=True, stop=True)
                    mm.then_inc(rhs_done, 1)
                    for k in range(2):
                        pe.wait_ge((rhs_ready0, rhs_ready1)[k], 1)
                        pe.wait_ge(x_ready, 11 + k)
                        for n in range(N4):
                            mm = pe.matmul(ps[:, k, n, 0:HD], x[k][:, 1, n, :], rhs[k][:, n, :], start=True, stop=True)
                        mm.then_inc(n_done, 1)
                    for k in range(2):
                        pe.wait_ge(n_ready, k + 1)
                        for n in range(N4):
                            d, a = prob(n)
                            if k == 0:
                                pe.matmul(ps[:, 4, n, 0:HD], bd[0][:, d, 2, a, :], val[0][:, d, a, :], start=True, stop=False)
                                mm = pe.matmul(ps[:, 4, n, 0:HD], bd[0][:, d, 1, a, :], nn[0][:, n, :], start=False, stop=True)
                            else:
                                mm = pe.matmul(ps[:, 5, n, 0:HD], bd[1][:, d, 5, a, :], nn[1][:, n, :], start=True, stop=True)
                        mm.then_inc(ds_done, 1)
                        for n in range(N4):
                            d, a = prob(n)
                            if k == 0:
                                pe.matmul(ps[:, 2, n, 0:HD], tq[0][:, 3, n, :], st[0][:, n, :], start=True, stop=False)
                                pe.matmul(ps[:, 2, n, 0:HD], rk[:, n, :], val[0][:, d, a, :], start=False, stop=False)
                                mm = pe.matmul(ps[:, 2, n, 0:HD], rb[:, n, :], nn[0][:, n, :], start=False, stop=True)
                            else:
                                pe.matmul(ps[:, 3, n, 0:HD], tq[1][:, 4, n, :], st[1][:, n, :], start=True, stop=False)
                                mm = pe.matmul(ps[:, 3, n, 0:HD], qk[:, n, :], nn[1][:, n, :], start=False, stop=True)
                        mm.then_inc(o_done, 1)

                @block.scalar
                def _(act):
                    act.wait_ge(du_ready, 2)
                    for w, sign in ((0, -1.0), (1, 1.0)):
                        act.activation(dd[:, w], du[:, w], ACT.Exp, scale=sign).then_inc(dd_ready, 1)
                    act.activation(dec[1][:], col[:, 1].rearrange("p d a -> p (d a)"), ACT.Exp).then_inc(gdec_ready, 1)
                    g = 0
                    for k in range(2):
                        for q in range(NT[k]):
                            act.wait_ge(tr_done, g + 1)
                            act.activation(tq[k][:, q], ps[:, g % 4], ACT.Copy).then_inc(tr_copied, 1)
                            g += 1
                    for lev in range(1, 6):
                        for k in range(2):
                            act.wait_ge(y_done, 2 * (lev - 1) + k + 1)
                            act.activation(y[k][:], ps[:, k], ACT.Copy).then_inc(y_ready, 1)
                    act.wait_ge(rhs_done, 1)
                    act.activation(rhs[0][:], ps[:, 6, :, 0:HD], ACT.Copy).then_inc(rhs_ready0, 1)
                    for k in range(2):
                        act.wait_ge(n_done, k + 1)
                        act.activation(nn[k][:], ps[:, k, :, 0:HD], ACT.Copy, scale=-1.0 if k == 0 else 1.0).then_inc(n_ready, 1)
                    for k in range(2):
                        act.wait_ge(o_done, k + 1)
                        act.activation(oo[k][:], ps[:, 2 + k, :, 0:HD], ACT.Copy).then_inc(o_ready, 1)

                @block.vector
                def _(v):
                    link = chained(v, dve_step)
                    v.wait_ge(col_in, 32)
                    for n in range(N4):
                        d, a = prob(n)
                        ins = v.tensor_scalar(diag[:, n, :], consts["ident"][:], col[:, 0, d, a:a + 1], None, ALU.mult)
                    ins.then_inc(diag_ready, 1)
                    v.wait_ge(diffs_done, 1)
                    for w, op in ((0, ALU.max), (1, ALU.min)):
                        for n in range(N4):
                            d, a = prob(n)
                            ins = v.tensor_scalar(du[:, w, n, :], ps[:, 7, n, :], col[:, 0, d, a:a + 1], 0.0, ALU.subtract, op)
                        ins.then_inc(du_ready, 1)
                    evac = [(am[0][:, 0], None), (am[0][:, 1], None), (am[1][:, 0], dd[:, 0]), (am[1][:, 1], dd[:, 1]),
                            (akt[:], masks[:, 0]), (rk[:], masks[:, 1]), (rb[:], masks[:, 1]), (qk[:], dd[:, 1])]
                    for g, (dst, by) in enumerate(evac):
                        v.wait_ge(gram_done, g + 1)
                        if g == 2:
                            v.wait_ge(dd_ready, 2)
                        if by is None:
                            v.tensor_copy(dst, ps[:, 4 + g % 3]).then_inc(gram_ready, 1)
                        elif g == 7:
                            link(v.tensor_tensor(dst, ps[:, 4 + g % 3], by, ALU.mult))
                            v.tensor_tensor(dst, dst, masks[:, 1], ALU.mult).then_inc(gram_ready, 1)
                        else:
                            v.tensor_tensor(dst, ps[:, 4 + g % 3], by, ALU.mult).then_inc(gram_ready, 1)
                    eye = consts["ident"][:].unsqueeze(1).to_broadcast([P, N4, P])
                    for k in range(2):
                        v.wait_ge(m_ready, 2 * k + 2)
                        v.tensor_tensor(x[k][:, 0], eye, m[k][:, 0, 0], ALU.subtract)
                        v.tensor_tensor(x[k][:, 1], eye, m[k][:, 0, 1], ALU.subtract).then_inc(x_ready, 1)
                    for lev in range(1, 6):
                        for k in range(2):
                            v.wait_ge(z_done, 2 * (lev - 1) + k + 1)
                            v.wait_ge(x_ready, 2 * (lev - 1) + k + 1)
                            if lev < 5:
                                v.tensor_tensor(x[k][:, 0], x[k][:, 0], ps[:, 2 + k], ALU.subtract)
                            v.tensor_tensor(x[k][:, 1], x[k][:, 1], ps[:, 4 + k], ALU.subtract).then_inc(x_ready, 1)
                    v.wait_ge(rhs_done, 2)
                    v.tensor_tensor(rhs[1][:], val[1][:].rearrange("p d a e -> p (d a) e"), ps[:, 7, :, 0:HD], ALU.subtract).then_inc(rhs_ready1, 1)
                    v.wait_ge(dec_in, 32)
                    v.wait_ge(ds_done, 1)
                    v.wait_ge(o_done, 1)
                    link(v.tensor_tensor(st[0][:], st[0][:], ps[:, 4, :, 0:HD], ALU.add))
                    link(v.tensor_tensor(st[0][:], st[0][:], head_bc(dec[0][:]), ALU.mult))
                    v.wait_ge(gdec_ready, 1)
                    v.wait_ge(ds_done, 2)
                    v.wait_ge(o_done, 2)
                    link(v.tensor_tensor(st[1][:], st[1][:], head_bc(dec[1][:]), ALU.mult))
                    link(v.tensor_tensor(st[1][:], st[1][:], ps[:, 5, :, 0:HD], ALU.add))


def scan_post_stage(nc, l, t, s, consts):
    with ExitStack() as es:
        sb = lambda n, sh: es.enter_context(nc.sbuf_tensor("po_" + n, sh, F32))
        lg, lb, gg = sb("lg", [P, GW]), sb("lb", [P, GW]), sb("gg", [P, HD])
        load_once(nc, [(lg[:], over_rows(t["rwkv_ln_g"][l])), (lb[:], over_rows(t["rwkv_ln_b"][l])), (gg[:], over_rows(t["gdn_norm_g"][l]))])
        y = sb("y", [P, 2, 2, GW])
        sq = sb("sq", [P, 2, GW])
        rp, gp = sb("rp", [P, 2, GW]), sb("gp", [P, GW])
        r = sb("r", [P, 6, 2 * HEADS])
        with nc.Fori(l * CTX_TILES, TILES) as i:
            with stage(nc, "y_in", "post_in", "var_ready", "root_ready", "dve_step", "out_ready", "stored") as \
                    (block, y_in, post_in, var_ready, root_ready, dve_step, out_ready, stored):
                @block.sync
                def _(sp):
                    for k in range(2):
                        for d in range(2):
                            src = s["scan"][k, d].rearrange("c t g -> (c t) g")[bass.ds(i * P + (0 if d == 0 else 8 * C), P), :]
                            sp.dma_start(y[:, k, d], src).then_inc(y_in, 16)
                    sp.dma_start(rp[:], s["rwpost"][i]).then_inc(post_in, 16)
                    sp.dma_start(gp[:], s["gdpost"][i]).then_inc(post_in, 16)
                    sp.wait_ge(out_ready, 1)
                    sp.dma_start(s["y"][bass.ds(i * P, P), GW:3 * GW].rearrange("p (k g) -> p k g", k=2), y[:, :, 0]).then_inc(stored, 16)
                    sp.wait_ge(stored, 16)

                @block.scalar
                def _(act):
                    act.wait_ge(var_ready, 1)
                    act.activation(r[:, 3, :], r[:, 2, :], ACT.Sqrt).then_inc(root_ready, 1)

                @block.vector
                def _(v):
                    link = chained(v, dve_step)
                    yb, yc = y[:, 0, 0], y[:, 1, 0]
                    v.wait_ge(y_in, 64)
                    link(v.tensor_tensor(y[:, :, 0], y[:, :, 0], y[:, :, 1], ALU.add))
                    link(v.tensor_reduce(r[:, 0, 0:HEADS], by_head(yb), X, ALU.add))
                    link(v.tensor_scalar(r[:, 0, 0:HEADS], r[:, 0, 0:HEADS], 1.0 / HD, None, ALU.mult))
                    link(v.tensor_tensor(by_head(yb), by_head(yb), head_bc(r[:, 0, 0:HEADS]), ALU.subtract))
                    link(v.tensor_tensor(sq[:], y[:, :, 0], y[:, :, 0], ALU.mult))
                    link(v.tensor_reduce(r[:, 1, :], sq[:].rearrange("p k (h e) -> p (k h) e", e=HD), X, ALU.add))
                    link(v.tensor_scalar(r[:, 2, 0:HEADS], r[:, 1, 0:HEADS], 1.0 / HD, GN_EPS, ALU.mult, ALU.add))
                    v.tensor_scalar(r[:, 2, HEADS:], r[:, 1, HEADS:], 1.0 / HD, NORM_EPS, ALU.mult, ALU.add).then_inc(var_ready, 1)
                    v.wait_ge(root_ready, 1)
                    link(v.reciprocal(r[:, 4, :], r[:, 3, :]))
                    link(v.tensor_tensor(y[:, :, 0].rearrange("p k (h e) -> p k h e", e=HD), y[:, :, 0].rearrange("p k (h e) -> p k h e", e=HD),
                                         r[:, 4, :].rearrange("p (k h) -> p k h", k=2).unsqueeze(3).to_broadcast([P, 2, HEADS, HD]), ALU.mult))
                    v.wait_ge(post_in, 32)
                    link(v.tensor_tensor(yb, yb, lg[:], ALU.mult))
                    link(v.tensor_tensor(yb, yb, lb[:], ALU.add))
                    link(v.tensor_tensor(yb, yb, rp[:, 0], ALU.add))
                    link(v.tensor_tensor(yb, yb, rp[:, 1], ALU.mult))
                    link(v.tensor_tensor(by_head(yc), by_head(yc), gg[:].unsqueeze(1).to_broadcast([P, HEADS, HD]), ALU.mult))
                    v.tensor_tensor(yc, yc, gp[:], ALU.mult).then_inc(out_ready, 1)


def post_norm(v, link, z, y, h, gate, g, b, stats, mv, var_ready, std_ready):
    link(v.tensor_tensor(z[:], y, gate, ALU.mult))
    link(v.scalar_tensor_tensor(z[:], h, ALPHA, z[:], ALU.mult, ALU.add))
    ln_first(v, link, z, stats, mv, var_ready)
    ln_last(v, link, z[:], z[:], mv, std_ready, 1)
    link(v.tensor_tensor(z[:], z[:], g[:], ALU.mult))
    return v.tensor_tensor(z[:], z[:], b[:], ALU.add)


def mix_stage(nc, l, t, s, consts):
    with ExitStack() as es:
        sb = lambda n, sh: es.enter_context(nc.sbuf_tensor("mx_" + n, sh, F32))
        w, g, b = sb("w", [P, KT, D]), sb("g", [P, D]), sb("b", [P, D])
        load_once(nc, [(w[:], t["w_out"][l].rearrange("(k p) n -> p k n", p=P)), (g[:], over_rows(t["ln_mix_g"][l])), (b[:], over_rows(t["ln_mix_b"][l]))])
        y, yT, h, gate, z = sb("y", [P, D]), sb("yT", [P, KT, P]), sb("h", [P, D]), sb("gate", [P, D]), sb("z", [P, D])
        stats, mv = sb("stats", [P, 2, 6]), sb("mv", [P, 8])
        ps = es.enter_context(nc.psum_tensor("mx_ps", [P, 4, 512], F32))
        with nc.Fori(l * CTX_TILES, TILES) as i:
            with stage(nc, "y_in", "h_in", "gate_in", "tr_done", "copied", "mm_done", "var_ready", "std_ready", "dve_step", "z_ready", "stored") as \
                    (block, y_in, h_in, gate_in, tr_done, copied, mm_done, var_ready, std_ready, dve_step, z_ready, stored):
                @block.sync
                def _(sp):
                    sp.dma_start(y[:], s["y"][bass.ds(i * P, P), :]).then_inc(y_in, 16)
                    sp.dma_start(h[:], s["h"][i]).then_inc(h_in, 16)
                    sp.dma_start(gate[:], over_rows(s["mods"][i, 2 * D:3 * D])).then_inc(gate_in, 16)
                    sp.wait_ge(z_ready, 1)
                    sp.dma_start(s["h"][i], z[:]).then_inc(stored, 16)
                    sp.wait_ge(stored, 16)

                @block.tensor
                def _(pe):
                    pe.wait_ge(y_in, 16)
                    for half in range(2):
                        for k in range(4):
                            kk = 4 * half + k
                            tr = pe.transpose(ps[:, half, k * P:(k + 1) * P], y[:, kk * P:(kk + 1) * P], consts["ident"][:])
                        tr.then_inc(tr_done, 1)
                    pe.wait_ge(copied, 2)
                    for half in range(2):
                        for k in range(KT):
                            mm = pe.matmul(ps[:, 2 + half, :], yT[:, k, :], w[:, k, half * 512:(half + 1) * 512], start=(k == 0), stop=(k == KT - 1))
                        mm.then_inc(mm_done, 1)

                @block.scalar
                def _(act):
                    for half in range(2):
                        act.wait_ge(tr_done, half + 1)
                        act.activation(yT[:, 4 * half:4 * half + 4, :].rearrange("p k n -> p (k n)"), ps[:, half], ACT.Copy).then_inc(copied, 1)
                    act.wait_ge(var_ready, 1)
                    act.activation(mv[:, 3:4], mv[:, 2:3], ACT.Sqrt).then_inc(std_ready, 1)

                @block.vector
                def _(v):
                    link = chained(v, dve_step)
                    v.wait_ge(h_in, 16)
                    v.wait_ge(gate_in, 16)
                    v.wait_ge(mm_done, 2)
                    post_norm(v, link, z, ps[:, 2:4].rearrange("p a b -> p (a b)"), h[:], gate[:], g, b, stats, mv, var_ready, std_ready).then_inc(z_ready, 1)


RING = 10
DIAGS = 32


def peer_stages(nc, l, t, s, consts):
    NS = 2 * PH
    with ExitStack() as es:
        sb = lambda n, sh, dt=F32: es.enter_context(nc.sbuf_tensor("pe_" + n, sh, dt))
        b = {"keys": sb("keys", [P, PH * 2 * PK]), "g": sb("g", [P, D]), "b": sb("b", [P, D]), "wq": sb("wq", [P, KT, PH * 2 * P]),
             "iota": sb("iota", [P, TOPK]), "tb": sb("tb", [P, D]), "slot": sb("slot", [P, SLOTS], U32), "gates": sb("gates", [P, SLOTS]),
             "m": sb("m", [P, 2, D]), "tbT": sb("tbT", [P, KT, P]), "qT": sb("qT", [P, 2, 4, P]), "sc": sb("sc", [P, NS, PK]),
             "sc2": sb("sc2", [P, TOPK * TOPK]), "stats": sb("stats", [P, 2, 6]), "mv": sb("mv", [P, 8]),
             "top": sb("top", [P, NS, TOPK]), "topi": sb("topi", [P, NS, TOPK], U32), "topf": sb("topf", [P, NS, TOPK]),
             "cand": sb("cand", [P, PH, TOPK, TOPK]), "best": sb("best", [P, PH, TOPK]), "pos": sb("pos", [P, PH, TOPK], U32),
             "posf": sb("posf", [P, 2, PH, TOPK]), "half": sb("half", [P, PH, TOPK], U32), "i0": sb("i0", [P, PH, TOPK]),
             "i1": sb("i1", [P, PH, TOPK]), "ex": sb("ex", [P, PH, TOPK]), "r8": sb("r8", [P, 2, PH])}
        ps = es.enter_context(nc.psum_tensor("ro_ps", [P, 8, 512], F32))
        load_once(nc, [(b["keys"][:], t["keys"][l]), (b["g"][:], over_rows(t["ln_ffn_g"][l])), (b["b"][:], over_rows(t["ln_ffn_b"][l])),
                       (b["wq"][:], t["peer_wq"][l].rearrange("(k p) n -> p k n", p=P)), (b["iota"][:], t["k_iota"])])
        with stage(nc, *ROUTE_SEMS) as (block, *rs):
            r = dict(zip(ROUTE_SEMS, rs))

            @block.sync
            def _(sp):
                route_loads(sp, l * CTX_TILES, s, b, r)

            @block.tensor
            def _(pe):
                for n in range(ROUTE_PE):
                    route_pe(pe, n, ps, b, consts, r)

            @block.scalar
            def _(act):
                for n in range(ROUTE_ACT):
                    route_act(act, n, ps, b, r)

            @block.vector
            def _(v):
                link = chained(v, r["dve_step"])
                for n in range(ROUTE_DVE):
                    route_dve(v, link, n, b, consts, r)
        with nc.Fori(l * CTX_TILES, TILES) as i:
            experts_stage(nc, i, t, s, b, ps, consts)


def experts_stage(nc, i, t, s, b, ps, consts):
    with ExitStack() as es:
        sb = lambda n, sh, dt=F32: es.enter_context(nc.sbuf_tensor("ex_" + n, sh, dt))
        ring, idx, gates, act_raw, wts = sb("ring", [P, RING, D]), sb("idx", [P, SLOTS], U32), sb("gates", [P, SLOTS]), sb("act", [P, SLOTS]), sb("wts", [P, SLOTS])
        y, z, diag = sb("y", [P, D]), sb("z", [P, D]), sb("diag", [P, DIAGS, P])
        stats, mv = sb("stats", [P, 2, 6]), sb("mv", [P, 8])
        names = ["idx_ready", "dots_done", "dve_used", "pe_used", "gelu_done", "w_ready", "diag_ready", "mm_done", "y_zero", "h_in", "gate_in", "z_free",
                 "n_var", "n_std", "z_ready", "stored"] + [f"row_in{k}" for k in range(RING)]
        with stage(nc, *names, *ROUTE_SEMS, pool_dmas=True) as (block, *sems):
            q = dict(zip(names + ROUTE_SEMS, sems))
            row_in = sems[16:16 + RING]
            half = SLOTS // 2

            @block.gpsimd
            def _(pool):
                pool.memset(y[:], 0.0).then_inc(q["y_zero"], 1)
                pool.wait_ge(q["idx_ready"], 1)
                for k in range(2 * SLOTS):
                    if k >= RING:
                        old = k - RING
                        if old < SLOTS:
                            pool.wait_ge(q["dots_done"], old + 1)
                        elif old % 2:
                            pool.wait_ge(q["pe_used"], (old - SLOTS) // 2 + 1)
                        else:
                            pool.wait_ge(q["dve_used"], (old - SLOTS) // 2 + 1)
                    table = t["peer_u"] if k < SLOTS else t["peer_v"]
                    col = k % SLOTS
                    pool.indirect_dma_start(ring[:, k % RING, :], None, table,
                                            bass.IndirectOffsetOnAxis(ap=idx[:, col:col + 1], axis=0)).then_inc(row_in[k % RING], 16)

            @block.sync
            def _(sp):
                sp.wait_ge(q["w_ready"], 1)
                route_loads(sp, i + 1, s, b, q)
                sp.wait_ge(q["route_m_free"], 1)
                sp.dma_start(b["m"][:, 0], over_rows(s["mods"][i, 5 * D:6 * D])).then_inc(q["gate_in"], 16)
                sp.dma_start(b["m"][:, 1], s["h"][i]).then_inc(q["h_in"], 16)
                sp.wait_ge(q["z_ready"], 1)
                sp.dma_start(s["h"][i], z[:]).then_inc(q["stored"], 16)
                sp.wait_ge(q["stored"], 16)

            @block.tensor
            def _(pe):
                for m in range(half):
                    k = SLOTS + 2 * m + 1
                    pe.wait_ge(q["diag_ready"], m + 1)
                    pe.wait_ge(row_in[k % RING], 16 * (k // RING + 1))
                    for c in range(2):
                        mm = pe.matmul(ps[:, 6 + c, :], diag[:, m % DIAGS, :], ring[:, k % RING, c * 512:(c + 1) * 512],
                                       start=(m == 0), stop=(m == half - 1))
                    mm.then_inc(q["pe_used"], 1)
                    if 3 <= m < 3 + ROUTE_PE:
                        route_pe(pe, m - 3, ps, b, consts, q)

            @block.scalar
            def _(act):
                act.wait_ge(q["dots_done"], SLOTS)
                act.activation(wts[:], act_raw[:], ACT.Gelu).then_inc(q["gelu_done"], 1)
                act.wait_ge(q["w_ready"], 1)

                def diags(first, last):
                    for m in range(first, last):
                        if m >= DIAGS:
                            act.wait_ge(q["pe_used"], m - DIAGS + 1)
                        act.activation(diag[:, m % DIAGS, :], consts["ident"][:], ACT.Copy, scale=wts[:, 2 * m + 1:2 * m + 2]).then_inc(q["diag_ready"], 1)

                diags(0, 8)
                for n in range(ROUTE_ACT):
                    if n == 1:
                        diags(8, DIAGS)
                    route_act(act, n, ps, b, q)
                    if n == ROUTE_ACT - 2:
                        diags(DIAGS, half)
                act.wait_ge(q["n_var"], 1)
                act.activation(mv[:, 3:4], mv[:, 2:3], ACT.Sqrt).then_inc(q["n_std"], 1)

            @block.vector
            def _(v):
                link = chained(v, q["dve_step"])
                v.tensor_copy(idx[:], b["slot"][:]).then_inc(q["idx_ready"], 1)
                link(v.tensor_copy(gates[:], b["gates"][:]))
                for k in range(SLOTS):
                    v.wait_ge(row_in[k % RING], 16 * (k // RING + 1))
                    if k >= 1:
                        v.wait_ge(q["dots_done"], k)
                    v.scalar_tensor_tensor(z[:], ring[:, k % RING, :], 1.0, b["tb"][:], ALU.mult, ALU.mult,
                                           accum_out=act_raw[:, k:k + 1]).then_inc(q["dots_done"], 1)
                v.wait_ge(q["gelu_done"], 1)
                v.tensor_tensor(wts[:], wts[:], gates[:], ALU.mult).then_inc(q["w_ready"], 1)
                v.wait_ge(q["w_ready"], 1)
                v.wait_ge(q["y_zero"], 1)
                n = 0
                for m in range(half):
                    k = SLOTS + 2 * m
                    v.wait_ge(row_in[k % RING], 16 * (k // RING + 1))
                    if m >= 1:
                        v.wait_ge(q["dve_used"], m)
                    v.scalar_tensor_tensor(y[:], ring[:, k % RING, :], wts[:, 2 * m:2 * m + 1], y[:], ALU.mult, ALU.add).then_inc(q["dve_used"], 1)
                    if m == 1 or (m >= DVE_FROM and n < ROUTE_DVE):
                        route_dve(v, link, n, b, consts, q)
                        n += 1
                assert n == ROUTE_DVE
                v.wait_ge(q["pe_used"], half)
                v.wait_ge(q["dve_used"], half)
                link(v.tensor_tensor(y[:], y[:], ps[:, 6:8].rearrange("p a b -> p (a b)"), ALU.add))
                v.wait_ge(q["gate_in"], 16)
                v.wait_ge(q["h_in"], 16)
                post_norm(v, link, z, y[:], b["m"][:, 1], b["m"][:, 0], b["g"], b["b"], stats, mv, q["n_var"], q["n_std"]).then_inc(q["z_ready"], 1)


ROUTE_SEMS = ["route_h_in", "route_m_in", "route_m_free", "route_var", "route_std", "tb_ready", "tr_done", "tbT_ready", "q_done", "q_ready",
              "s_done", "s_ready", "gap_ready", "exp_ready", "dve_step"]
ROUTE_PE = 10
ROUTE_ACT = 12
ROUTE_DVE = 27
DVE_FROM = 25


def route_loads(sp, i, s, b, q):
    sp.dma_start(b["tb"][:], s["h"][i]).then_inc(q["route_h_in"], 16)
    sp.dma_start(b["m"][:], over_rows(s["mods"][i, 3 * D:5 * D]).rearrange("p (a n) -> p a n", a=2)).then_inc(q["route_m_in"], 16)


def route_pe(pe, n, ps, b, consts, q):
    if n < 2:
        pe.wait_ge(q["tb_ready"], 1)
        for k in range(4):
            kk = 4 * n + k
            tr = pe.transpose(ps[:, n, k * P:(k + 1) * P], b["tb"][:, kk * P:(kk + 1) * P], consts["ident"][:])
        tr.then_inc(q["tr_done"], 1)
        return
    part, g = (n - 2) % 2, (n - 2) // 2
    if part == 0:
        pe.wait_ge(q["tbT_ready"], 2)
        if g >= 2:
            pe.wait_ge(q["q_ready"], g - 1)
        for x in range(4):
            hp = 4 * g + x
            for k in range(KT):
                mm = pe.matmul(ps[:, 2 + g % 2, x * P:(x + 1) * P], b["wq"][:, k, hp * P:(hp + 1) * P], b["tbT"][:, k, :], start=(k == 0), stop=(k == KT - 1))
        mm.then_inc(q["q_done"], 1)
    else:
        pe.wait_ge(q["q_ready"], g + 1)
        if g >= 2:
            pe.wait_ge(q["s_ready"], g - 1)
        for x in range(4):
            hp = 4 * g + x
            mm = pe.matmul(ps[:, 4 + g % 2, x * P:(x + 1) * P], b["qT"][:, g % 2, x, :], b["keys"][:, hp * PK:(hp + 1) * PK], start=True, stop=True)
        mm.then_inc(q["s_done"], 1)


def route_act(act, n, ps, b, q):
    if n == 0:
        act.wait_ge(q["route_var"], 1)
        act.activation(b["mv"][:, 3:4], b["mv"][:, 2:3], ACT.Sqrt).then_inc(q["route_std"], 1)
    elif n <= 2:
        act.wait_ge(q["tr_done"], n)
        act.activation(b["tbT"][:, 4 * n - 4:4 * n, :].rearrange("p k n -> p (k n)"), ps[:, n - 1], ACT.Copy).then_inc(q["tbT_ready"], 1)
    elif n <= 10:
        part, g = (n - 3) % 2, (n - 3) // 2
        if part == 0:
            act.wait_ge(q["q_done"], g + 1)
            if g >= 2:
                act.wait_ge(q["s_done"], g - 1)
            act.activation(b["qT"][:, g % 2].rearrange("p k n -> p (k n)"), ps[:, 2 + g % 2], ACT.Copy).then_inc(q["q_ready"], 1)
        else:
            act.wait_ge(q["s_done"], g + 1)
            act.activation(b["sc"][:, 4 * g:4 * g + 4, :].rearrange("p k n -> p (k n)"), ps[:, 4 + g % 2], ACT.Copy).then_inc(q["s_ready"], 1)
    else:
        act.wait_ge(q["gap_ready"], 1)
        act.activation(b["ex"][:], b["best"][:], ACT.Exp).then_inc(q["exp_ready"], 1)


def top16(v, link, src, spare, vals, inds):
    link(v.max(vals[:, 0:8], src))
    link(v.max_index(inds[:, 0:8], vals[:, 0:8], src))
    link(v.match_replace(out=spare, in_to_replace=vals[:, 0:8], in_values=src, imm_value=-3e38))
    link(v.max(vals[:, 8:16], spare))
    link(v.max_index(inds[:, 8:16], vals[:, 8:16], spare))


def route_dve(v, link, n, b, consts, q):
    tb, m, stats, mv = b["tb"], b["m"], b["stats"], b["mv"]
    halves = lambda x: x[:].rearrange("p (h two) k -> p h two k", two=2)
    if n == 0:
        v.wait_ge(q["route_h_in"], 16)
        ln_first(v, link, tb, stats, mv, q["route_var"])
        ln_last(v, link, tb[:], tb[:], mv, q["route_std"], 1)
        v.wait_ge(q["route_m_in"], 16)
        link(v.tensor_tensor(tb[:], tb[:], m[:, 1, :], ALU.mult))
        link(v.tensor_tensor(tb[:], tb[:], m[:, 0, :], ALU.add))
        v.sem_inc(q["tb_ready"], 1)
        v.sem_inc(q["route_m_free"], 1)
    elif n <= 16:
        v.wait_ge(q["s_ready"], (n - 1) // 4 + 1)
        top16(v, link, b["sc"][:, n - 1, :], b["sc2"][:, 0:PK], b["top"][:, n - 1, :], b["topi"][:, n - 1, :])
    elif n == 17:
        link(v.tensor_tensor(b["cand"][:], halves(b["top"])[:, :, 0].unsqueeze(3).to_broadcast([P, PH, TOPK, TOPK]),
                             halves(b["top"])[:, :, 1].unsqueeze(2).to_broadcast([P, PH, TOPK, TOPK]), ALU.add))
    elif n <= 25:
        h = n - 18
        top16(v, link, b["cand"][:, h].rearrange("p a b -> p (a b)"), b["sc2"][:], b["best"][:, h, :], b["pos"][:, h, :])
    else:
        best, ex, r8 = b["best"], b["ex"], b["r8"]
        link(v.tensor_copy(r8[:, 0, :], best[:, :, 0]))
        v.tensor_tensor(best[:], best[:], r8[:, 0, :].unsqueeze(2).to_broadcast([P, PH, TOPK]), ALU.subtract).then_inc(q["gap_ready"], 1)
        for x, (op, by) in enumerate(((ALU.logical_shift_right, 4), (ALU.bitwise_and, 15))):
            link(v.tensor_scalar(b["half"][:], b["pos"][:], by, None, op))
            link(v.tensor_copy(b["posf"][:, x], b["half"][:]))
        link(v.tensor_copy(b["topf"][:], b["topi"][:]))
        eq = b["cand"][:].rearrange("p h k n -> p (h k) n")
        for out, x in ((b["i0"], 0), (b["i1"], 1)):
            at = b["posf"][:, x].rearrange("p h k -> p (h k)").unsqueeze(2).to_broadcast([P, SLOTS, TOPK])
            link(v.tensor_tensor(eq, at, b["iota"][:].unsqueeze(1).to_broadcast([P, SLOTS, TOPK]), ALU.is_equal))
            link(v.tensor_tensor(b["cand"][:], b["cand"][:], halves(b["topf"])[:, :, x].unsqueeze(2).to_broadcast([P, PH, TOPK, TOPK]), ALU.mult))
            link(v.tensor_reduce(out[:].rearrange("p h k -> p (h k)"), eq, X, ALU.add))
        link(v.scalar_tensor_tensor(b["i0"][:], b["i0"][:], float(PK), b["i1"][:], ALU.mult, ALU.add))
        link(v.tensor_scalar(b["i0"][:], b["i0"][:], consts["layer"][:, 2:3], None, ALU.add))
        link(v.tensor_copy(b["slot"][:], b["i0"][:].rearrange("p h k -> p (h k)")))
        v.wait_ge(q["exp_ready"], 1)
        link(v.tensor_reduce(r8[:, 0, :], ex[:], X, ALU.add))
        link(v.reciprocal(r8[:, 1, :], r8[:, 0, :]))
        link(v.tensor_tensor(b["gates"][:].rearrange("p (h k) -> p h k", h=PH), ex[:], r8[:, 1, :].unsqueeze(2).to_broadcast([P, PH, TOPK]), ALU.mult))


def load_once(nc, pairs):
    with stage(nc, "once_in") as (block, once_in):
        @block.sync
        def _(sp):
            for dst, src in pairs:
                sp.dma_start(dst, src).then_inc(once_in, 16)
            sp.wait_ge(once_in, 16 * len(pairs))


def build(nc, t, out, upto=99):
    with ExitStack() as es:
        dram = lambda n, s: nc.dram_tensor(n, s, F32, kind="Internal").ap()
        s = {
            "h": dram("h_dram", (TILES + 1, P, D)),
            "mods": dram("mods_dram", (TILES + 1, 6 * D)),
            "p": dram("p_dram", (TOK + 2, IN_COLS)),
            "y": dram("y_dram", (TOK, D)),
            "rw": dram("rw_dram", (2 * TILES, 2, 2, 2, C, 5, 2, HD)),
            "rwdec": dram("rwdec_dram", (2 * TILES * 2, 2, GW)),
            "rwpost": dram("rwpost_dram", (TILES, P, 2, GW)),
            "gd": dram("gd_dram", (2 * TILES, 2, 2, 2, C, 7, 2, HD)),
            "gdcol": dram("gdcol_dram", (2 * TILES * 2, 2, 2, C, HEADS)),
            "gdpost": dram("gdpost_dram", (TILES, P, GW)),
            "scan": dram("scan_dram", (2, 2, 24, C, GW)),
        }
        consts = {}
        for name, key in (("ident", "k_ident"), ("sums", "k_sums"), ("rows", "k_rows")):
            ap = t[key]
            consts[name] = es.enter_context(nc.sbuf_tensor("c_" + name, list(ap.shape), F32))
        layer = es.enter_context(nc.sbuf_tensor("c_layer", [P, 4], F32))
        consts["layer"] = layer
        load_once(nc, [(consts["ident"][:], t["k_ident"]), (consts["sums"][:], t["k_sums"]), (consts["rows"][:], t["k_rows"]),
                       (s["h"][0:CTX_TILES].rearrange("i p n -> (i p) n"), t["ctx"]),
                       (s["h"][CTX_TILES:TILES].rearrange("i p n -> (i p) n"), t["x"]),
                       (s["h"][TILES], t["x"][0:P]),
                       (s["p"][0:1, :], t["k_zero"][0:1, :]), (s["p"][TOK + 1:TOK + 2, :], t["k_zero"][1:2, :])])
        with nc.Fori(0, DEPTH) as l:
            load_once(nc, [(layer[:], t["k_layer"][l])])
            ada_stage(nc, l, t, s["mods"], consts)
            with nc.sbuf_tensor("uT", [P, KT, TOK], F32) as uT:
                norm_stage(nc, l, t, s["h"], s["mods"], consts, uT)
                project_stage(nc, l, t, s["p"], uT)
            if upto >= 2:
                attention_stages(nc, l, t, s, consts)
            if upto >= 3:
                scan_stages(nc, l, t, s, consts)
            if upto >= 5:
                mix_stage(nc, l, t, s, consts)
            if upto >= 6:
                peer_stages(nc, l, t, s, consts)
        load_once(nc, [(out, s["h"][CTX_TILES:TILES].rearrange("i p n -> (i p) n"))])


def laid_out(inputs):
    a = {k: np.asarray(v) for k, v in inputs.items()}
    r = {n: a[n] for n in ("w_ada", "b_ada", "w_in", "w_out", "ln_mix_g", "ln_mix_b", "ln_ffn_g", "ln_ffn_b", "diff_norm_g",
                           "rwkv_mu", "rwkv_kk", "rwkv_ka", "rwkv_ln_g", "rwkv_ln_b", "rwkv_g2", "gdn_conv", "gdn_norm_g",
                           "peer_wq")}
    r["x"] = a["x"].reshape(SEQ, D)
    r["ctx"] = a["ctx"].reshape(CTX, D)
    r["cond"] = np.ascontiguousarray(np.stack([a["c"][0], a["c_ctx"]]).reshape(2, KT, P).transpose(2, 1, 0))
    r["diff_lam"] = a["diff_lam"].reshape(DEPTH, -1)
    r["rwkv_w0"] = a["rwkv_w0"].reshape(DEPTH, -1)
    r["rwkv_a0"] = a["rwkv_a0"].reshape(DEPTH, -1)
    r["rwkv_w2"] = a["rwkv_w2"]
    r["rwkv_a2"] = a["rwkv_a2"]
    r["rwkv_rk"] = a["rwkv_rk"].reshape(DEPTH, -1)
    r["gdn_a_log"] = a["gdn_a_log"].reshape(DEPTH, -1)
    r["gdn_dt_bias"] = a["gdn_dt_bias"].reshape(DEPTH, -1)
    r["bias"] = window_bias(a["nat_rpb"])
    r["keys"] = np.ascontiguousarray(a["peer_keys"].transpose(0, 4, 1, 2, 3).reshape(DEPTH, P, PH * 2 * PK))
    r["peer_u"] = a["peer_u"].reshape(DEPTH * EXPERTS, D)
    r["peer_v"] = a["peer_v"].reshape(DEPTH * EXPERTS, D)
    r.update(constants())
    return {"in_" + k: np.ascontiguousarray(v) for k, v in r.items()}


def kernel(**inputs):
    import concourse.bacc as bacc
    from concourse.bass_utils import run_bass_kernel_spmd

    nc = bacc.Bacc("TRN2", target_bir_lowering=False, num_devices=1)
    arrays = laid_out(inputs)
    t = {}
    for name, a in arrays.items():
        t[name[3:]] = nc.dram_tensor(name, a.shape, mybir.dt.from_np(a.dtype), kind="ExternalInput").ap()
    out = nc.dram_tensor("out", (SEQ, D), F32, kind="ExternalOutput").ap()
    build(nc, t, out)
    r = run_bass_kernel_spmd(nc, [arrays], core_ids=[0])
    return r.results[0]["out"].reshape(1, SEQ, D)
```

```python
from contextlib import ExitStack, contextmanager

import numpy as np

import concourse.bass as bass
import concourse.mybir as mybir

F32 = mybir.dt.float32
U32 = mybir.dt.uint32
ALU = mybir.AluOpType
ACT = mybir.ActivationFunctionType
X = mybir.AxisListType.X
P = 128

D = 1024
SEQ = 512
CTX = 256
TOK = CTX + SEQ
TILES = TOK // P
CTX_TILES = CTX // P
DEPTH = 2
GRID_W = 64
HD = 64
HEADS = 4
GW = HEADS * HD
ATTN_COLS = 3 * GW
LORA = 64
RWKV_COLS = 3 * GW + 4 * LORA + 128
GDN_QKV = 3 * GW
GDN_COLS = 4 * GW + 4 * HEADS
IN_COLS = ATTN_COLS + RWKV_COLS + GDN_COLS + ATTN_COLS
COL_A = 0
COL_B = ATTN_COLS
COL_C = COL_B + RWKV_COLS
COL_D = COL_C + GDN_COLS
KT = D // P
WCHUNK = 466
NCHUNKS = IN_COLS // WCHUNK
WIN_H, WIN_W = 8, 16
C = 64
CHUNKS = TOK // C
CTX_CHUNKS = CTX // C
LEVELS = (1, 2, 4, 8, 16, 32)
PH, PK, TOPK = 8, 128, 16
EXPERTS = PK * PK
SLOTS = PH * TOPK
ALPHA = (2 * DEPTH) ** 0.25
LN_EPS = 1e-5
GN_EPS = 64e-5
NORM_EPS = 1e-6
NEG = -1e30
DECAY = -float(np.exp(-0.5))


def constants():
    c = {}
    i = np.arange(P)
    same = (i[:, None] // C) == (i[None, :] // C)
    low = i[:, None] >= i[None, :]
    c["k_sums"] = np.stack([same & low.T, same & low, same]).astype(np.float32).transpose(1, 0, 2)
    c["k_ident"] = np.eye(P, dtype=np.float32)
    strict = same & (i[:, None] > i[None, :])
    both = lambda m: np.stack([m.T, m])
    blocks = lambda m: np.concatenate([m[:, b * C:(b + 1) * C, b * C:(b + 1) * C] for b in range(2)], axis=1)
    c["k_near"] = np.stack([blocks(both(strict)), blocks(both(same & low))]).transpose(2, 0, 1, 3).astype(np.float32).copy()
    joins = [both(((i[:, None] // (2 * s)) == (i[None, :] // (2 * s))) & ((i[:, None] // s) > (i[None, :] // s))) for s in LEVELS]
    c["k_joins"] = np.stack(joins).transpose(2, 0, 1, 3).astype(np.float32).copy()
    c["k_rows"] = np.stack([(i // 64 == 0), (i // 64 == 1)] + [(i // 32 == g) for g in range(4)]).T.astype(np.float32).copy()
    e = np.ones((TILES, P, 2), np.float32)
    e[0, 0, 0] = e[CTX_TILES, 0, 0] = 0
    e[CTX_TILES - 1, P - 1, 1] = e[TILES - 1, P - 1, 1] = 0
    c["k_edges"] = e
    t = np.arange(SEQ)
    inv = (10000.0 ** (-np.arange(8, dtype=np.float32) / 8)).astype(np.float32)
    rope = np.zeros((2, TOK, HD), np.float32)
    rope[0] = 1
    for part, pos in ((0, t // GRID_W), (1, t % GRID_W)):
        ang = pos.astype(np.float32)[:, None] * inv
        for half in (0, 1):
            o = 32 * half + 16 * part
            rope[0, CTX:, o:o + 8] = rope[0, CTX:, o + 8:o + 16] = np.cos(ang)
            rope[1, CTX:, o:o + 8] = -np.sin(ang)
            rope[1, CTX:, o + 8:o + 16] = np.sin(ang)
    rope = np.broadcast_to(rope.reshape(2, TILES, P, 1, HD), (2, TILES, P, 8, HD))
    c["k_rope"] = np.ascontiguousarray(rope.transpose(1, 2, 0, 3, 4))
    c["k_iota"] = np.broadcast_to(np.arange(TOPK, dtype=np.float32), (P, TOPK)).copy()
    c["k_zero"] = np.zeros((2, IN_COLS), np.float32)
    lam = [0.8 - 0.6 * float(np.exp(-0.3 * l)) for l in range(DEPTH)]
    c["k_layer"] = np.stack([np.broadcast_to(np.array([lam[l], 1.0 - lam[l], l * EXPERTS, 0.0], np.float32), (P, 4))
                             for l in range(DEPTH)]).copy()
    return c


def window_bias(rpb):
    q = np.arange(SEQ)
    r, cq = q // GRID_W, q % GRID_W
    start = np.clip(cq - WIN_W // 2, 0, GRID_W - WIN_W)
    ok = (cq[None, :] >= start[:, None]) & (cq[None, :] < start[:, None] + WIN_W)
    dr = r[None, :] - r[:, None] + WIN_H - 1
    dc = np.clip(cq[None, :] - cq[:, None], -(WIN_W - 1), WIN_W - 1) + WIN_W - 1
    laid = np.asarray(rpb)[:, :, dr, dc]
    laid = np.where(ok[None, None], laid, np.float32(NEG)).astype(np.float32)
    return np.ascontiguousarray(laid.reshape(DEPTH, HEADS, SEQ // P, P, SEQ).transpose(0, 2, 3, 1, 4))


@contextmanager
def stage(nc, *names, pool_dmas=False):
    with ExitStack() as es:
        sems = [es.enter_context(nc.semaphore(n)) for n in names]
        with nc.Block() as block:
            yield (block, *sems)
        with nc.Block() as clear:
            if pool_dmas:
                @clear.gpsimd
                def _(pool):
                    pool.dma_reset()
                    for s in sems:
                        pool.sem_clear(s)
            else:
                @clear.sync
                def _(sp):
                    for s in sems:
                        sp.sem_clear(s)


def chained(eng, sem):
    count = [0]

    def link(ins):
        count[0] += 1
        ins.then_inc(sem, 1)
        eng.wait_ge(sem, count[0])
        return ins

    return link


def over_rows(row, *shape):
    return row.unsqueeze(0).to_broadcast([P] + list(row.shape))


def ln_first(v, link, x, stats, mv, var_ready):
    for k in range(2):
        link(v.bn_stats(stats[:, k, :], x[:, k * 512:(k + 1) * 512]))
    link(v.bn_aggr(mv[:, 0:2], stats[:, :, :].rearrange("p a b -> p (a b)")))
    v.tensor_scalar(mv[:, 2:3], mv[:, 1:2], LN_EPS, None, ALU.add).then_inc(var_ready, 1)


def ln_last(v, link, out, x, mv, std_ready, n):
    v.wait_ge(std_ready, n)
    link(v.reciprocal(mv[:, 4:5], mv[:, 3:4]))
    link(v.tensor_scalar(out, x, mv[:, 0:1], mv[:, 4:5], ALU.subtract, ALU.mult))


def ada_stage(nc, l, t, mods, consts):
    n_chunks, bufs = 6 * D // 512, 4
    with ExitStack() as es:
        cc = es.enter_context(nc.sbuf_tensor("cond", [P, KT, 2], F32))
        sc = es.enter_context(nc.sbuf_tensor("cond_silu", [P, KT, 2], F32))
        w = es.enter_context(nc.sbuf_tensor("ada_w", [P, bufs, KT, 512], F32))
        b = es.enter_context(nc.sbuf_tensor("ada_b", [2, 6 * D], F32))
        row = es.enter_context(nc.sbuf_tensor("ada_rows", [2, 6 * D], F32))
        ps = es.enter_context(nc.psum_tensor("ada_ps", [2, 2, 512], F32))
        wait = es.enter_context(stage(nc, "cond_in", "bias_in", "silu_done", "chunk_done", "row_done", "rows_out",
                                      "dve_step", *[f"w_in{k}" for k in range(bufs)]))
        block, cond_in, bias_in, silu_done, chunk_done, row_done, rows_out, dve_step, *w_in = wait
        wv = t["w_ada"][l].rearrange("(k p) n -> p k n", p=P)

        @block.sync
        def _(sp):
            sp.dma_start(cc[:], t["cond"]).then_inc(cond_in, 16)
            sp.dma_start(b[:], t["b_ada"][l].unsqueeze(0).to_broadcast([2, 6 * D])).then_inc(bias_in, 16)
            for n in range(n_chunks):
                if n >= bufs:
                    sp.wait_ge(chunk_done, n - bufs + 1)
                sp.dma_start(w[:, n % bufs], wv[:, :, n * 512:(n + 1) * 512]).then_inc(w_in[n % bufs], 16)
            sp.wait_ge(row_done, n_chunks)
            for i in range(TILES + 1):
                r = 1 if i < CTX_TILES else 0
                sp.dma_start(mods[i:i + 1, :], row[r:r + 1, :]).then_inc(rows_out, 16)
            sp.wait_ge(rows_out, 16 * (TILES + 1))

        @block.scalar
        def _(act):
            act.wait_ge(cond_in, 16)
            act.activation(sc[:], cc[:], ACT.Silu).then_inc(silu_done, 1)

        @block.tensor
        def _(pe):
            pe.wait_ge(silu_done, 1)
            for n in range(n_chunks):
                pe.wait_ge(w_in[n % bufs], 16 * (n // bufs + 1))
                if n >= 2:
                    pe.wait_ge(row_done, n - 1)
                for k in range(KT):
                    mm = pe.matmul(ps[:, n % 2, :], sc[:, k, :], w[:, n % bufs, k, :], start=(k == 0), stop=(k == KT - 1))
                mm.then_inc(chunk_done, 1)

        @block.vector
        def _(v):
            v.wait_ge(bias_in, 16)
            for n in range(n_chunks):
                cols = slice(n * 512, (n + 1) * 512)
                v.wait_ge(chunk_done, n + 1)
                one = 1.0 if n // 2 in (1, 4) else 0.0
                v.scalar_tensor_tensor(row[:, cols], ps[:, n % 2, :], one, b[:, cols], ALU.add, ALU.add).then_inc(row_done, 1)


def norm_stage(nc, l, t, h_dram, mods, consts, uT):
    with ExitStack() as es:
        sb = lambda n, sh: es.enter_context(nc.sbuf_tensor("n_" + n, sh, F32))
        h, m = [sb(f"h{u}", [P, D]) for u in range(2)], sb("mod", [P, 2, D])
        stats, mv = [sb(f"stats{u}", [P, 2, 6]) for u in range(2)], [sb(f"mv{u}", [P, 8]) for u in range(2)]
        ps = es.enter_context(nc.psum_tensor("n_ps", [P, 4, 4, P], F32))
        with nc.Fori(0, TILES // 2) as pair:
            i = pair * 2
            with stage(nc, "h0_in", "h1_in", "mod_in", "var_ready", "std_ready", "dve_step", "u_ready", "tr_done", "copied") as \
                    (block, h0_in, h1_in, mod_in, var_ready, std_ready, dve_step, u_ready, tr_done, copied):

                @block.sync
                def _(sp):
                    for u, sem in enumerate((h0_in, h1_in)):
                        sp.dma_start(h[u][:], h_dram[i + u]).then_inc(sem, 16)
                        if u == 0:
                            sp.dma_start(m[:], over_rows(mods[i, 0:2 * D]).rearrange("p (a n) -> p a n", a=2)).then_inc(mod_in, 16)

                @block.vector
                def _(v):
                    link = chained(v, dve_step)
                    for u, sem in enumerate((h0_in, h1_in)):
                        v.wait_ge(sem, 16)
                        ln_first(v, link, h[u], stats[u], mv[u], var_ready)
                    v.wait_ge(mod_in, 16)
                    for u in range(2):
                        ln_last(v, link, h[u][:], h[u][:], mv[u], std_ready, u + 1)
                        link(v.tensor_tensor(h[u][:], h[u][:], m[:, 1, :], ALU.mult))
                        v.tensor_tensor(h[u][:], h[u][:], m[:, 0, :], ALU.add).then_inc(u_ready, 1)

                @block.scalar
                def _(act):
                    for u in range(2):
                        act.wait_ge(var_ready, u + 1)
                        act.activation(mv[u][:, 3:4], mv[u][:, 2:3], ACT.Sqrt).then_inc(std_ready, 1)
                    for u in range(2):
                        for half in range(2):
                            act.wait_ge(tr_done, 2 * u + half + 1)
                            act.activation(uT[:, 4 * half:4 * half + 4, bass.ds((i + u) * P, P)], ps[:, 2 * u + half], ACT.Copy).then_inc(copied, 1)

                @block.tensor
                def _(pe):
                    for u in range(2):
                        pe.wait_ge(u_ready, u + 1)
                        for half in range(2):
                            for k in range(4):
                                kk = 4 * half + k
                                tr = pe.transpose(ps[:, 2 * u + half, k, :], h[u][:, kk * P:(kk + 1) * P], consts["ident"][:])
                            tr.then_inc(tr_done, 1)


def project_stage(nc, l, t, p_dram, uT, w):
    with ExitStack() as es:
        o = es.enter_context(nc.sbuf_tensor("p_out", [P, 4, WCHUNK], F32))
        ps = es.enter_context(nc.psum_tensor("p_ps", [P, 4, 512], F32))
        wv = t["w_in"][l].rearrange("(k p) n -> p k n", p=P)
        with nc.Fori(0, NCHUNKS // 2) as j:
            with stage(nc, "w0_in", "w1_in", "mm_done", "out_ready", "gone0", "gone1", "gone2", "gone3") as \
                    (block, w0_in, w1_in, mm_done, out_ready, *gone):

                @block.sync
                def _(sp):
                    sp.dma_start(w[:, 1], wv[:, :, bass.ds(j * 2 * WCHUNK + WCHUNK, WCHUNK)]).then_inc(w1_in, 16)
                    sp.wait_ge(mm_done, TILES)
                    nxt = sp.snap((j + 1) % (NCHUNKS // 2))
                    sp.dma_start(w[:, 0], wv[:, :, bass.ds(nxt * 2 * WCHUNK, WCHUNK)]).then_inc(w0_in, 16)
                    sp.wait_ge(w0_in, 16)

                @block.tensor
                def _(pe):
                    for q in range(2 * TILES):
                        ch, i = q // TILES, q % TILES
                        if q == TILES:
                            pe.wait_ge(w1_in, 16)
                        if q >= 4:
                            pe.wait_ge(out_ready, q - 3)
                        for k in range(KT):
                            mm = pe.matmul(ps[:, q % 4, 0:WCHUNK], uT[:, k, i * P:(i + 1) * P], w[:, ch, k, :],
                                           start=(k == 0), stop=(k == KT - 1))
                        mm.then_inc(mm_done, 1)

                @block.vector
                def _(v):
                    for q in range(2 * TILES):
                        v.wait_ge(mm_done, q + 1)
                        if q >= 4:
                            v.wait_ge(gone[q % 4], 16 * (q // 4))
                        v.tensor_copy(o[:, q % 4, :], ps[:, q % 4, 0:WCHUNK]).then_inc(out_ready, 1)

                @block.scalar
                def _(act):
                    for q in range(2 * TILES):
                        ch, i = q // TILES, q % TILES
                        act.wait_ge(out_ready, q + 1)
                        dst = p_dram[1 + i * P:1 + (i + 1) * P, bass.ds(j * 2 * WCHUNK + ch * WCHUNK, WCHUNK)]
                        act.dma_start(dst, o[:, q % 4, :]).then_inc(gone[q % 4], 16)
                    for g in gone:
                        act.wait_ge(g, 16 * 2 * TILES // 4)


def attention_stages(nc, l, t, s, consts):
    with ExitStack() as es:
        sb = lambda n, sh: es.enter_context(nc.sbuf_tensor(n, sh, F32))
        b = {"qA": sb("at_qA", [P, 2, TOK]), "kA": sb("at_kA", [P, 2, TOK]), "qD": sb("at_qD", [P, 2, TOK]),
             "kD": sb("at_kD", [P, 2, TOK]), "vA": sb("at_vA", [P, TILES, GW]), "vD": sb("at_vD", [P, TILES, GW]),
             "lam": sb("at_lam", [P, 8]), "g": sb("at_g", [P, HD])}
        v_src = lambda col: s["p"][1:1 + TOK, col + 2 * GW:col + 3 * GW].rearrange("(i p) n -> p i n", p=P)
        load_once(nc, [(b["vA"][:], v_src(COL_A)), (b["vD"][:], v_src(COL_D))])
        lambda_stage(nc, l, t, b, consts)
        qk_stage(nc, t, s, b, consts)
        attend_stage(nc, s, b, consts, "A", CTX_TILES, TILES, TILES, None)
        attend_stage(nc, s, b, consts, "A", 0, CTX_TILES, CTX_TILES, None)
        attend_stage(nc, s, b, consts, "D", CTX_TILES, TILES, TILES, t["bias"][l])
        attend_stage(nc, s, b, consts, "D", 0, CTX_TILES, CTX_TILES, None)


def lambda_stage(nc, l, t, b, consts):
    with ExitStack() as es:
        lv = es.enter_context(nc.sbuf_tensor("lv", [P, 4, 32], F32))
        pr = es.enter_context(nc.sbuf_tensor("lv_prod", [P, 2, 32], F32))
        lam = b["lam"]
        with stage(nc, "lv_in", "g_in", "dots_ready", "exps_ready", "dve_step") as (block, lv_in, g_in, dots_ready, exps_ready, dve_step):
            @block.sync
            def _(sp):
                sp.dma_start(lv[:].rearrange("p a b -> p (a b)"), over_rows(t["diff_lam"][l])).then_inc(lv_in, 16)
                sp.dma_start(b["g"][:], over_rows(t["diff_norm_g"][l])).then_inc(g_in, 16)

            @block.vector
            def _(v):
                link = chained(v, dve_step)
                v.wait_ge(lv_in, 16)
                for k in range(2):
                    link(v.tensor_tensor(pr[:, k, :], lv[:, 2 * k, :], lv[:, 2 * k + 1, :], ALU.mult))
                v.tensor_reduce(lam[:, 2:4], pr[:], X, ALU.add).then_inc(dots_ready, 1)
                v.wait_ge(exps_ready, 1)
                link(v.tensor_tensor(lam[:, 6:7], lam[:, 4:5], lam[:, 5:6], ALU.subtract))
                link(v.tensor_tensor(lam[:, 0:1], lam[:, 6:7], consts["layer"][:, 0:1], ALU.add))
                v.wait_ge(g_in, 16)
                link(v.tensor_scalar(b["g"][:], b["g"][:], consts["layer"][:, 1:2], None, ALU.mult))

            @block.scalar
            def _(act):
                act.wait_ge(dots_ready, 1)
                act.activation(lam[:, 4:6], lam[:, 2:4], ACT.Exp).then_inc(exps_ready, 1)


def qk_stage(nc, t, s, b, consts):
    with ExitStack() as es:
        sb = lambda n, sh: es.enter_context(nc.sbuf_tensor(n, sh, F32))
        a, d, tab, rot, t2 = sb("qk_a", [P, 512]), sb("qk_d", [P, 512]), sb("qk_tab", [P, 2, 512]), sb("qk_rot", [P, 512]), sb("qk_t2", [P, 512])
        ps = es.enter_context(nc.psum_tensor("qk_ps", [P, 2, 4, P], F32))
        pairs = lambda x: x.rearrange("p (g two e) -> p g two e", two=2, e=8)
        with nc.Fori(0, TILES) as i:
            with stage(nc, "a_in", "d_in", "tab_in", "dve_step", "rot_ready", "tr_done", "copied") as \
                    (block, a_in, d_in, tab_in, dve_step, rot_ready, tr_done, copied):
                @block.sync
                def _(sp):
                    rows = bass.ds(i * P + 1, P)
                    sp.dma_start(a[:], s["p"][rows, COL_A:COL_A + 512]).then_inc(a_in, 16)
                    sp.dma_start(tab[:], t["k_rope"][i].rearrange("p a h e -> p a (h e)")).then_inc(tab_in, 16)
                    sp.dma_start(d[:], s["p"][rows, COL_D:COL_D + 512]).then_inc(d_in, 16)

                @block.vector
                def _(v):
                    link = chained(v, dve_step)
                    v.wait_ge(a_in, 16)
                    v.wait_ge(tab_in, 16)
                    v.tensor_tensor(rot[:], a[:], tab[:, 0], ALU.mult)
                    for x in range(2):
                        mul = v.tensor_tensor(pairs(t2[:])[:, :, x], pairs(a[:])[:, :, 1 - x], pairs(tab[:, 1])[:, :, x], ALU.mult)
                    link(mul)
                    v.tensor_tensor(rot[:], rot[:], t2[:], ALU.add).then_inc(rot_ready, 1)

                @block.tensor
                def _(pe):
                    pe.wait_ge(d_in, 16)
                    for k in range(4):
                        tr = pe.transpose(ps[:, 1, k, :], d[:, k * P:(k + 1) * P], consts["ident"][:])
                    tr.then_inc(tr_done, 1)
                    pe.wait_ge(rot_ready, 1)
                    for k in range(4):
                        tr = pe.transpose(ps[:, 0, k, :], rot[:, k * P:(k + 1) * P], consts["ident"][:])
                    tr.then_inc(tr_done, 1)

                @block.scalar
                def _(act):
                    cols = bass.ds(i * P, P)
                    for n, (bank, q, k) in enumerate(((1, "qD", "kD"), (0, "qA", "kA"))):
                        act.wait_ge(tr_done, n + 1)
                        act.activation(b[q][:, :, cols], ps[:, bank, 0:2], ACT.Copy).then_inc(copied, 1)
                        act.activation(b[k][:, :, cols], ps[:, bank, 2:4], ACT.Copy).then_inc(copied, 1)


def attend_stage(nc, s, b, consts, group, first, last, key_tiles, bias_dram):
    diff = group == "A"
    parts = 2 if diff else 1
    per_tile = HEADS * parts
    jobs = 2 * HEADS
    nk = key_tiles * P
    scale = 32 ** -0.5 if diff else HD ** -0.5
    qT, kT, vt = b["q" + group], b["k" + group], b["v" + group]
    col = 0 if diff else 3 * GW
    nm = f"at{group}{first}_"
    with ExitStack() as es:
        sb = lambda n, sh: es.enter_context(nc.sbuf_tensor(nm + n, sh, F32))
        q = sb("q", [P, 2 * per_tile, P])
        e = sb("e", [P, 4, nk])
        pr = sb("p", [P, 2, nk])
        pt = sb("pt", [P, 2, key_tiles, P])
        st = sb("st", [P, 4, 2 * per_tile])
        sx = sb("sx", [P, 2, nk])
        bias = sb("bias", [P, 2, HEADS, SEQ]) if bias_dram is not None else None
        o = sb("o", [P, 2 * HEADS, HD])
        sq = sb("sq", [P, 2 * HEADS, HD])
        r = sb("r", [P, 3, 2 * HEADS])
        ps = es.enter_context(nc.psum_tensor(nm + "ps", [P, 2, 1024], F32))
        pst = es.enter_context(nc.psum_tensor(nm + "pst", [P, 8, P], F32))
        pso = es.enter_context(nc.psum_tensor(nm + "pso", [P, 2, 512], F32))
        with nc.Fori(first // 2, last // 2) as pair:
            i = pair * 2
            with stage(nc, "q_ready", "bias0_in", "bias1_in", "scores_done", "scores_read", "max_ready", "exp_done", "probs_ready", "tr_done",
                       "pt_ready", "av_done", "dve_step", "sq_ready", "sqrt_done", "o_ready", "o_gone") as \
                    (block, q_ready, bias0_in, bias1_in, scores_done, scores_read, max_ready, exp_done, probs_ready, tr_done,
                     pt_ready, av_done, dve_step, sq_ready, sqrt_done, o_ready, o_gone):

                @block.sync
                def _(sp):
                    if bias_dram is not None:
                        for tt in range(2):
                            sp.dma_start(bias[:, tt], bias_dram[i - first + tt]).then_inc((bias0_in, bias1_in)[tt], 16)
                    sp.wait_ge(o_ready, 1)
                    for tt in range(2):
                        sp.dma_start(s["y"][bass.ds((i + tt) * P, P), col:col + GW],
                                     o[:, tt * HEADS:(tt + 1) * HEADS].rearrange("p h e -> p (h e)")).then_inc(o_gone, 16)
                    sp.wait_ge(o_gone, 32)

                @block.tensor
                def _(pe):
                    def score(u):
                        h = u // parts % HEADS
                        if u % per_tile == 0:
                            pe.wait_ge(q_ready, u // per_tile + 1)
                        if u >= 2:
                            pe.wait_ge(scores_read, u - 1)
                        for c0 in range(0, nk, 512):
                            c1 = min(nk, c0 + 512)
                            mm = pe.matmul(ps[:, u % 2, c0:c1], q[:, u, :], kT[:, h // 2, c0:c1], start=True, stop=True)
                        mm.then_inc(scores_done, 1)

                    def weighted(j):
                        h = j % HEADS
                        pe.wait_ge(pt_ready, j + 1)
                        for k in range(key_tiles):
                            mm = pe.matmul(pso[:, j // HEADS, h * HD:(h + 1) * HD], pt[:, j % 2, k, :], vt[:, k, h * HD:(h + 1) * HD],
                                           start=(k == 0), stop=(k == key_tiles - 1))
                        mm.then_inc(av_done, 1)

                    for u in range(2):
                        score(u)
                    for j in range(jobs):
                        for u in range(parts * j + 2, parts * (j + 1) + 2):
                            if u < parts * jobs:
                                score(u)
                        pe.wait_ge(probs_ready, j + 1)
                        if j >= 1:
                            pe.wait_ge(pt_ready, j)
                        for k in range(key_tiles):
                            tr = pe.transpose(pst[:, k, :], pr[:, j % 2, k * P:(k + 1) * P], consts["ident"][:])
                        tr.then_inc(tr_done, 1)
                        if j >= 1:
                            weighted(j - 1)
                    weighted(jobs - 1)

                @block.scalar
                def _(act):
                    for j in range(jobs + 1):
                        if j < jobs:
                            for u in range(parts * j, parts * (j + 1)):
                                act.wait_ge(max_ready, u + 1)
                                if u >= 4:
                                    act.wait_ge(probs_ready, (u - 4) // parts + 1)
                                src = sx[:, u % 2, :] if bias is not None else ps[:, u % 2, 0:nk]
                                act.activation(e[:, u % 4, :], src, ACT.Exp, bias=st[:, 1, u:u + 1],
                                               scale=1.0 if bias is not None else scale,
                                               accum_out=st[:, 2, u:u + 1]).then_inc(exp_done, 1)
                                if bias is None:
                                    act.wait_ge(exp_done, u + 1)
                                    act.sem_inc(scores_read, 1)
                        if j >= 1:
                            act.wait_ge(tr_done, j)
                            if j >= 3:
                                act.wait_ge(av_done, j - 2)
                            act.activation(pt[:, (j - 1) % 2], pst[:, 0:key_tiles, :], ACT.Copy).then_inc(pt_ready, 1)
                    if diff:
                        act.wait_ge(sq_ready, 1)
                        act.activation(r[:, 1, :], r[:, 0, :], ACT.Sqrt).then_inc(sqrt_done, 1)

                @block.vector
                def _(v):
                    link = chained(v, dve_step)

                    def masked_queries(tt):
                        for x in range(per_tile):
                            h = x // parts
                            row = 2 + (h % 2) * 2 + x % 2 if diff else h % 2
                            mask = v.tensor_scalar(q[:, tt * per_tile + x, :], qT[:, h // 2, bass.ds((i + tt) * P, P)], consts["rows"][:, row:row + 1], None, ALU.mult)
                        mask.then_inc(q_ready, 1)

                    def maximum(u):
                        v.wait_ge(scores_done, u + 1)
                        src = ps[:, u % 2, 0:nk]
                        if bias is not None:
                            if u % HEADS == 0:
                                v.wait_ge((bias0_in, bias1_in)[u // HEADS], 16)
                            if u >= 2:
                                v.wait_ge(exp_done, u - 1)
                            v.tensor_scalar(sx[:, u % 2, 0:CTX], ps[:, u % 2, 0:CTX], scale, None, ALU.mult)
                            link(v.scalar_tensor_tensor(sx[:, u % 2, CTX:nk], ps[:, u % 2, CTX:nk], scale, bias[:, u // HEADS, u % HEADS, :], ALU.mult, ALU.add))
                            v.sem_inc(scores_read, 1)
                            src = sx[:, u % 2, :]
                        link(v.tensor_reduce(st[:, 0, u:u + 1], src, X, ALU.max))
                        v.tensor_scalar(st[:, 1, u:u + 1], st[:, 0, u:u + 1], -1.0 if bias is not None else -scale, None, ALU.mult).then_inc(max_ready, 1)

                    masked_queries(0)
                    for u in range(parts):
                        maximum(u)
                    masked_queries(1)
                    for j in range(jobs):
                        if not diff and j + 1 < jobs:
                            maximum(j + 1)
                        u = parts * j
                        v.wait_ge(exp_done, u + parts)
                        if j >= 2:
                            v.wait_ge(tr_done, j - 1)
                        link(v.reciprocal(st[:, 3, u:u + parts], st[:, 2, u:u + parts]))
                        if diff:
                            x1, x2 = u, u + 1
                            link(v.tensor_scalar(e[:, x2 % 4, :], e[:, x2 % 4, :], st[:, 3, x2:x2 + 1], b["lam"][:, 0:1], ALU.mult, ALU.mult))
                            v.scalar_tensor_tensor(pr[:, j % 2, :], e[:, x1 % 4, :], st[:, 3, x1:x1 + 1], e[:, x2 % 4, :],
                                                   ALU.mult, ALU.subtract).then_inc(probs_ready, 1)
                        else:
                            v.tensor_scalar(pr[:, j % 2, :], e[:, u % 4, :], st[:, 3, u:u + 1], None, ALU.mult).then_inc(probs_ready, 1)
                        if diff and j + 1 < jobs:
                            for u in range(parts * (j + 1), parts * (j + 2)):
                                maximum(u)
                    v.wait_ge(av_done, jobs)
                    out = v.tensor_copy(o[:].rearrange("p (t h) e -> p t (h e)", t=2), pso[:, :, 0:GW])
                    if not diff:
                        out.then_inc(o_ready, 1)
                        return
                    link(out)
                    link(v.tensor_tensor(sq[:], o[:], o[:], ALU.mult))
                    link(v.tensor_reduce(r[:, 2, :], sq[:], X, ALU.add))
                    v.tensor_scalar(r[:, 0, :], r[:, 2, :], 1.0 / HD, NORM_EPS, ALU.mult, ALU.add).then_inc(sq_ready, 1)
                    v.wait_ge(sqrt_done, 1)
                    link(v.reciprocal(r[:, 2, :], r[:, 1, :]))
                    link(v.tensor_tensor(o[:], o[:], r[:, 2, :].unsqueeze(2).to_broadcast([P, 2 * HEADS, HD]), ALU.mult))
                    v.tensor_tensor(o[:], o[:], b["g"][:].unsqueeze(1).to_broadcast([P, 2 * HEADS, HD]), ALU.mult).then_inc(o_ready, 1)


def head_bc(x):
    return x.unsqueeze(2).to_broadcast(list(x.shape) + [HD])


def by_head(x):
    return x.rearrange("p (h e) -> p h e", e=HD)


def store_chunks(eng, dst, src, i, back, sem):
    for d, tile in ((0, i), (1, back)):
        for half in range(2):
            eng.dma_start(dst[tile, half, d].rearrange("b t q a e -> t b (q a e)"),
                          src[half * C:(half + 1) * C, d].rearrange("t b q a e -> t b (q a e)")).then_inc(sem, 16)


def heads_of(x):
    return x.rearrange("p (a b e) -> p a b e", a=2, b=2)


def heads_bc(x):
    return x.rearrange("p (a b) -> p a b", a=2).unsqueeze(3).to_broadcast([P, 2, 2, HD])


def prep_stage(nc, l, t, s, consts):
    W, V = RWKV_COLS, GDN_QKV
    ND = 2 * HEADS
    with ExitStack() as es:
        sb = lambda n, sh: es.enter_context(nc.sbuf_tensor("pp_" + n, sh, F32))
        mu, w2, a2, g2 = sb("mu", [P, 3, W]), sb("w2", [P, 2, GW]), sb("a2", [P, 2, GW]), sb("g2", [P, GW])
        w0, a0, kk_g, ka_g, rk_g = sb("w0", [P, 2 * GW]), sb("a0", [P, 2 * GW]), sb("kkg", [P, GW]), sb("kag", [P, GW]), sb("rkg", [P, GW])
        raw, f, fp, fn, edge = sb("raw", [P, W]), sb("f", [P, W]), sb("fp", [P, W]), sb("fn", [P, W]), sb("edge", [P, 2])
        low, lowT = sb("low", [P, 2, P]), sb("lowT", [P, 3, P])
        wr, ar, sg, ex, av = [sb(n, [P, 2, GW]) for n in ("wr", "ar", "sg", "ex", "av")]
        e_in, e_neg, e_ex, dec = [sb(n, [P, 2, GW]) for n in ("ein", "eneg", "eex", "dec")]
        kk, sq, kd, kka = sb("kk", [P, GW]), sb("sq", [P, GW]), sb("kd", [P, 2, GW]), sb("kka", [P, 2, GW])
        n4 = sb("n4", [P, 4, HEADS])
        out, post, rks = sb("out", [P, 2, 2, 5, 2, HD]), sb("post", [P, 2, GW]), sb("rks", [P, 2, GW])
        cw, alog, dtb = sb("cw", [P, 3, V]), sb("alog", [P, ND]), sb("dtb", [P, ND])
        gf, gfp, gfn = sb("gf", [P, GDN_COLS]), sb("gfp", [P, V]), sb("gfn", [P, V])
        qkv, gsq, n8 = sb("qkv", [P, V]), sb("gsq", [P, 2 * GW]), sb("n8", [P, 4, ND])
        x8, cols, cols_b = sb("x8", [P, 16, ND]), sb("cols", [P, 2, ND]), sb("cols_b", [P, 2, ND])
        gout, gpost = sb("gout", [P, 2, 2, 7, 2, HD]), sb("gpost", [P, GW])
        ps = es.enter_context(nc.psum_tensor("pp_ps", [P, 7, 512], F32))
        flat = lambda x: x[:].rearrange("p a b -> p (a b)")
        over_dir = lambda x: x.unsqueeze(1).to_broadcast([P, 2, GW])
        quantity = lambda o, d, n: o[:, d, :, n].rearrange("p b a e -> p a b e")
        x, neg, ax, u, den, z, z2, acc, top, g, gap, beta, egc, egap, bg = [x8[:, k, :] for k in range(15)]

        def load_tile(sp, i, sem):
            rows = lambda shift: bass.ds(i * P + shift, P)
            for dst, src in ((raw, s["p"][rows(1), COL_B:COL_B + W]), (gf, s["p"][rows(1), COL_C:COL_C + GDN_COLS]), (edge, t["k_edges"][i]),
                             (fp, s["p"][rows(0), COL_B:COL_B + W]), (fn, s["p"][rows(2), COL_B:COL_B + W]),
                             (gfp, s["p"][rows(0), COL_C:COL_C + V]), (gfn, s["p"][rows(2), COL_C:COL_C + V])):
                sp.dma_start(dst[:], src).then_inc(sem, 16)

        with stage(nc, "zeroed", "params_in", "first_in", "mid", "exp_done") as (block, zeroed, params_in, first_in, mid, exp_done):
            @block.gpsimd
            def _(pool):
                pool.memset(w2[:], 0.0).then_inc(zeroed, 1)
                pool.memset(a2[:], 0.0).then_inc(zeroed, 1)

            @block.sync
            def _(sp):
                loads = [(mu[:, 0], over_rows(t["rwkv_mu"][l, 0])), (mu[:, 2], over_rows(t["rwkv_mu"][l, 1])), (g2[:], t["rwkv_g2"][l]),
                         (w0[:], over_rows(t["rwkv_w0"][l])), (a0[:], over_rows(t["rwkv_a0"][l])), (kk_g[:], over_rows(t["rwkv_kk"][l])),
                         (ka_g[:], over_rows(t["rwkv_ka"][l])), (rk_g[:], over_rows(t["rwkv_rk"][l]))]
                loads += [(cw[:, k], over_rows(t["gdn_conv"][l, k])) for k in range(3)]
                loads += [(alog[:], over_rows(t["gdn_a_log"][l])), (dtb[:], over_rows(t["gdn_dt_bias"][l]))]
                sp.wait_ge(zeroed, 2)
                for d in range(2):
                    for dst, src in ((w2, "rwkv_w2"), (a2, "rwkv_a2")):
                        loads.append((dst[d * LORA:(d + 1) * LORA, d, :], t[src][l, d]))
                for dst, src in loads:
                    sp.dma_start(dst, src).then_inc(params_in, 16)
                load_tile(sp, 0, first_in)
                sp.wait_ge(params_in, 16 * 17)
                sp.wait_ge(first_in, 16 * 7)

            @block.vector
            def _(v):
                v.wait_ge(params_in, 16 * 17)
                v.tensor_tensor(mu[:, 1], mu[:, 0], mu[:, 2], ALU.add).then_inc(mid, 1)
                v.wait_ge(mid, 1)
                v.tensor_scalar(mu[:, 1], mu[:, 1], -1.0, 1.0, ALU.mult, ALU.add)

            @block.scalar
            def _(act):
                act.wait_ge(params_in, 16 * 17)
                act.activation(alog[:], alog[:], ACT.Exp).then_inc(exp_done, 1)

        with nc.Fori(0, TILES) as i:
            with stage(nc, "next_in", "sides_ready", "gsides_ready", "f_ready", "low_ready", "low_done", "lowT_ready",
                       "raw_done", "raw_ready", "gates_ready", "g_copied", "sums_done", "ex_ready", "exps_ready", "sq_ready", "root_ready",
                       "dve_step", "out_ready", "stored", "abs_ready", "exp_ready", "g_ready", "gsums_done", "conv_ready", "qkv_ready",
                       "gate_ready", "beta_ready", "gsq_ready", "groot_ready", "dec_ready", "gexps_ready", "gout_ready", "gstored") as \
                    (block, next_in, sides_ready, gsides_ready, f_ready, low_ready, low_done, lowT_ready,
                     raw_done, raw_ready, gates_ready, g_copied, sums_done, ex_ready, exps_ready, sq_ready, root_ready,
                     dve_step, out_ready, stored, abs_ready, exp_ready, g_ready, gsums_done, conv_ready, qkv_ready,
                     gate_ready, beta_ready, gsq_ready, groot_ready, dec_ready, gexps_ready, gout_ready, gstored):
                @block.sync
                def _(sp):
                    sp.wait_ge(conv_ready, 1)
                    sp.wait_ge(beta_ready, 1)
                    sp.wait_ge(gate_ready, 1)
                    load_tile(sp, sp.snap((i + 1) % TILES), next_in)
                    back = sp.snap((i + 4) % TILES + CTX_TILES)
                    sp.wait_ge(dec_ready, 1)
                    for d, tile in ((0, i), (1, back)):
                        for half in range(2):
                            sp.dma_start(s["gdcol"][tile * 2 + half, d].rearrange("b t m -> t b m"),
                                         cols_b[half * C:(half + 1) * C, :, 4 * d:4 * d + 4]).then_inc(gstored, 16)
                    sp.dma_start(s["gdpost"][i], gpost[:]).then_inc(gstored, 16)
                    sp.wait_ge(exps_ready, 4)
                    for d, tile in ((0, i), (1, back)):
                        sp.dma_start(s["rwdec"][bass.ds(tile * 2, 2), d], dec[0:C + 1:C, d, :]).then_inc(stored, 16)
                    sp.wait_ge(out_ready, 1)
                    store_chunks(sp, s["rw"], out, i, back, stored)
                    sp.dma_start(s["rwpost"][i], post[:]).then_inc(stored, 16)
                    sp.wait_ge(gout_ready, 1)
                    store_chunks(sp, s["gd"], gout, i, back, gstored)
                    sp.wait_ge(stored, 16 * 7)
                    sp.wait_ge(gstored, 16 * 9)
                    sp.wait_ge(next_in, 16 * 7)

                @block.gpsimd
                def _(pool):
                    pool.tensor_tensor(fp[:], fp[:], mu[:, 0], ALU.mult).then_inc(sides_ready, 1)
                    pool.tensor_tensor(fn[:], fn[:], mu[:, 2], ALU.mult).then_inc(sides_ready, 1)
                    pool.tensor_tensor(gfp[:], gfp[:], cw[:, 0], ALU.mult).then_inc(gsides_ready, 1)
                    pool.tensor_tensor(gfn[:], gfn[:], cw[:, 2], ALU.mult).then_inc(gsides_ready, 1)

                @block.vector
                def _(v):
                    link = chained(v, dve_step)
                    r, k, val = f[:, 0:GW], f[:, GW:2 * GW], f[:, 2 * GW:3 * GW]

                    link(v.tensor_tensor(x, gf[:, 4 * GW:4 * GW + ND], dtb[:], ALU.add))
                    link(v.tensor_scalar(neg, x, -1.0, None, ALU.mult))
                    v.tensor_tensor(ax, x, neg, ALU.max).then_inc(abs_ready, 1)
                    v.tensor_scalar(top, x, 0.0, None, ALU.max)
                    link(v.tensor_tensor(f[:], raw[:], mu[:, 1], ALU.mult))
                    v.wait_ge(sides_ready, 1)
                    link(v.scalar_tensor_tensor(f[:], fp[:], edge[:, 0:1], f[:], ALU.mult, ALU.add))
                    v.wait_ge(sides_ready, 2)
                    link(v.scalar_tensor_tensor(f[:], fn[:], edge[:, 1:2], f[:], ALU.mult, ALU.add))
                    v.sem_inc(f_ready, 1)
                    link(v.tensor_tensor(qkv[:], gf[:, 0:V], cw[:, 1], ALU.mult))
                    v.wait_ge(gsides_ready, 1)
                    link(v.scalar_tensor_tensor(qkv[:], gfp[:], edge[:, 0:1], qkv[:], ALU.mult, ALU.add))
                    v.wait_ge(gsides_ready, 2)
                    v.scalar_tensor_tensor(qkv[:], gfn[:], edge[:, 1:2], qkv[:], ALU.mult, ALU.add).then_inc(conv_ready, 1)
                    link(v.tensor_tensor(kk[:], k, kk_g[:], ALU.mult))
                    link(v.tensor_tensor(sq[:], kk[:], kk[:], ALU.mult))
                    link(v.tensor_reduce(n4[:, 0, :], by_head(sq[:]), X, ALU.add))
                    v.tensor_scalar(n4[:, 1, :], n4[:, 0, :], NORM_EPS, None, ALU.add).then_inc(sq_ready, 1)
                    v.wait_ge(exp_ready, 1)
                    link(v.tensor_scalar(den, u, 2.0, None, ALU.add))
                    link(v.reciprocal(z2, den))
                    link(v.tensor_tensor(z, u, z2, ALU.mult))
                    link(v.tensor_tensor(z2, z, z, ALU.mult))
                    link(v.tensor_scalar(acc, z2, 2.0 / 19, 2.0 / 17, ALU.mult, ALU.add))
                    for odd in (15, 13, 11, 9, 7, 5, 3, 1):
                        link(v.tensor_tensor(acc, acc, z2, ALU.mult))
                        link(v.tensor_scalar(acc, acc, 2.0 / odd, None, ALU.add))
                    link(v.tensor_tensor(acc, acc, z, ALU.mult))
                    link(v.tensor_tensor(acc, acc, top, ALU.add))
                    v.scalar_tensor_tensor(g, acc, -1.0, alog[:], ALU.mult, ALU.mult).then_inc(g_ready, 1)
                    v.wait_ge(raw_done, 1)
                    v.tensor_tensor(flat(wr), ps[:, 1, :], w0[:], ALU.add).then_inc(raw_ready, 1)
                    v.wait_ge(raw_done, 2)
                    v.tensor_tensor(flat(ar), ps[:, 2, :], a0[:], ALU.add).then_inc(raw_ready, 1)
                    v.wait_ge(qkv_ready, 1)
                    link(v.tensor_tensor(gsq[:], qkv[:, 0:2 * GW], qkv[:, 0:2 * GW], ALU.mult))
                    link(v.tensor_reduce(n8[:, 0, :], by_head(gsq[:]), X, ALU.add))
                    v.tensor_scalar(n8[:, 1, :], n8[:, 0, :], NORM_EPS, None, ALU.add).then_inc(gsq_ready, 1)
                    v.wait_ge(gsums_done, 1)
                    link(v.tensor_copy(cols[:], ps[:, 6, 0:2 * ND].rearrange("p (a n) -> p a n", a=2)))
                    for w in range(2):
                        for b in range(2):
                            v.tensor_copy(cols_b[:, b].rearrange("p (d w a) -> p d w a", d=2, w=2)[:, :, w, :],
                                          cols[:, w].rearrange("p (d a b) -> p d a b", d=2, a=2)[:, :, :, b])
                    v.tensor_tensor(gap, cols[:, 1], cols[:, 0], ALU.subtract).then_inc(dec_ready, 1)
                    v.wait_ge(root_ready, 1)
                    link(v.reciprocal(n4[:, 3, :], n4[:, 2, :]))
                    link(v.tensor_tensor(by_head(kk[:]), by_head(kk[:]), head_bc(n4[:, 3, :]), ALU.mult))
                    v.wait_ge(sums_done, 1)
                    v.wait_ge(gates_ready, 2)
                    v.tensor_tensor(flat(ex), ps[:, 4, :], flat(sg), ALU.subtract).then_inc(ex_ready, 1)
                    v.tensor_tensor(kka[:], av[:], over_dir(kk[:]), ALU.mult)
                    link(v.scalar_tensor_tensor(kd[:], av[:], -1.0, over_dir(ka_g[:]), ALU.add, ALU.mult))
                    link(v.scalar_tensor_tensor(kd[:], kd[:], 1.0, over_dir(k), ALU.add, ALU.mult))
                    v.tensor_tensor(rks[:, 0], r, rk_g[:], ALU.mult)
                    link(v.tensor_tensor(sq[:], kd[:, 0], kd[:, 1], ALU.add))
                    link(v.tensor_tensor(rks[:, 1], rks[:, 0], sq[:], ALU.mult))
                    link(v.tensor_reduce(n4[:, 0, :], by_head(rks[:, 1]), X, ALU.add))
                    v.tensor_tensor(by_head(post[:, 0]), by_head(val), head_bc(n4[:, 0, :]), ALU.mult)
                    for d in range(2):
                        v.tensor_copy(quantity(out, d, 4), heads_of(val))
                    v.wait_ge(exps_ready, 4)
                    for d in range(2):
                        v.tensor_tensor(quantity(out, d, 0), heads_of(e_ex[:, d]), heads_of(kk[:]), ALU.mult)
                        v.tensor_tensor(quantity(out, d, 1), heads_of(e_neg[:, d]), heads_of(kka[:, d]), ALU.mult)
                        v.tensor_tensor(quantity(out, d, 2), heads_of(e_neg[:, d]), heads_of(kd[:, d]), ALU.mult)
                        last = v.tensor_tensor(quantity(out, d, 3), heads_of(e_in[:, d]), heads_of(r), ALU.mult)
                    v.wait_ge(g_copied, 1)
                    link(last)
                    v.sem_inc(out_ready, 1)
                    v.wait_ge(groot_ready, 1)
                    link(v.reciprocal(n8[:, 3, :], n8[:, 2, :]))
                    link(v.tensor_scalar(n8[:, 3, 0:HEADS], n8[:, 3, 0:HEADS], HD ** -0.5, None, ALU.mult))
                    link(v.tensor_tensor(by_head(qkv[:, 0:2 * GW]), by_head(qkv[:, 0:2 * GW]), head_bc(n8[:, 3, :]), ALU.mult))
                    v.wait_ge(gexps_ready, 2)
                    v.wait_ge(beta_ready, 1)
                    link(v.tensor_tensor(bg, beta, egc, ALU.mult))
                    gq, gk, gval = [qkv[:, m * GW:(m + 1) * GW] for m in range(3)]
                    for d in range(2):
                        hs = slice(d * HEADS, (d + 1) * HEADS)
                        for n, (src, by) in enumerate(((gk, bg), (gk, beta), (gk, None), (gq, None), (gq, egc), (gk, egap), (gval, beta))):
                            if by is None:
                                last = v.tensor_copy(quantity(gout, d, n), heads_of(src))
                            else:
                                last = v.tensor_tensor(quantity(gout, d, n), heads_of(src), heads_bc(by[:, hs]), ALU.mult)
                    link(last)
                    v.wait_ge(gate_ready, 1)
                    v.sem_inc(gout_ready, 1)

                @block.scalar
                def _(act):
                    act.wait_ge(abs_ready, 1)
                    act.activation(u, ax, ACT.Exp, scale=-1.0).then_inc(exp_ready, 1)
                    act.wait_ge(f_ready, 1)
                    act.activation(low[:, 0], f[:, 3 * GW:3 * GW + P], ACT.Tanh).then_inc(low_ready, 1)
                    act.activation(low[:, 1], f[:, 3 * GW + 2 * P:3 * GW + 3 * P], ACT.Sigmoid).then_inc(low_ready, 1)
                    act.activation(beta, gf[:, 4 * GW + ND:4 * GW + 2 * ND], ACT.Sigmoid).then_inc(beta_ready, 1)
                    act.wait_ge(low_done, 1)
                    act.activation(lowT[:], ps[:, 0, 0:3 * P].rearrange("p (a b) -> p a b", a=3), ACT.Copy).then_inc(lowT_ready, 1)
                    act.activation(gpost[:], gf[:, 3 * GW:4 * GW], ACT.Silu).then_inc(gate_ready, 1)
                    act.wait_ge(conv_ready, 1)
                    act.activation(qkv[:], qkv[:], ACT.Silu).then_inc(qkv_ready, 1)
                    act.wait_ge(raw_ready, 1)
                    act.activation(flat(sg), flat(wr), ACT.Sigmoid).then_inc(gates_ready, 1)
                    act.wait_ge(raw_ready, 2)
                    act.activation(flat(av), flat(ar), ACT.Sigmoid).then_inc(gates_ready, 1)
                    act.wait_ge(raw_done, 3)
                    act.activation(post[:, 1], ps[:, 3, 0:GW], ACT.Copy).then_inc(g_copied, 1)
                    act.wait_ge(sq_ready, 1)
                    act.activation(n4[:, 2, :], n4[:, 1, :], ACT.Sqrt).then_inc(root_ready, 1)
                    act.wait_ge(gsq_ready, 1)
                    act.activation(n8[:, 2, :], n8[:, 1, :], ACT.Sqrt).then_inc(groot_ready, 1)
                    act.wait_ge(ex_ready, 1)
                    act.activation(flat(e_in), ps[:, 4, :], ACT.Exp, scale=DECAY).then_inc(exps_ready, 1)
                    act.activation(flat(e_neg), ps[:, 4, :], ACT.Exp, scale=-DECAY).then_inc(exps_ready, 1)
                    act.activation(flat(e_ex), flat(ex), ACT.Exp, scale=DECAY).then_inc(exps_ready, 1)
                    act.wait_ge(sums_done, 2)
                    act.activation(flat(dec), ps[:, 5, :], ACT.Exp, scale=DECAY).then_inc(exps_ready, 1)
                    act.wait_ge(dec_ready, 1)
                    act.activation(egc, cols[:, 0], ACT.Exp).then_inc(gexps_ready, 1)
                    act.activation(egap, gap, ACT.Exp).then_inc(gexps_ready, 1)

                @block.tensor
                def _(pe):
                    pe.wait_ge(low_ready, 2)
                    for n, src in enumerate((low[:, 0], f[:, 3 * GW + P:3 * GW + 2 * P], low[:, 1])):
                        tr = pe.transpose(ps[:, 0, n * P:(n + 1) * P], src, consts["ident"][:])
                    tr.then_inc(low_done, 1)
                    pe.wait_ge(lowT_ready, 1)
                    pe.matmul(ps[:, 1, :], lowT[:, 0], flat(w2), start=True, stop=True).then_inc(raw_done, 1)
                    pe.matmul(ps[:, 2, :], lowT[:, 1], flat(a2), start=True, stop=True).then_inc(raw_done, 1)
                    pe.matmul(ps[:, 3, 0:GW], lowT[:, 2], g2[:], start=True, stop=True).then_inc(raw_done, 1)
                    pe.wait_ge(g_ready, 1)
                    for d in range(2):
                        pe.matmul(ps[:, 6, d * HEADS:(d + 1) * HEADS], consts["sums"][:, d, :], g[:, d * HEADS:(d + 1) * HEADS], start=True, stop=True)
                    pe.matmul(ps[:, 6, ND:2 * ND], consts["sums"][:, 2, :], g, start=True, stop=True).then_inc(gsums_done, 1)
                    pe.wait_ge(gates_ready, 1)
                    for d in range(2):
                        mm = pe.matmul(ps[:, 4, d * GW:(d + 1) * GW], consts["sums"][:, d, :], sg[:, d], start=True, stop=True)
                    mm.then_inc(sums_done, 1)
                    pe.matmul(ps[:, 5, :], consts["sums"][:, 2, :], flat(sg), start=True, stop=True).then_inc(sums_done, 1)


def chunk_stage(nc, t, s, consts):
    NQ = (4, 6)
    N4 = 4
    with ExitStack() as es:
        sb = lambda n, sh: es.enter_context(nc.sbuf_tensor("ch_" + n, sh, F32))
        full = lambda n: sb(n, [P, N4, P])
        stacked = lambda n: sb(n, [P, N4, C])
        near, joins = sb("near", [P, 2, 2, C]), sb("joins", [P, 6, 2, P])
        eye = sb("eye", [P, C])
        nat = [sb(f"nat{k}", [P, 2, NQ[k] + 1, 2, HD]) for k in range(2)]
        col, dec_in = sb("col", [P, 2, 2, 2]), sb("dec_in", [P, N4])
        bd = [sb(f"bd{k}", [P, 2, NQ[k], 2, P]) for k in range(2)]
        val = [sb(f"val{k}", [P, 2, 2, HD]) for k in range(2)]
        tf = {(k, q): full(f"t{k}{q}") for k, q in [(0, q) for q in range(4)] + [(1, q) for q in range(5)]}
        at = [full(f"at{k}") for k in range(2)]
        m = [sb(f"m{k}", [P, 6, N4, P]) for k in range(2)]
        xt = [full(f"xt{k}") for k in range(2)]
        x = [full(f"x{k}") for k in range(2)]
        y = [full(f"y{k}") for k in range(2)]
        akt, rk, rb, qk = [full(n) for n in ("akt", "rk", "rb", "qk")]
        diag, du, dd, ddm = [stacked(n) for n in ("diag", "du", "dd", "ddm")]
        st, rhs, nn, oo = [[sb(f"{n}{k}", [P, N4, HD]) for k in range(2)] for n in ("st", "rhs", "nn", "oo")]
        dec = [sb(f"dec{k}", [P, N4]) for k in range(2)]
        ps = es.enter_context(nc.psum_tensor("ch_ps", [P, 8, N4, P], F32))
        prob = lambda n: (n // 2, n % 2)
        half = lambda x, b: x[b * C:(b + 1) * C]
        block_of = lambda x, b: x[b * C:(b + 1) * C, :, b * C:(b + 1) * C]
        out_of = lambda bank: ps[:, bank, :, 0:C]
        over_pairs = lambda x: x.unsqueeze(2).to_broadcast([x.shape[0], 2, 2, x.shape[-1]])
        by_pair = lambda x: x.rearrange("p (d a) c -> p d a c", d=2)
        eye_s = eye[:].unsqueeze(1).to_broadcast([P, N4, C])
        src_dram = (s["rw"], s["gd"])

        def load_chunk(sp, fwd, bwd, sem):
            for d, chunk in enumerate((fwd, bwd)):
                sp.dma_start(col[:, :, d], s["gdcol"][chunk, d].rearrange("b t (w a) -> (b t) w a", w=2)).then_inc(sem, 16)
                for k in range(2):
                    sp.dma_start(nat[k][:, d], src_dram[k].rearrange("i c d b t q a e -> (i c) d (b t) q a e")[chunk, d]).then_inc(sem, 16)
                sp.dma_start(dec_in[:, 2 * d:2 * d + 2], s["rwdec"][chunk, d].rearrange("(a p) -> p a", p=P),
                             allow_slow_non_contiguous=True).then_inc(sem, 16)

        def store_outputs(sp, chunk, sem):
            for k in range(2):
                for b in range(2):
                    for d, place in ((0, chunk), (1, 23 - chunk), (1, 11 - chunk)):
                        sp.dma_start(s["scan"][k, d, place].rearrange("t (a b e) -> b t a e", a=2, b=2)[b],
                                     oo[k][b * C:(b + 1) * C, 2 * d:2 * d + 2]).then_inc(sem, 16)

        with stage(nc, "masks_in", "first_in") as (block, masks_in, first_in):
            @block.sync
            def _(sp):
                sp.dma_start(near[:], t["k_near"]).then_inc(masks_in, 16)
                sp.dma_start(joins[:], t["k_joins"]).then_inc(masks_in, 16)
                for b in range(2):
                    sp.dma_start(half(eye, b), t["k_ident"][b * C:(b + 1) * C, b * C:(b + 1) * C]).then_inc(masks_in, 16)
                load_chunk(sp, 0, 15, first_in)
                sp.wait_ge(masks_in, 64)
                sp.wait_ge(first_in, 16 * 8)

            @block.gpsimd
            def _(pool):
                for k in range(2):
                    pool.memset(bd[k][:], 0.0)
                    pool.memset(st[k][:], 0.0)
                    pool.memset(oo[k][:], 0.0)
                    pool.memset(at[k][:], 0.0)

            @block.vector
            def _(v):
                for blocks in (akt, rk, rb, qk):
                    v.memset(blocks[:], 0.0)

        names = ["top_spread", "bottom_spread", "vals_kept", "next_in", "diag_ready", "diffs_done", "du_ready", "dd_ready", "tr_done",
                 "tr_copied", "gram_done", "at_ready", "fill_done", "fill_ready", "m_ready", "x_done", "x_ready", "xt_ready",
                 "y_done", "y_ready", "z_done", "rhs_done", "rhs_ready0",
                 "rhs_ready1", "n_done", "n_ready", "o_done", "o_ready", "ds_done", "dve_step", "dec_ready", "stored"]
        with nc.Fori(0, CHUNKS) as c:
            with stage(nc, *names) as (block, top_spread, bottom_spread, vals_kept, next_in, diag_ready, diffs_done, du_ready, dd_ready, tr_done,
                                       tr_copied, gram_done, at_ready, fill_done, fill_ready, m_ready, x_done, x_ready, xt_ready,
                                       y_done, y_ready, z_done, rhs_done, rhs_ready0,
                                       rhs_ready1, n_done, n_ready, o_done, o_ready, ds_done, dve_step, dec_ready, stored):
                order = [(0, 1), (0, 0), (1, 2), (1, 1), (0, 2), (0, 3), (1, 3), (1, 0), (1, 4)]
                fills = [((0, 2), (0, 0)), ((0, 2), (0, 3)), ((0, 1), (0, 3)), ((1, 2), (1, 3))]

                def spread(k, b):
                    return (bd[k][b * C:(b + 1) * C, :, :, :, b * C:(b + 1) * C].rearrange("p d q a e -> p d (q a) e"),
                            half(nat[k], b)[:, :, 0:NQ[k]].rearrange("p d q a e -> p d (q a) e"))

                @block.sync
                def _(sp):
                    store_outputs(sp, sp.snap((c + CHUNKS - 1) % CHUNKS), stored)
                    ahead = sp.snap((c + 1) % CHUNKS)
                    sp.wait_ge(top_spread, 2)
                    sp.wait_ge(bottom_spread, 2)
                    sp.wait_ge(vals_kept, 2)
                    sp.wait_ge(du_ready, 1)
                    sp.wait_ge(dec_ready, 2)
                    load_chunk(sp, ahead, 15 - ahead, next_in)
                    sp.wait_ge(stored, 16 * 12)
                    sp.wait_ge(next_in, 16 * 8)

                @block.gpsimd
                def _(pool):
                    for k in range(2):
                        pool.tensor_copy(val[k][:], nat[k][:, :, NQ[k]]).then_inc(vals_kept, 1)
                    for lev in range(6):
                        for k in range(2):
                            if lev == 0:
                                pool.wait_ge(at_ready, k + 1)
                            pool.tensor_tensor(by_pair(m[k][:, lev]), by_pair(at[k][:]), over_pairs(joins[:, lev]), ALU.mult).then_inc(m_ready, 1)

                @block.tensor
                def _(pe):
                    gram = lambda bank, left, right, n: pe.matmul(ps[:, bank, n, :], tf[left][:, n, :], tf[right][:, n, :], start=True, stop=True)
                    for g, (k, q) in enumerate(order):
                        pe.wait_ge(top_spread, k + 1)
                        pe.wait_ge(bottom_spread, k + 1)
                        if g >= 4:
                            pe.wait_ge(tr_copied, g - 3)
                        for n in range(N4):
                            d, a = prob(n)
                            tr = pe.transpose(ps[:, g % 4, n, :], bd[k][:, d, q, a, :], consts["ident"][:])
                        tr.then_inc(tr_done, 1)
                        if g == 1:
                            pe.wait_ge(diag_ready, 1)
                            pe.matmul(ps[:, 7].rearrange("p a b -> p (a b)")[:, 0:N4 * C], consts["sums"][:, 2, :],
                                      diag[:].rearrange("p a b -> p (a b)"), start=True, stop=True).then_inc(diffs_done, 1)
                        if g in (3, 5):
                            k2 = (g - 3) // 2
                            pe.wait_ge(tr_copied, (2, 4)[k2])
                            for n in range(N4):
                                mm = gram(4 + k2, ((0, 1), (1, 2))[k2], ((0, 0), (1, 1))[k2], n)
                            mm.then_inc(gram_done, 1)
                    pe.wait_ge(tr_copied, 9)
                    for lev in range(1, 6):
                        for k in range(2):
                            pe.wait_ge(xt_ready, 2 * (lev - 1) + k + 1)
                            for n in range(N4):
                                mm = pe.transpose(ps[:, 2 + k, n, :], xt[k][:, n, :], consts["ident"][:])
                            mm.then_inc(x_done, 1)
                        for k in range(2):
                            pe.wait_ge(x_ready, 2 * (lev - 1) + k + 1)
                            pe.wait_ge(m_ready, 2 * lev + k + 1)
                            for n in range(N4):
                                mm = pe.matmul(ps[:, k, n, :], m[k][:, lev, n, :], x[k][:, n, :], start=True, stop=True)
                            mm.then_inc(y_done, 1)
                        if lev < 5:
                            if lev > 2:
                                pe.wait_ge(fill_ready, lev - 2)
                            for n in range(N4):
                                mm = gram(6 + lev % 2, *fills[lev - 1], n)
                            mm.then_inc(fill_done, 1)
                        else:
                            pe.wait_ge(fill_ready, 4)
                            pe.wait_ge(vals_kept, 2)
                            for n in range(N4):
                                pe.matmul(ps[:, 6, n, 0:HD], tf[0, 0][:, n, :], st[0][:, n, :], start=True, stop=False)
                                mm = pe.matmul(ps[:, 6, n, 0:HD], akt[:, n, :], val[0][:, n // 2, n % 2, :], start=False, stop=True)
                            mm.then_inc(rhs_done, 1)
                            for n in range(N4):
                                mm = pe.matmul(ps[:, 7, n, 0:HD], tf[1, 0][:, n, :], st[1][:, n, :], start=True, stop=True)
                            mm.then_inc(rhs_done, 1)
                        for k in range(2):
                            pe.wait_ge(y_ready, 2 * (lev - 1) + k + 1)
                            for n in range(N4):
                                mm = pe.matmul(ps[:, 4 + k, n, :], y[k][:, n, :], xt[k][:, n, :], start=True, stop=True)
                            mm.then_inc(z_done, 1)
                    for k in range(2):
                        pe.wait_ge((rhs_ready0, rhs_ready1)[k], 1)
                        pe.wait_ge(xt_ready, 11 + k)
                        for n in range(N4):
                            mm = pe.matmul(ps[:, k, n, 0:HD], xt[k][:, n, :], rhs[k][:, n, :], start=True, stop=True)
                        mm.then_inc(n_done, 1)
                    for k in range(2):
                        pe.wait_ge(n_ready, k + 1)
                        for n in range(N4):
                            d, a = prob(n)
                            if k == 0:
                                pe.matmul(ps[:, 2, n, 0:HD], tf[0, 3][:, n, :], st[0][:, n, :], start=True, stop=False)
                                pe.matmul(ps[:, 2, n, 0:HD], rk[:, n, :], val[0][:, d, a, :], start=False, stop=False)
                                mm = pe.matmul(ps[:, 2, n, 0:HD], rb[:, n, :], nn[0][:, n, :], start=False, stop=True)
                            else:
                                pe.matmul(ps[:, 3, n, 0:HD], tf[1, 4][:, n, :], st[1][:, n, :], start=True, stop=False)
                                mm = pe.matmul(ps[:, 3, n, 0:HD], qk[:, n, :], nn[1][:, n, :], start=False, stop=True)
                        mm.then_inc(o_done, 1)
                        for n in range(N4):
                            d, a = prob(n)
                            if k == 0:
                                pe.matmul(ps[:, 4, n, 0:HD], bd[0][:, d, 2, a, :], val[0][:, d, a, :], start=True, stop=False)
                                mm = pe.matmul(ps[:, 4, n, 0:HD], bd[0][:, d, 1, a, :], nn[0][:, n, :], start=False, stop=True)
                            else:
                                mm = pe.matmul(ps[:, 5, n, 0:HD], bd[1][:, d, 5, a, :], nn[1][:, n, :], start=True, stop=True)
                        mm.then_inc(ds_done, 1)

                @block.scalar
                def _(act):
                    for k in range(2):
                        act.activation(*spread(k, 1), ACT.Copy).then_inc(bottom_spread, 1)
                    act.activation(dec[1][:], col[:, 1].rearrange("p d a -> p (d a)"), ACT.Exp).then_inc(dec_ready, 1)
                    act.activation(dec[0][:], dec_in[:], ACT.Copy).then_inc(dec_ready, 1)
                    for g, key in enumerate(order):
                        act.wait_ge(tr_done, g + 1)
                        act.activation(tf[key][:], ps[:, g % 4], ACT.Copy).then_inc(tr_copied, 1)
                        if g == 1:
                            act.wait_ge(du_ready, 2)
                            act.activation(dd[:], du[:], ACT.Exp).then_inc(dd_ready, 1)
                    for lev in range(1, 6):
                        for k in range(2):
                            act.wait_ge(x_done, 2 * (lev - 1) + k + 1)
                            act.activation(x[k][:], ps[:, 2 + k], ACT.Copy).then_inc(x_ready, 1)
                        for k in range(2):
                            act.wait_ge(y_done, 2 * (lev - 1) + k + 1)
                            act.activation(y[k][:], ps[:, k], ACT.Copy).then_inc(y_ready, 1)
                    act.wait_ge(rhs_done, 1)
                    act.activation(rhs[0][:], out_of(6), ACT.Copy).then_inc(rhs_ready0, 1)
                    for k in range(2):
                        act.wait_ge(n_done, k + 1)
                        act.activation(nn[k][:], out_of(k), ACT.Copy, scale=-1.0 if k == 0 else 1.0).then_inc(n_ready, 1)
                    act.wait_ge(stored, 16 * 12)
                    for k in range(2):
                        act.wait_ge(o_done, k + 1)
                        act.activation(oo[k][:], out_of(2 + k), ACT.Copy).then_inc(o_ready, 1)

                @block.vector
                def _(v):
                    link = chained(v, dve_step)
                    v.tensor_copy(*spread(0, 0)).then_inc(top_spread, 1)
                    gc = col[:, 0].rearrange("p d a -> p (d a)").unsqueeze(2).to_broadcast([P, N4, C])
                    v.tensor_tensor(diag[:], eye_s, gc, ALU.mult).then_inc(diag_ready, 1)
                    v.tensor_copy(*spread(1, 0)).then_inc(top_spread, 1)
                    v.wait_ge(diffs_done, 1)
                    v.tensor_tensor(du[:], ps[:, 7].rearrange("p a b -> p (a b)")[:, 0:N4 * C].rearrange("p (a b) -> p a b", a=N4), gc,
                                    ALU.subtract).then_inc(du_ready, 1)
                    v.wait_ge(du_ready, 1)
                    v.tensor_scalar(du[:], du[:], 0.0, None, ALU.min).then_inc(du_ready, 1)
                    v.wait_ge(gram_done, 1)
                    v.tensor_copy(at[0][:], ps[:, 4]).then_inc(at_ready, 1)
                    v.wait_ge(dd_ready, 1)
                    link(v.tensor_tensor(by_pair(ddm[:]), by_pair(dd[:]), over_pairs(near[:, 1]), ALU.mult))
                    v.wait_ge(gram_done, 2)
                    v.tensor_tensor(block_of(at[1], 0), block_of(ps[:, 5], 0), half(dd, 0), ALU.mult)
                    v.tensor_tensor(block_of(at[1], 1), block_of(ps[:, 5], 1), half(dd, 1), ALU.mult).then_inc(at_ready, 1)
                    eye_f = consts["ident"][:].unsqueeze(1).to_broadcast([P, N4, P])
                    for k in range(2):
                        v.wait_ge(m_ready, k + 1)
                        v.tensor_tensor(xt[k][:], eye_f, m[k][:, 0], ALU.subtract).then_inc(xt_ready, 1)
                    evac = [(akt, near[:, 0]), (rk, near[:, 1]), (rb, near[:, 1]), (qk, None)]
                    for lev in range(1, 6):
                        if lev == 5:
                            v.wait_ge(rhs_done, 2)
                            v.wait_ge(vals_kept, 2)
                            v.tensor_tensor(rhs[1][:], val[1][:].rearrange("p d a e -> p (d a) e"), out_of(7), ALU.subtract).then_inc(rhs_ready1, 1)
                        for k in range(2):
                            v.wait_ge(z_done, 2 * (lev - 1) + k + 1)
                            v.wait_ge(xt_ready, 2 * (lev - 1) + k + 1)
                            v.tensor_tensor(xt[k][:], xt[k][:], ps[:, 4 + k], ALU.subtract).then_inc(xt_ready, 1)
                        if lev < 5:
                            dst, mask = evac[lev - 1]
                            v.wait_ge(fill_done, lev)
                            for b in range(2):
                                src = block_of(ps[:, 6 + lev % 2], b)
                                if mask is None:
                                    ins = v.tensor_tensor(block_of(dst, b), src, half(ddm, b), ALU.mult)
                                else:
                                    ins = v.tensor_tensor(by_pair(block_of(dst, b)), by_pair(src), over_pairs(half(mask, b)), ALU.mult)
                            ins.then_inc(fill_ready, 1)
                    v.wait_ge(dec_ready, 2)
                    v.wait_ge(ds_done, 1)
                    link(v.tensor_tensor(st[0][:], st[0][:], out_of(4), ALU.add))
                    link(v.tensor_tensor(st[0][:], st[0][:], head_bc(dec[0][:]), ALU.mult))
                    v.wait_ge(ds_done, 2)
                    link(v.tensor_tensor(st[1][:], st[1][:], head_bc(dec[1][:]), ALU.mult))
                    link(v.tensor_tensor(st[1][:], st[1][:], out_of(5), ALU.add))

        with stage(nc, "last_stored") as (block, last_stored):
            @block.sync
            def _(sp):
                store_outputs(sp, CHUNKS - 1, last_stored)
                sp.wait_ge(last_stored, 16 * 12)


def load_queries_part(sp, l, t, wq, pair, first, sem):
    k = sp.snap(first + ((pair + 1) % 2) * 2)
    sp.dma_start(wq[:, bass.ds(k, 2)], t["peer_wq"][l].rearrange("(k p) n -> p k n", p=P)[:, bass.ds(k, 2)]).then_inc(sem, 16)


def scan_post_stage(nc, l, t, s, wq, consts):
    with ExitStack() as es:
        sb = lambda n, sh: es.enter_context(nc.sbuf_tensor("po_" + n, sh, F32))
        lg, lb, gg = sb("lg", [P, GW]), sb("lb", [P, GW]), sb("gg", [P, HD])
        load_once(nc, [(lg[:], over_rows(t["rwkv_ln_g"][l])), (lb[:], over_rows(t["rwkv_ln_b"][l])), (gg[:], over_rows(t["gdn_norm_g"][l]))])
        tiles = [[sb(f"{n}{u}", sh) for n, sh in (("y", [P, 2, 2, GW]), ("sq", [P, 2, GW]), ("rp", [P, 2, GW]), ("gp", [P, GW]),
                                                   ("r", [P, 6, 2 * HEADS]))] for u in range(2)]
        with nc.Fori(l * (CTX_TILES // 2), TILES // 2) as pair:
            i = pair * 2
            with stage(nc, "y0_in", "y1_in", "post0_in", "post1_in", "var_ready", "root_ready", "dve_step", "out_ready", "stored",
                       "wq_in") as \
                    (block, y0_in, y1_in, post0_in, post1_in, var_ready, root_ready, dve_step, out_ready, stored, wq_in):
                y_in, post_in = (y0_in, y1_in), (post0_in, post1_in)

                @block.sync
                def _(sp):
                    for u, (y, sq, rp, gp, r) in enumerate(tiles):
                        for k in range(2):
                            for d in range(2):
                                src = s["scan"][k, d].rearrange("c t g -> (c t) g")[bass.ds((i + u) * P + (0 if d == 0 else 8 * C), P), :]
                                sp.dma_start(y[:, k, d], src).then_inc(y_in[u], 16)
                        sp.dma_start(rp[:], s["rwpost"][i + u]).then_inc(post_in[u], 16)
                        sp.dma_start(gp[:], s["gdpost"][i + u]).then_inc(post_in[u], 16)
                    load_queries_part(sp, l, t, wq, pair, 0, wq_in)
                    for u, (y, sq, rp, gp, r) in enumerate(tiles):
                        sp.wait_ge(out_ready, u + 1)
                        sp.dma_start(s["y"][bass.ds((i + u) * P, P), GW:3 * GW].rearrange("p (k g) -> p k g", k=2), y[:, :, 0]).then_inc(stored, 16)
                    sp.wait_ge(stored, 32)
                    sp.wait_ge(wq_in, 16)

                @block.scalar
                def _(act):
                    for u, (y, sq, rp, gp, r) in enumerate(tiles):
                        act.wait_ge(var_ready, u + 1)
                        act.activation(r[:, 3, :], r[:, 2, :], ACT.Sqrt).then_inc(root_ready, 1)

                @block.vector
                def _(v):
                    link = chained(v, dve_step)
                    for u, (y, sq, rp, gp, r) in enumerate(tiles):
                        yb, yc = y[:, 0, 0], y[:, 1, 0]
                        v.wait_ge(y_in[u], 64)
                        link(v.tensor_tensor(y[:, :, 0], y[:, :, 0], y[:, :, 1], ALU.add))
                        link(v.tensor_reduce(r[:, 0, 0:HEADS], by_head(yb), X, ALU.add))
                        link(v.tensor_scalar(r[:, 0, 0:HEADS], r[:, 0, 0:HEADS], 1.0 / HD, None, ALU.mult))
                        link(v.tensor_tensor(by_head(yb), by_head(yb), head_bc(r[:, 0, 0:HEADS]), ALU.subtract))
                        link(v.tensor_tensor(sq[:], y[:, :, 0], y[:, :, 0], ALU.mult))
                        link(v.tensor_reduce(r[:, 1, :], sq[:].rearrange("p k (h e) -> p (k h) e", e=HD), X, ALU.add))
                        link(v.tensor_scalar(r[:, 2, 0:HEADS], r[:, 1, 0:HEADS], 1.0 / HD, GN_EPS, ALU.mult, ALU.add))
                        v.tensor_scalar(r[:, 2, HEADS:], r[:, 1, HEADS:], 1.0 / HD, NORM_EPS, ALU.mult, ALU.add).then_inc(var_ready, 1)
                    for u, (y, sq, rp, gp, r) in enumerate(tiles):
                        yb, yc = y[:, 0, 0], y[:, 1, 0]
                        v.wait_ge(root_ready, u + 1)
                        link(v.reciprocal(r[:, 4, :], r[:, 3, :]))
                        link(v.tensor_tensor(y[:, :, 0].rearrange("p k (h e) -> p k h e", e=HD), y[:, :, 0].rearrange("p k (h e) -> p k h e", e=HD),
                                             r[:, 4, :].rearrange("p (k h) -> p k h", k=2).unsqueeze(3).to_broadcast([P, 2, HEADS, HD]), ALU.mult))
                        v.wait_ge(post_in[u], 32)
                        link(v.tensor_tensor(yb, yb, lg[:], ALU.mult))
                        link(v.tensor_tensor(yb, yb, lb[:], ALU.add))
                        link(v.tensor_tensor(yb, yb, rp[:, 0], ALU.add))
                        link(v.tensor_tensor(yb, yb, rp[:, 1], ALU.mult))
                        link(v.tensor_tensor(by_head(yc), by_head(yc), gg[:].unsqueeze(1).to_broadcast([P, HEADS, HD]), ALU.mult))
                        v.tensor_tensor(yc, yc, gp[:], ALU.mult).then_inc(out_ready, 1)


def post_norm(v, link, z, y, h, gate, g, b, stats, mv, var_ready, std_ready, n=1):
    link(v.tensor_tensor(z[:], y, gate, ALU.mult))
    link(v.scalar_tensor_tensor(z[:], h, ALPHA, z[:], ALU.mult, ALU.add))
    ln_first(v, link, z, stats, mv, var_ready)
    ln_last(v, link, z[:], z[:], mv, std_ready, n)
    link(v.tensor_tensor(z[:], z[:], g[:], ALU.mult))
    return v.tensor_tensor(z[:], z[:], b[:], ALU.add)


def mix_stage(nc, l, t, s, w, wq, consts):
    with ExitStack() as es:
        sb = lambda n, sh: es.enter_context(nc.sbuf_tensor("mx_" + n, sh, F32))
        g, b = sb("g", [P, D]), sb("b", [P, D])
        load_once(nc, [(g[:], over_rows(t["ln_mix_g"][l])), (b[:], over_rows(t["ln_mix_b"][l]))])
        gate, yT = sb("gate", [P, D]), [sb(f"yT{u}", [P, KT, P]) for u in range(2)]
        y, h, z = [[sb(f"{n}{u}", [P, D]) for u in range(2)] for n in ("y", "h", "z")]
        stats, mv = sb("stats", [P, 2, 6]), sb("mv", [P, 8])
        ps = es.enter_context(nc.psum_tensor("mx_ps", [P, 8, 512], F32))
        with nc.Fori(l * (CTX_TILES // 2), TILES // 2) as pair:
            i = pair * 2
            with stage(nc, "y0_in", "y1_in", "h0_in", "h1_in", "gate_in", "tr_done", "copied", "mm_done", "var_ready", "std_ready", "dve_step",
                       "z_ready", "stored", "wq_in") as \
                    (block, y0_in, y1_in, h0_in, h1_in, gate_in, tr_done, copied, mm_done, var_ready, std_ready, dve_step, z_ready, stored, wq_in):
                y_in, h_in = (y0_in, y1_in), (h0_in, h1_in)

                @block.sync
                def _(sp):
                    for u in range(2):
                        sp.dma_start(y[u][:], s["y"][bass.ds((i + u) * P, P), :]).then_inc(y_in[u], 16)
                    for u in range(2):
                        sp.dma_start(h[u][:], s["h"][i + u]).then_inc(h_in[u], 16)
                    sp.dma_start(gate[:], over_rows(s["mods"][i, 2 * D:3 * D])).then_inc(gate_in, 16)
                    load_queries_part(sp, l, t, wq, pair, KT // 2, wq_in)
                    for u in range(2):
                        sp.wait_ge(z_ready, u + 1)
                        sp.dma_start(s["h"][i + u], z[u][:]).then_inc(stored, 16)
                    sp.wait_ge(stored, 32)
                    sp.wait_ge(wq_in, 16)

                @block.tensor
                def _(pe):
                    for u in range(2):
                        pe.wait_ge(y_in[u], 16)
                        for half in range(2):
                            for k in range(4):
                                kk = 4 * half + k
                                tr = pe.transpose(ps[:, 4 * u + half, k * P:(k + 1) * P], y[u][:, kk * P:(kk + 1) * P], consts["ident"][:])
                            tr.then_inc(tr_done, 1)
                    for u in range(2):
                        pe.wait_ge(copied, 2 * u + 2)
                        for half in range(2):
                            for k in range(KT):
                                mm = pe.matmul(ps[:, 4 * u + 2 + half, :], yT[u][:, k, :], w[:, k, half * 512:(half + 1) * 512],
                                               start=(k == 0), stop=(k == KT - 1))
                            mm.then_inc(mm_done, 1)

                @block.scalar
                def _(act):
                    for u in range(2):
                        for half in range(2):
                            act.wait_ge(tr_done, 2 * u + half + 1)
                            act.activation(yT[u][:, 4 * half:4 * half + 4, :].rearrange("p k n -> p (k n)"), ps[:, 4 * u + half], ACT.Copy).then_inc(copied, 1)
                    for u in range(2):
                        act.wait_ge(var_ready, u + 1)
                        act.activation(mv[:, 3:4], mv[:, 2:3], ACT.Sqrt).then_inc(std_ready, 1)

                @block.vector
                def _(v):
                    link = chained(v, dve_step)
                    v.wait_ge(gate_in, 16)
                    for u in range(2):
                        v.wait_ge(h_in[u], 16)
                        v.wait_ge(mm_done, 2 * u + 2)
                        post_norm(v, link, z[u], ps[:, 4 * u + 2:4 * u + 4].rearrange("p a b -> p (a b)"), h[u][:], gate[:], g, b, stats, mv,
                                  var_ready, std_ready, u + 1).then_inc(z_ready, 1)


RING = 10
DIAGS = 32


def peer_stages(nc, l, t, s, wq, consts):
    NS = 2 * PH
    with ExitStack() as es:
        sb = lambda n, sh, dt=F32: es.enter_context(nc.sbuf_tensor("pe_" + n, sh, dt))
        b = {"keys": sb("keys", [P, PH * 2 * PK]), "g": sb("g", [P, D]), "b": sb("b", [P, D]), "wq": wq,
             "iota": sb("iota", [P, TOPK]), "tb": sb("tb", [P, D]), "slot": sb("slot", [P, SLOTS], U32), "gates": sb("gates", [P, SLOTS]),
             "m": sb("m", [P, 2, D]), "tbT": sb("tbT", [P, KT, P]), "qT": sb("qT", [P, 2, 4, P]), "sc": sb("sc", [P, NS, PK]),
             "sc2": sb("sc2", [P, TOPK * TOPK]), "stats": sb("stats", [P, 2, 6]), "mv": sb("mv", [P, 8]),
             "top": sb("top", [P, NS, TOPK]), "topi": sb("topi", [P, NS, TOPK], U32), "topf": sb("topf", [P, NS, TOPK]),
             "cand": sb("cand", [P, PH, TOPK, TOPK]), "best": sb("best", [P, PH, TOPK]), "pos": sb("pos", [P, PH, TOPK], U32),
             "posf": sb("posf", [P, 2, PH, TOPK]), "half": sb("half", [P, PH, TOPK], U32), "i0": sb("i0", [P, PH, TOPK]),
             "ring": sb("ring", [P, RING, D]), "i1": sb("i1", [P, PH, TOPK]), "ex": sb("ex", [P, PH, TOPK]), "r8": sb("r8", [P, 2, PH])}
        ps = es.enter_context(nc.psum_tensor("ro_ps", [P, 8, 512], F32))
        load_once(nc, [(b["keys"][:], t["keys"][l]), (b["g"][:], over_rows(t["ln_ffn_g"][l])), (b["b"][:], over_rows(t["ln_ffn_b"][l])),
                       (b["iota"][:], t["k_iota"])])
        with stage(nc, *ROUTE_SEMS) as (block, *rs):
            r = dict(zip(ROUTE_SEMS, rs))

            @block.sync
            def _(sp):
                route_loads(sp, l * CTX_TILES, s, b, r)

            @block.tensor
            def _(pe):
                for n in range(ROUTE_PE):
                    route_pe(pe, n, ps, b, consts, r)

            @block.scalar
            def _(act):
                for n in range(ROUTE_ACT):
                    route_act(act, n, ps, b, r)

            @block.vector
            def _(v):
                link = chained(v, r["dve_step"])
                for n in range(ROUTE_DVE):
                    route_dve(v, link, n, b, consts, r)
        with stage(nc, "rows_in", pool_dmas=True) as (block, rows_in):
            @block.gpsimd
            def _(pool):
                for k in range(RING):
                    gather_row(pool, t["peer_u"], b["ring"][:, k, :], b["slot"][:, k:k + 1]).then_inc(rows_in, 16)
                pool.wait_ge(rows_in, 16 * RING)
        with nc.Fori(l * CTX_TILES, TILES) as i:
            experts_stage(nc, i, t, s, b, ps, consts)


def gather_row(pool, table, dst, index):
    return pool.indirect_dma_start(dst, None, table, bass.IndirectOffsetOnAxis(ap=index, axis=0))


def experts_stage(nc, i, t, s, b, ps, consts):
    with ExitStack() as es:
        sb = lambda n, sh, dt=F32: es.enter_context(nc.sbuf_tensor("ex_" + n, sh, dt))
        ring = b["ring"]
        idx, gates, act_raw, wts = sb("idx", [P, SLOTS], U32), sb("gates", [P, SLOTS]), sb("act", [P, SLOTS]), sb("wts", [P, SLOTS])
        y, z, diag = sb("y", [P, D]), sb("z", [P, D]), sb("diag", [P, DIAGS, P])
        stats, mv = sb("stats", [P, 2, 6]), sb("mv", [P, 8])
        names = ["idx_ready", "dots_done", "dve_used", "pe_used", "gelu_done", "w_ready", "diag_ready", "mm_done", "y_zero", "h_in", "gate_in", "z_free",
                 "n_var", "n_std", "z_ready", "stored"] + [f"row_in{k}" for k in range(RING)]
        with stage(nc, *names, *ROUTE_SEMS, pool_dmas=True) as (block, *sems):
            q = dict(zip(names + ROUTE_SEMS, sems))
            row_in = sems[16:16 + RING]
            half = SLOTS // 2

            @block.gpsimd
            def _(pool):
                pool.memset(y[:], 0.0).then_inc(q["y_zero"], 1)
                pool.wait_ge(q["idx_ready"], 1)

                def wait_free(old):
                    if old < SLOTS:
                        pool.wait_ge(q["dots_done"], old + 1)
                    elif old % 2:
                        pool.wait_ge(q["pe_used"], (old - SLOTS) // 2 + 1)
                    else:
                        pool.wait_ge(q["dve_used"], (old - SLOTS) // 2 + 1)

                for k in range(RING, 2 * SLOTS):
                    wait_free(k - RING)
                    gather_row(pool, t["peer_u"] if k < SLOTS else t["peer_v"], ring[:, k % RING, :],
                               idx[:, k % SLOTS:k % SLOTS + 1]).then_inc(row_in[k % RING], 16)
                pool.wait_ge(q["slot_ready"], 1)
                for old in range(2 * SLOTS - RING, 2 * SLOTS):
                    wait_free(old)
                    k = old % RING
                    gather_row(pool, t["peer_u"], ring[:, k, :], b["slot"][:, k:k + 1]).then_inc(row_in[k], 16)
                for old in range(2 * SLOTS - RING, 2 * SLOTS):
                    pool.wait_ge(row_in[old % RING], 16 * (old // RING + 1))

            @block.sync
            def _(sp):
                sp.wait_ge(q["w_ready"], 1)
                route_loads(sp, i + 1, s, b, q)
                sp.wait_ge(q["route_m_free"], 1)
                sp.dma_start(b["m"][:, 0], over_rows(s["mods"][i, 5 * D:6 * D])).then_inc(q["gate_in"], 16)
                sp.dma_start(b["m"][:, 1], s["h"][i]).then_inc(q["h_in"], 16)
                sp.wait_ge(q["z_ready"], 1)
                sp.dma_start(s["h"][i], z[:]).then_inc(q["stored"], 16)
                sp.wait_ge(q["stored"], 16)

            @block.tensor
            def _(pe):
                for m in range(half):
                    k = SLOTS + 2 * m + 1
                    pe.wait_ge(q["diag_ready"], m + 1)
                    pe.wait_ge(row_in[k % RING], 16 * (k // RING))
                    for c in range(2):
                        mm = pe.matmul(ps[:, 6 + c, :], diag[:, m % DIAGS, :], ring[:, k % RING, c * 512:(c + 1) * 512],
                                       start=(m == 0), stop=(m == half - 1))
                    mm.then_inc(q["pe_used"], 1)
                    if 3 <= m < 3 + ROUTE_PE:
                        route_pe(pe, m - 3, ps, b, consts, q)

            @block.scalar
            def _(act):
                act.wait_ge(q["dots_done"], SLOTS)
                act.activation(wts[:], act_raw[:], ACT.Gelu).then_inc(q["gelu_done"], 1)
                act.wait_ge(q["w_ready"], 1)

                def diags(first, last):
                    for m in range(first, last):
                        if m >= DIAGS:
                            act.wait_ge(q["pe_used"], m - DIAGS + 1)
                        act.activation(diag[:, m % DIAGS, :], consts["ident"][:], ACT.Copy, scale=wts[:, 2 * m + 1:2 * m + 2]).then_inc(q["diag_ready"], 1)

                diags(0, 8)
                for n in range(ROUTE_ACT):
                    if n == 1:
                        diags(8, DIAGS)
                    route_act(act, n, ps, b, q)
                    if n == ROUTE_ACT - 2:
                        diags(DIAGS, half)
                act.wait_ge(q["n_var"], 1)
                act.activation(mv[:, 3:4], mv[:, 2:3], ACT.Sqrt).then_inc(q["n_std"], 1)

            @block.vector
            def _(v):
                link = chained(v, q["dve_step"])
                v.tensor_copy(idx[:], b["slot"][:]).then_inc(q["idx_ready"], 1)
                link(v.tensor_copy(gates[:], b["gates"][:]))
                for k in range(SLOTS):
                    if k >= RING:
                        v.wait_ge(row_in[k % RING], 16 * (k // RING))
                    if k >= 1:
                        v.wait_ge(q["dots_done"], k)
                    v.scalar_tensor_tensor(z[:], ring[:, k % RING, :], 1.0, b["tb"][:], ALU.mult, ALU.mult,
                                           accum_out=act_raw[:, k:k + 1]).then_inc(q["dots_done"], 1)
                v.wait_ge(q["gelu_done"], 1)
                v.tensor_tensor(wts[:], wts[:], gates[:], ALU.mult).then_inc(q["w_ready"], 1)
                v.wait_ge(q["w_ready"], 1)
                v.wait_ge(q["y_zero"], 1)
                n = 0
                for m in range(half):
                    k = SLOTS + 2 * m
                    v.wait_ge(row_in[k % RING], 16 * (k // RING))
                    if m >= 1:
                        v.wait_ge(q["dve_used"], m)
                    v.scalar_tensor_tensor(y[:], ring[:, k % RING, :], wts[:, 2 * m:2 * m + 1], y[:], ALU.mult, ALU.add).then_inc(q["dve_used"], 1)
                    if m == 1 or (m >= DVE_FROM and n < ROUTE_DVE):
                        route_dve(v, link, n, b, consts, q)
                        n += 1
                assert n == ROUTE_DVE
                v.wait_ge(q["pe_used"], half)
                v.wait_ge(q["dve_used"], half)
                link(v.tensor_tensor(y[:], y[:], ps[:, 6:8].rearrange("p a b -> p (a b)"), ALU.add))
                v.wait_ge(q["gate_in"], 16)
                v.wait_ge(q["h_in"], 16)
                post_norm(v, link, z, y[:], b["m"][:, 1], b["m"][:, 0], b["g"], b["b"], stats, mv, q["n_var"], q["n_std"]).then_inc(q["z_ready"], 1)


ROUTE_SEMS = ["route_h_in", "route_m_in", "route_m_free", "route_var", "route_std", "tb_ready", "tr_done", "tbT_ready", "q_done", "q_ready",
              "s_done", "s_ready", "gap_ready", "exp_ready", "slot_ready", "dve_step"]
ROUTE_PE = 10
ROUTE_ACT = 12
ROUTE_DVE = 34
DVE_FROM = 25


def route_loads(sp, i, s, b, q):
    sp.dma_start(b["tb"][:], s["h"][i]).then_inc(q["route_h_in"], 16)
    sp.dma_start(b["m"][:], over_rows(s["mods"][i, 3 * D:5 * D]).rearrange("p (a n) -> p a n", a=2)).then_inc(q["route_m_in"], 16)


def route_pe(pe, n, ps, b, consts, q):
    if n < 2:
        pe.wait_ge(q["tb_ready"], 1)
        for k in range(4):
            kk = 4 * n + k
            tr = pe.transpose(ps[:, n, k * P:(k + 1) * P], b["tb"][:, kk * P:(kk + 1) * P], consts["ident"][:])
        tr.then_inc(q["tr_done"], 1)
        return
    part, g = (n - 2) % 2, (n - 2) // 2
    if part == 0:
        pe.wait_ge(q["tbT_ready"], 2)
        if g >= 2:
            pe.wait_ge(q["q_ready"], g - 1)
        for x in range(4):
            hp = 4 * g + x
            for k in range(KT):
                mm = pe.matmul(ps[:, 2 + g % 2, x * P:(x + 1) * P], b["wq"][:, k, hp * P:(hp + 1) * P], b["tbT"][:, k, :], start=(k == 0), stop=(k == KT - 1))
        mm.then_inc(q["q_done"], 1)
    else:
        pe.wait_ge(q["q_ready"], g + 1)
        if g >= 2:
            pe.wait_ge(q["s_ready"], g - 1)
        for x in range(4):
            hp = 4 * g + x
            mm = pe.matmul(ps[:, 4 + g % 2, x * P:(x + 1) * P], b["qT"][:, g % 2, x, :], b["keys"][:, hp * PK:(hp + 1) * PK], start=True, stop=True)
        mm.then_inc(q["s_done"], 1)


def route_act(act, n, ps, b, q):
    if n == 0:
        act.wait_ge(q["route_var"], 1)
        act.activation(b["mv"][:, 3:4], b["mv"][:, 2:3], ACT.Sqrt).then_inc(q["route_std"], 1)
    elif n <= 2:
        act.wait_ge(q["tr_done"], n)
        act.activation(b["tbT"][:, 4 * n - 4:4 * n, :].rearrange("p k n -> p (k n)"), ps[:, n - 1], ACT.Copy).then_inc(q["tbT_ready"], 1)
    elif n <= 10:
        part, g = (n - 3) % 2, (n - 3) // 2
        if part == 0:
            act.wait_ge(q["q_done"], g + 1)
            if g >= 2:
                act.wait_ge(q["s_done"], g - 1)
            act.activation(b["qT"][:, g % 2].rearrange("p k n -> p (k n)"), ps[:, 2 + g % 2], ACT.Copy).then_inc(q["q_ready"], 1)
        else:
            act.wait_ge(q["s_done"], g + 1)
            act.activation(b["sc"][:, 4 * g:4 * g + 4, :].rearrange("p k n -> p (k n)"), ps[:, 4 + g % 2], ACT.Copy).then_inc(q["s_ready"], 1)
    else:
        act.wait_ge(q["gap_ready"], 1)
        act.activation(b["ex"][:], b["best"][:], ACT.Exp).then_inc(q["exp_ready"], 1)


def top16(v, link, src, spare, vals, inds):
    link(v.max(vals[:, 0:8], src))
    link(v.max_index(inds[:, 0:8], vals[:, 0:8], src))
    link(v.match_replace(out=spare, in_to_replace=vals[:, 0:8], in_values=src, imm_value=-3e38))
    link(v.max(vals[:, 8:16], spare))
    link(v.max_index(inds[:, 8:16], vals[:, 8:16], spare))


def route_dve(v, link, n, b, consts, q):
    tb, m, stats, mv = b["tb"], b["m"], b["stats"], b["mv"]
    halves = lambda x: x[:].rearrange("p (h two) k -> p h two k", two=2)
    if n == 0:
        v.wait_ge(q["route_h_in"], 16)
        ln_first(v, link, tb, stats, mv, q["route_var"])
        ln_last(v, link, tb[:], tb[:], mv, q["route_std"], 1)
        v.wait_ge(q["route_m_in"], 16)
        link(v.tensor_tensor(tb[:], tb[:], m[:, 1, :], ALU.mult))
        link(v.tensor_tensor(tb[:], tb[:], m[:, 0, :], ALU.add))
        v.sem_inc(q["tb_ready"], 1)
        v.sem_inc(q["route_m_free"], 1)
    elif n <= 16:
        v.wait_ge(q["s_ready"], (n - 1) // 4 + 1)
        top16(v, link, b["sc"][:, n - 1, :], b["sc2"][:, 0:PK], b["top"][:, n - 1, :], b["topi"][:, n - 1, :])
    elif n == 17:
        link(v.tensor_tensor(b["cand"][:], halves(b["top"])[:, :, 0].unsqueeze(3).to_broadcast([P, PH, TOPK, TOPK]),
                             halves(b["top"])[:, :, 1].unsqueeze(2).to_broadcast([P, PH, TOPK, TOPK]), ALU.add))
    elif n <= 25:
        h = n - 18
        top16(v, link, b["cand"][:, h].rearrange("p a b -> p (a b)"), b["sc2"][:], b["best"][:, h, :], b["pos"][:, h, :])
    elif n == 26:
        best, r8 = b["best"], b["r8"]
        link(v.tensor_copy(r8[:, 0, :], best[:, :, 0]))
        v.tensor_tensor(best[:], best[:], r8[:, 0, :].unsqueeze(2).to_broadcast([P, PH, TOPK]), ALU.subtract).then_inc(q["gap_ready"], 1)
        for x, (op, by) in enumerate(((ALU.logical_shift_right, 4), (ALU.bitwise_and, 15))):
            link(v.tensor_scalar(b["half"][:], b["pos"][:], by, None, op))
            link(v.tensor_copy(b["posf"][:, x], b["half"][:]))
        link(v.tensor_copy(b["topf"][:], b["topi"][:]))
    elif n <= 32:
        x, step = (n - 27) // 3, (n - 27) % 3
        eq = b["cand"][:].rearrange("p h k n -> p (h k) n")
        if step == 0:
            at = b["posf"][:, x].rearrange("p h k -> p (h k)").unsqueeze(2).to_broadcast([P, SLOTS, TOPK])
            link(v.tensor_tensor(eq, at, b["iota"][:].unsqueeze(1).to_broadcast([P, SLOTS, TOPK]), ALU.is_equal))
        elif step == 1:
            link(v.tensor_tensor(b["cand"][:], b["cand"][:], halves(b["topf"])[:, :, x].unsqueeze(2).to_broadcast([P, PH, TOPK, TOPK]), ALU.mult))
        else:
            link(v.tensor_reduce((b["i0"], b["i1"])[x][:].rearrange("p h k -> p (h k)"), eq, X, ALU.add))
    else:
        ex, r8 = b["ex"], b["r8"]
        link(v.scalar_tensor_tensor(b["i0"][:], b["i0"][:], float(PK), b["i1"][:], ALU.mult, ALU.add))
        link(v.tensor_scalar(b["i0"][:], b["i0"][:], consts["layer"][:, 2:3], None, ALU.add))
        link(v.tensor_copy(b["slot"][:], b["i0"][:].rearrange("p h k -> p (h k)")))
        v.sem_inc(q["slot_ready"], 1)
        v.wait_ge(q["exp_ready"], 1)
        link(v.tensor_reduce(r8[:, 0, :], ex[:], X, ALU.add))
        link(v.reciprocal(r8[:, 1, :], r8[:, 0, :]))
        link(v.tensor_tensor(b["gates"][:].rearrange("p (h k) -> p h k", h=PH), ex[:], r8[:, 1, :].unsqueeze(2).to_broadcast([P, PH, TOPK]), ALU.mult))


def load_once(nc, pairs):
    with stage(nc, "once_in") as (block, once_in):
        @block.sync
        def _(sp):
            for dst, src in pairs:
                sp.dma_start(dst, src).then_inc(once_in, 16)
            sp.wait_ge(once_in, 16 * len(pairs))


@contextmanager
def loading(nc, name, pairs):
    with nc.semaphore(name) as ahead_in:
        with nc.Block() as start:
            @start.scalar
            def _(act):
                for dst, src in pairs:
                    act.dma_start(dst, src).then_inc(ahead_in, 16)
        yield
        with nc.Block() as end:
            @end.scalar
            def _(act):
                act.wait_ge(ahead_in, 16 * len(pairs))
        with nc.Block() as clear:
            @clear.scalar
            def _(act):
                act.sem_clear(ahead_in)


def build(nc, t, out):
    with ExitStack() as es:
        dram = lambda n, s: nc.dram_tensor(n, s, F32, kind="Internal").ap()
        s = {
            "h": dram("h_dram", (TILES + 1, P, D)),
            "mods": dram("mods_dram", (TILES + 1, 6 * D)),
            "p": dram("p_dram", (TOK + 2, IN_COLS)),
            "y": dram("y_dram", (TOK, D)),
            "rw": dram("rw_dram", (2 * TILES, 2, 2, 2, C, 5, 2, HD)),
            "rwdec": dram("rwdec_dram", (2 * TILES * 2, 2, GW)),
            "rwpost": dram("rwpost_dram", (TILES, P, 2, GW)),
            "gd": dram("gd_dram", (2 * TILES, 2, 2, 2, C, 7, 2, HD)),
            "gdcol": dram("gdcol_dram", (2 * TILES * 2, 2, 2, C, HEADS)),
            "gdpost": dram("gdpost_dram", (TILES, P, GW)),
            "scan": dram("scan_dram", (2, 2, 24, C, GW)),
        }
        consts = {}
        for name, key in (("ident", "k_ident"), ("sums", "k_sums"), ("rows", "k_rows")):
            ap = t[key]
            consts[name] = es.enter_context(nc.sbuf_tensor("c_" + name, list(ap.shape), F32))
        layer = es.enter_context(nc.sbuf_tensor("c_layer", [P, 4], F32))
        consts["layer"] = layer
        load_once(nc, [(consts["ident"][:], t["k_ident"]), (consts["sums"][:], t["k_sums"]), (consts["rows"][:], t["k_rows"]),
                       (s["h"][0:CTX_TILES].rearrange("i p n -> (i p) n"), t["ctx"]),
                       (s["h"][CTX_TILES:TILES].rearrange("i p n -> (i p) n"), t["x"]),
                       (s["h"][TILES], t["x"][0:P]),
                       (s["p"][0:1, :], t["k_zero"][0:1, :]), (s["p"][TOK + 1:TOK + 2, :], t["k_zero"][1:2, :])])
        with nc.Fori(0, DEPTH) as l:
            load_once(nc, [(layer[:], t["k_layer"][l])])
            ada_stage(nc, l, t, s["mods"], consts)
            with nc.sbuf_tensor("uT", [P, KT, TOK], F32) as uT:
                with nc.sbuf_tensor("p_w", [P, 2, KT, WCHUNK], F32) as w:
                    with loading(nc, "w_in_ahead", [(w[:, 0], t["w_in"][l].rearrange("(k p) n -> p k n", p=P)[:, :, 0:WCHUNK])]):
                        norm_stage(nc, l, t, s["h"], s["mods"], consts, uT)
                    project_stage(nc, l, t, s["p"], uT, w)
            attention_stages(nc, l, t, s, consts)
            prep_stage(nc, l, t, s, consts)
            chunk_stage(nc, t, s, consts)
            with nc.sbuf_tensor("peer_wq", [P, KT, PH * 2 * P], F32) as wq:
                with nc.sbuf_tensor("mix_w", [P, KT, D], F32) as w:
                    with loading(nc, "w_out_ahead", [(w[:], t["w_out"][l].rearrange("(k p) n -> p k n", p=P))]):
                        scan_post_stage(nc, l, t, s, wq, consts)
                    mix_stage(nc, l, t, s, w, wq, consts)
                peer_stages(nc, l, t, s, wq, consts)
        load_once(nc, [(out, s["h"][CTX_TILES:TILES].rearrange("i p n -> (i p) n"))])


def laid_out(inputs):
    a = {k: np.asarray(v) for k, v in inputs.items()}
    r = {n: a[n] for n in ("w_ada", "b_ada", "w_in", "w_out", "ln_mix_g", "ln_mix_b", "ln_ffn_g", "ln_ffn_b", "diff_norm_g",
                           "rwkv_mu", "rwkv_kk", "rwkv_ka", "rwkv_ln_g", "rwkv_ln_b", "rwkv_g2", "gdn_conv", "gdn_norm_g",
                           "peer_wq")}
    r["x"] = a["x"].reshape(SEQ, D)
    r["ctx"] = a["ctx"].reshape(CTX, D)
    r["cond"] = np.ascontiguousarray(np.stack([a["c"][0], a["c_ctx"]]).reshape(2, KT, P).transpose(2, 1, 0))
    r["diff_lam"] = a["diff_lam"].reshape(DEPTH, -1)
    r["rwkv_w0"] = a["rwkv_w0"].reshape(DEPTH, -1)
    r["rwkv_a0"] = a["rwkv_a0"].reshape(DEPTH, -1)
    r["rwkv_w2"] = a["rwkv_w2"]
    r["rwkv_a2"] = a["rwkv_a2"]
    r["rwkv_rk"] = a["rwkv_rk"].reshape(DEPTH, -1)
    r["gdn_a_log"] = a["gdn_a_log"].reshape(DEPTH, -1)
    r["gdn_dt_bias"] = a["gdn_dt_bias"].reshape(DEPTH, -1)
    r["bias"] = window_bias(a["nat_rpb"])
    r["keys"] = np.ascontiguousarray(a["peer_keys"].transpose(0, 4, 1, 2, 3).reshape(DEPTH, P, PH * 2 * PK))
    r["peer_u"] = a["peer_u"].reshape(DEPTH * EXPERTS, D)
    r["peer_v"] = a["peer_v"].reshape(DEPTH * EXPERTS, D)
    r.update(constants())
    return {"in_" + k: np.ascontiguousarray(v) for k, v in r.items()}


def kernel(**inputs):
    import concourse.bacc as bacc
    from concourse.bass_utils import run_bass_kernel_spmd

    nc = bacc.Bacc("TRN2", target_bir_lowering=False, num_devices=1)
    arrays = laid_out(inputs)
    t = {}
    for name, a in arrays.items():
        t[name[3:]] = nc.dram_tensor(name, a.shape, mybir.dt.from_np(a.dtype), kind="ExternalInput").ap()
    out = nc.dram_tensor("out", (SEQ, D), F32, kind="ExternalOutput").ap()
    build(nc, t, out)
    r = run_bass_kernel_spmd(nc, [arrays], core_ids=[0])
    return r.results[0]["out"].reshape(1, SEQ, D)
```
